# Optimizing a Trainium2 kernel written in Bass

```python
import math
import jax, jax.numpy as jnp
from jax import lax
import numpy as np

D_MODEL = 1024
BATCH = 1
SEQ = 512
DEPTH = 1

HEAD_DIM = 64
MIX_WIDTH = D_MODEL
DIFF_VDIM = 2 * HEAD_DIM
DIFF_HEADS = (MIX_WIDTH // 2) // DIFF_VDIM
SB_HEADS = (MIX_WIDTH // 2) // HEAD_DIM
DIFF_QK = DIFF_HEADS * 2 * HEAD_DIM
DIFF_V = DIFF_HEADS * DIFF_VDIM
SB_W = SB_HEADS * HEAD_DIM
IN_COLS = 2 * DIFF_QK + DIFF_V + 3 * SB_W
Q_BLOCK = 128
N_GROUPS = 4
EXPERTS_PER_GROUP = 8
TOP_K_IN_GROUP = 2
D_EXPERT = 256
N_MOD = 6
EPS = 1e-6

kernel_name = "hymba_diff_stickbreak_hmoe_block"

def rms_norm(x, g):
    xf = x.astype(jnp.float32)
    y = xf * lax.rsqrt(jnp.mean(xf * xf, axis=-1, keepdims=True) + EPS)
    return (y * g.astype(jnp.float32)).astype(x.dtype)

def modulate(h, shift, scale):
    return h * (1.0 + scale[:, None, :]) + shift[:, None, :]

def alibi_slopes(n_heads):
    return 2.0 ** (-8.0 * jnp.arange(1, n_heads + 1, dtype=jnp.float32) / n_heads)

def diff_attention(q, k, v, lam):
    B, H, _, S, d = q.shape
    nb = S // Q_BLOCK
    slopes = alibi_slopes(H)
    spos = jnp.arange(S)
    qb = q.reshape(B, H, 2, nb, Q_BLOCK, d).transpose(3, 0, 1, 2, 4, 5)

    def one_block(args):
        q_blk, i = args
        tpos = i * Q_BLOCK + jnp.arange(Q_BLOCK)
        dist = tpos[:, None] - spos[None, :]
        s = jnp.einsum('bhmqd,bhmkd->bhmqk', q_blk, k).astype(jnp.float32)
        bias = -slopes[:, None, None, None] * dist.astype(jnp.float32)
        s = jnp.where(dist >= 0, s + bias, -jnp.inf)
        p = jax.nn.softmax(s, axis=-1)
        a = p[:, :, 0] - lam * p[:, :, 1]
        return jnp.einsum('bhqk,bhkd->bhqd', a.astype(v.dtype), v)

    out = lax.map(one_block, (qb, jnp.arange(nb)))
    return out.transpose(1, 0, 3, 2, 4).reshape(B, S, H, v.shape[-1])

def stick_breaking_attention(q, k, v):
    B, H, S, d = q.shape
    nb = S // Q_BLOCK
    scale = 1.0 / math.sqrt(d)
    spos = jnp.arange(S)
    qb = q.reshape(B, H, nb, Q_BLOCK, d).transpose(2, 0, 1, 3, 4)

    def one_block(args):
        q_blk, i = args
        tpos = i * Q_BLOCK + jnp.arange(Q_BLOCK)
        mask = spos[None, :] < tpos[:, None]
        z = jnp.einsum('bhqd,bhkd->bhqk', q_blk, k).astype(jnp.float32) * scale
        log_beta = jax.nn.log_sigmoid(z)
        log_rem = jnp.where(mask, jax.nn.log_sigmoid(-z), 0.0)
        suffix = lax.cumsum(log_rem, axis=3, reverse=True) - log_rem
        a = jnp.where(mask, jnp.exp(log_beta + suffix), 0.0)
        return jnp.einsum('bhqk,bhkd->bhqd', a.astype(v.dtype), v)

    out = lax.map(one_block, (qb, jnp.arange(nb)))
    return out.transpose(1, 0, 3, 2, 4).reshape(B, S, H, d)

def hier_moe(h, w_group, b_group, w_erouter, b_expert, w1, w3, w2):
    B, S, D = h.shape
    ht = h.reshape(B * S, D)
    g_logits = (ht @ w_group + b_group).astype(jnp.float32)
    p_group = jax.nn.softmax(g_logits, axis=-1)
    _, g_sel = lax.top_k(g_logits, 1)
    gate_group = jnp.take_along_axis(p_group, g_sel, axis=-1)
    g_sel = g_sel[:, 0]
    e_all = (jnp.einsum('td,gde->tge', ht, w_erouter) + b_expert).astype(jnp.float32)
    e_logits = jnp.take_along_axis(e_all, g_sel[:, None, None], axis=1)[:, 0]
    top_vals, top_idx = lax.top_k(e_logits, TOP_K_IN_GROUP)
    top_w = jax.nn.softmax(top_vals, axis=-1)
    within = jnp.sum(jax.nn.one_hot(top_idx, EXPERTS_PER_GROUP, dtype=jnp.float32)
                     * top_w[..., None], axis=1)
    combine = (gate_group[:, :, None]
               * jax.nn.one_hot(g_sel, N_GROUPS, dtype=jnp.float32)[:, :, None]
               * within[:, None, :]).astype(ht.dtype)
    out = jnp.zeros_like(ht)
    for g in range(N_GROUPS):
        hg = jax.nn.silu(jnp.einsum('td,edf->tef', ht, w1[g])) * jnp.einsum('td,edf->tef', ht, w3[g])
        out = out + jnp.einsum('tef,efd->td', hg * combine[:, g, :, None], w2[g])
    return out.reshape(B, S, D)

def setup_inputs(seed: int = 0) -> dict:
    key = jax.random.key(seed)
    ks = jax.random.split(key, 24)
    f32 = jnp.float32
    L, D, d = DEPTH, D_MODEL, HEAD_DIM
    G, E, F = N_GROUPS, EXPERTS_PER_GROUP, D_EXPERT
    nrm = lambda k, shape, s: jax.random.normal(k, shape, f32) * s
    return {
        "x": nrm(ks[0], (BATCH, SEQ, D), 1.0),
        "c": nrm(ks[1], (BATCH, D), 1.0),
        "w_ada": nrm(ks[2], (L, D, N_MOD * D), 0.5 * D ** -0.5),
        "b_ada": nrm(ks[3], (L, N_MOD * D), 0.02),
        "g_attn": 1.0 + nrm(ks[4], (L, D), 0.05),
        "w_in": nrm(ks[5], (L, D, IN_COLS), D ** -0.5),
        "q_norm_g": 1.0 + nrm(ks[6], (L, d), 0.05),
        "k_norm_g": 1.0 + nrm(ks[7], (L, d), 0.05),
        "lambda_q1": nrm(ks[8], (L, d), 0.1),
        "lambda_k1": nrm(ks[9], (L, d), 0.1),
        "lambda_q2": nrm(ks[10], (L, d), 0.1),
        "lambda_k2": nrm(ks[11], (L, d), 0.1),
        "diff_out_g": 1.0 + nrm(ks[12], (L, DIFF_VDIM), 0.05),
        "sb_out_g": 1.0 + nrm(ks[13], (L, d), 0.05),
        "w_out": nrm(ks[14], (L, MIX_WIDTH, D), MIX_WIDTH ** -0.5),
        "g_ffn": 1.0 + nrm(ks[15], (L, D), 0.05),
        "w_group": nrm(ks[16], (L, D, G), D ** -0.5),
        "b_group": nrm(ks[17], (L, G), 0.01),
        "w_erouter": nrm(ks[18], (L, G, D, E), D ** -0.5),
        "b_expert": nrm(ks[19], (L, G, E), 0.01),
        "w1": nrm(ks[20], (L, G, E, D, F), D ** -0.5),
        "w3": nrm(ks[21], (L, G, E, D, F), D ** -0.5),
        "w2": nrm(ks[22], (L, G, E, F, D), F ** -0.5),
    }

def reference(x, c, w_ada, b_ada, g_attn, w_in, q_norm_g, k_norm_g,
              lambda_q1, lambda_k1, lambda_q2, lambda_k2, diff_out_g, sb_out_g,
              w_out, g_ffn, w_group, b_group, w_erouter, b_expert, w1, w3, w2):
    B, S, D = x.shape
    d = HEAD_DIM
    qk_scale = 1.0 / math.sqrt(d)
    for layer in range(DEPTH):
        lambda_init = 0.8 - 0.6 * math.exp(-0.3 * layer)
        mod = jax.nn.silu(c) @ w_ada[layer] + b_ada[layer]
        sh_a, sc_a, gt_a, sh_f, sc_f, gt_f = jnp.split(mod, N_MOD, axis=-1)

        h = modulate(rms_norm(x, g_attn[layer]), sh_a, sc_a)
        proj = h @ w_in[layer]
        cuts = np.cumsum([DIFF_QK, DIFF_QK, DIFF_V, SB_W, SB_W])
        dq, dk, dv, sq, sk, sv = jnp.split(proj, cuts.tolist(), axis=-1)

        dq = dq.reshape(B, S, DIFF_HEADS, 2, d).transpose(0, 2, 3, 1, 4)
        dk = dk.reshape(B, S, DIFF_HEADS, 2, d).transpose(0, 2, 3, 1, 4)
        dq = rms_norm(dq, q_norm_g[layer]) * qk_scale
        dk = rms_norm(dk, k_norm_g[layer])
        dv = dv.reshape(B, S, DIFF_HEADS, DIFF_VDIM).transpose(0, 2, 1, 3)
        lam = (jnp.exp(jnp.sum(lambda_q1[layer] * lambda_k1[layer]).astype(jnp.float32))
               - jnp.exp(jnp.sum(lambda_q2[layer] * lambda_k2[layer]).astype(jnp.float32))
               + lambda_init)
        a_out = diff_attention(dq, dk, dv, lam)
        a_out = rms_norm(a_out, diff_out_g[layer]) * (1.0 - lambda_init)
        a_out = a_out.reshape(B, S, DIFF_V)

        sq = sq.reshape(B, S, SB_HEADS, d).transpose(0, 2, 1, 3)
        sk = sk.reshape(B, S, SB_HEADS, d).transpose(0, 2, 1, 3)
        sv = sv.reshape(B, S, SB_HEADS, d).transpose(0, 2, 1, 3)
        b_out = stick_breaking_attention(sq, sk, sv)
        b_out = rms_norm(b_out, sb_out_g[layer]).reshape(B, S, SB_W)

        y = jnp.concatenate([a_out, b_out], axis=-1) @ w_out[layer]
        x = x + gt_a[:, None, :] * y

        h = modulate(rms_norm(x, g_ffn[layer]), sh_f, sc_f)
        y = hier_moe(h, w_group[layer], b_group[layer], w_erouter[layer], b_expert[layer],
                     w1[layer], w3[layer], w2[layer])
        x = x + gt_f[:, None, :] * y
    return x


_drawn_inputs = setup_inputs


def setup_inputs(seed=0):
    import zlib

    import numpy as np

    out = dict(_drawn_inputs(seed))
    spreads = {}
    factors = {'g_attn': 3.439,
     'q_norm_g': 6.832,
     'k_norm_g': 7.317,
     'lambda_q1': 4.368,
     'lambda_k1': 8.0,
     'lambda_q2': 8.0,
     'diff_out_g': 5.338,
     'sb_out_g': 4.548,
     'g_ffn': 3.164,
     'b_group': 8.0,
     'b_expert': 8.0}
    for name, (base, spread) in spreads.items():
        noise = np.random.default_rng([zlib.crc32(name.encode()), seed]).standard_normal(out[name].shape)
        drawn = base * np.exp(spread * noise) if base else spread * noise
        out[name] = __import__('jax').numpy.asarray(drawn.astype(out[name].dtype))
    for name, factor in factors.items():
        out[name] = (out[name] * factor).astype(out[name].dtype)
    return out
```

```python
from contextlib import ExitStack

import concourse.bass as bass
from concourse import mybir

F32 = mybir.dt.float32
BF16 = mybir.dt.bfloat16
I32 = mybir.dt.int32
ALU = mybir.AluOpType
ACT = mybir.ActivationFunctionType
X = mybir.AxisListType.X

P = 128
T = 512
D = 1024
NT = T // P
KD = D // P
HD = 64
DH = 4
SH = 8
G = 4
EG = 8
E = G * EG
F = 256
FC = F // P
NR = G + G * EG
C = 64
MAXOV = 2 * T // (C + 1)
SLOTS = C * (E + MAXOV)
SKIP = 60000
EPS = 1e-6
LAMBDA_INIT = 0.2
PADS = 2 * -(-SLOTS // P)

ZOFF = {0: 0, 1: 512, 3: 896, 2: 1024}
ZCOLS = 1280


def plan_jobs():
    head = [("qk", n) for n in range(8)] + [("v", t, 0) for t in range(NT)] + [("gate", 0, 0), ("gate", 0, 1)]
    steps = {s: [] for s in range(20)}
    for n in range(4):
        steps[n].append(("sq", n))
        steps[4 + n].append(("sk", n))
        steps[8 + n].append(("v", n, 1))
    steps[2].insert(0, ("col", 2))
    steps[7].insert(0, ("col", 3))
    steps[8].insert(0, ("shift_router",))
    steps[12].append(("gate", 1, 0))
    steps[13].append(("gate", 1, 1))
    order = head + [j for s in range(20) for j in steps[s]]
    return head, steps, {j: n for n, j in enumerate(order)}


SHIFT_A, SCALE_A, GATE_A, SHIFT_F, SCALE_F, GATE_F = range(6)
PIECES = [("ada", SHIFT_A, 0), ("ada", SHIFT_A, 1), ("ada", SCALE_A, 0), ("ada", SCALE_A, 1),
          ("in", 0), ("in", 1), ("in", 2), ("ada", GATE_A, 0), ("ada", GATE_A, 1),
          ("in", 3), ("ada", SHIFT_F, 0), ("ada", SHIFT_F, 1),
          ("in", 4), ("ada", SCALE_F, 0), ("ada", SCALE_F, 1),
          ("in", 5), ("ada", GATE_F, 0), ("ada", GATE_F, 1), ("out", 0), ("out", 1)]
NSTAGE = 3
PIECE_AT = {p: n for n, p in enumerate(PIECES)}
ADA_ORDER = [SHIFT_A, SCALE_A, GATE_A, SHIFT_F, SCALE_F, GATE_F]


DIFF_STEPS, STICK_STEPS = NT * DH + 2, SH + 4


def fin_step(f):
    return 4 * f + 5 if f < DH else DIFF_STEPS + 2 * (f - DH) + 3


def plan_transposes():
    order = []
    for s in range(DIFF_STEPS + STICK_STEPS):
        if s >= DIFF_STEPS:
            order += [("fin", f) for f in range(DH) if s == fin_step(f) + 2]
        if 1 <= s <= NT * DH:
            order.append(("unit", s - 1))
        if s < DIFF_STEPS:
            order += [("fin", f) for f in range(DH) if s == fin_step(f) + 2]
        order += [("fin", f) for f in range(DH, 2 * DH) if s == fin_step(f) + 2]
    return order, {w: n for n, w in enumerate(order)}


def plan_releases(job_no):
    freed, count = {}, [0, 0]
    for job, n in sorted(job_no.items(), key=lambda kv: kv[1]):
        if job[0] == "qk":
            freed[job] = ("qk", job[1] + 1)
        else:
            count[n % 2] += 1
            freed[job] = (n % 2, count[n % 2])
    return freed


def hymba_block(nc, x, c, w_ada, b_ada, g_attn, w_in, q_norm_g, k_norm_g, lambda_q1, lambda_k1,
                lambda_q2, lambda_k2, diff_out_g, sb_out_g, w_out, g_ffn, w_group, b_group,
                w_erouter, b_expert, w1, w3, w2, out):
    head_jobs, step_jobs, job_no = plan_jobs()
    job_at = {n: job for job, n in job_no.items()}
    T_order, T_no = plan_transposes()
    freed = plan_releases(job_no)

    xn_dram = nc.dram_tensor("xn_rows", (T, D), F32, kind="Internal").ap()
    table_dram = nc.dram_tensor("slot_table", (P * PADS // 2, 2), I32, kind="Internal").ap()
    y_dram = nc.dram_tensor("pair_rows", (2 * T, D), F32, kind="Internal").ap()

    with ExitStack() as ctx:
        def sb(name, shape, dt=F32):
            return ctx.enter_context(nc.sbuf_tensor(name, shape, dt))

        def sem(name):
            return ctx.enter_context(nc.semaphore(name))

        xr = sb("xr", [P, NT, D])
        stage = sb("stage", [P, NSTAGE, 4096])
        hT = sb("hT", [P, KD, T])
        qkT = sb("qkT", [P, 16, T])
        val = sb("val", [P, NT, 1024])
        mixT = sb("mixT", [P, KD, T])
        gates = sb("gates", [P, 2, D])
        alibi = sb("alibi", [P, DH, T])
        work = sb("work", [P, 8192])
        obuf = sb("obuf", [P, 4, T])
        consts = sb("consts", [P, 5, P])
        wr = sb("wr", [P, KD, NR])
        wrA = sb("wrA", [P, KD, NR])
        small = sb("small", [P, 288])
        router_row = sb("router_row", [1, 2, NR])
        tri_bf = sb("tri_bf", [P, P], BF16)
        ones_bf = sb("ones_bf", [P, P], BF16)
        table_sb = sb("table_sb", [P, E // 2, 2], I32)
        table_ov = sb("table_ov", [C, 2], I32)
        ints = sb("ints", [P, 96], I32)
        records = sb("records", [P, NT, 2, 2], I32)
        plan = sb("plan", [1, MAXOV + 2], I32)

        ident, negtri, negones, ones, halves = (consts[:, n, :] for n in range(5))
        acc = mixT[:, 4:8, :].rearrange("p (v a) t -> p v (a t)", v=2)
        xn = qkT[:, 0:8, :].rearrange("p (t a) c -> p t (a c)", t=NT)
        prob = work[:, 0:2048].rearrange("p (r m k) -> p r m k", r=2, m=2)
        probT = work[:, 2048:3072].rearrange("p (r k) -> p r k", r=2)
        sqb = work[:, 3072:4096].rearrange("p (r k) -> p r k", r=2)
        rqk = work[:, 4096:5120].rearrange("p (r k) -> p r k", r=2)
        soft = work[:, 3072:3072 + 2 * ZCOLS].rearrange("p (r k) -> p r k", r=2)
        stick = work[:, 5632:5632 + 2 * ZCOLS].rearrange("p (r k) -> p r k", r=2)
        xnb = work[:, 0:2048].rearrange("p (r k) -> p r k", r=2)
        x2T = work[:, 2048:4096].rearrange("p (r k) -> p r k", r=2)
        rows = work[:, 4096:6144].rearrange("p (r k) -> p r k", r=2)
        heT = work[:, 0:2048].rearrange("p (r k) -> p r k", r=2)
        ysb = work[:, 2048:4096].rearrange("p (r k) -> p r k", r=2)
        gact = work[:, 6144:6400].rearrange("p (r k) -> p r k", r=2)
        geT = work[:, 6400:6656].rearrange("p (r k) -> p r k", r=2)
        rt = work[:, 6656:8192]
        hT_f = hT[:].rearrange("p a b -> p (a b)")
        qk_f = qkT[:].rearrange("p a b -> p (a b)")
        val_f = val[:].rearrange("p a b -> p (a b)")
        slots = [
            (hT_f[:, 0:2048], hT_f[:, 2048:4096], stage[:, 2, 0:2048]),
            (qk_f[:, 0:2048], qk_f[:, 2048:4096], qk_f[:, 4096:6144]),
            (qk_f[:, 6144:8192], val_f[:, 0:2048], val_f[:, 2048:4096]),
            (stage[:, 0, 0:2048], stage[:, 0, 2048:4096], stage[:, 1, 0:2048]),
        ]
        w1s = [s[0].rearrange("p (k f) -> p k f", k=KD) for s in slots]
        w3s = [s[1].rearrange("p (k f) -> p k f", k=KD) for s in slots]
        w2s = [s[2].rearrange("p (f n) -> p f n", f=FC) for s in slots]

        ramp = work[:, 7168:7680].bitcast(I32)
        lam_in = work[:, 7936:8192].rearrange("p (v d) -> p v d", v=4)
        fill = work[:, 7680:7680 + PADS].bitcast(I32)
        masks = rt[:, 1200:1392].bitcast(BF16).rearrange("p (k t e) -> p k t e", k=3, t=NT)
        exp_g = rt[:, 1400:1416]
        exp_d = rt[:, 1416:1420]

        def fin_pair(t):
            n = t * 2048
            return stage[:].rearrange("p a b -> p (a b)")[:, n:n + 2048].rearrange("p (k n) -> p k n", k=2)

        at = [0]

        def cols(n):
            at[0] += n
            return small[:, at[0] - n:at[0]]

        c_col, cs = cols(8), cols(8)
        b_col = cols(32).rearrange("p (v k) -> p v k", v=4)
        g_col = cols(16).rearrange("p (v k) -> p v k", v=2)
        mod = cols(32).rearrange("p (v k) -> p v k", v=4)
        gqk, out_g = cols(2), cols(2)
        eps = cols(1)
        ssx, rx, ss2, r2 = cols(4), cols(4), cols(4), cols(4)
        lam, neglam = cols(4), cols(1)
        mx, nmx, lsum, rl = (cols(4).rearrange("p (r m) -> p r m", r=2) for _ in range(4))
        sso, ro = cols(16).rearrange("p (r k) -> p r k", r=2), cols(16).rearrange("p (r k) -> p r k", r=2)
        wpair = cols(8).rearrange("p (k t) -> p k t", k=2)
        rev = cols(8)
        e64 = cols(32)
        zero32 = cols(32)
        b_iota = cols(MAXOV + 1)
        assert at[0] <= 288

        banks = ctx.enter_context(nc.psum_tensor("banks", [P, 8, 512], F32))
        zps = [banks[:, 3 * r:3 * r + 3, :].rearrange("p b k -> p (b k)") for r in range(2)]

        x_in, params_in, fill_in = sem("x_in"), sem("params_in"), sem("fill_in")
        stage_in = [sem(f"stage_in{n}") for n in range(NSTAGE)]
        consts_ready, memset_ready = sem("consts_ready"), sem("memset_ready")
        silu_c, acc_done, acc_half, ada_used = sem("silu_c"), sem("acc_done"), sem("acc_half"), sem("ada_used")
        col_a, mod_a = sem("col_a"), sem("mod_a")
        xn_ready, xT_done = sem("xn_ready"), sem("xT_done")
        hT_act, hT_dve = sem("hT_act"), sem("hT_dve")
        job_done = sem("job_done")
        bank_free = [sem("bank_free0"), sem("bank_free1")]
        sq_ready, norm_done, rqk_ready = sem("sq_ready"), sem("norm_done"), sem("rqk_ready")
        qk_act, qk_dve, v_ready = sem("qk_act"), sem("qk_dve"), sem("v_ready")
        alibi_ready, lam_ready = sem("alibi_ready"), sem("lam_ready")
        score_done, max_ready, exp_ready, prob_ready = (sem(n) for n in (
            "score_done", "max_ready", "exp_ready", "prob_ready"))
        T_done, probT_ready, pv_done = sem("T_done"), sem("probT_ready"), sem("pv_done")
        o_copied, o_sums, o_rstd, o_ready, oT_done, mix_ready = (sem(n) for n in (
            "o_copied", "o_sums", "o_rstd", "o_ready", "oT_done", "mix_ready"))
        z_done, ln_ready, soft_raw, soft_ready, tri_done, stick_raw, stick_ready, spv_done = (sem(n) for n in (
            "z_done", "ln_ready", "soft_raw", "soft_ready", "tri_done", "stick_raw", "stick_ready", "spv_done"))
        y_done, y_scaled, x2_ready = sem("y_done"), sem("y_scaled"), sem("x2_ready")
        xnb_ready, xn_stored, fT_done, x2T_ready, logits_done = (sem(n) for n in (
            "xnb_ready", "xn_stored", "fT_done", "x2T_ready", "logits_done"))
        wrA_ready, row_ready, gate_ready = sem("wrA_ready"), sem("row_ready"), sem("gate_ready")
        g_exp_in, g_exp, d_in, d_exp = sem("g_exp_in"), sem("g_exp"), sem("d_in"), sem("d_exp")
        masks_ready, rank_done, pos_ready, scattered, table_in = (sem(n) for n in (
            "masks_ready", "rank_done", "pos_ready", "scattered", "table_in"))
        plan_ready = sem("plan_ready")
        w_in_slot = [sem(f"w_slot{n}") for n in range(4)]
        rows_in = [sem("rows_in0"), sem("rows_in1")]
        rows_zero = sem("rows_zero")
        eT_done, he_mul, heT_ready, h_done, silu_ready, ge_ready, ye_done, ysb_ready = (sem(n) for n in (
            "eT_done", "he_mul", "heT_ready", "h_done", "silu_ready", "ge_ready", "ye_done", "ysb_ready"))
        y_stored = [sem("y_stored0"), sem("y_stored1")]
        ov_table = sem("ov_table")
        pairs_in = [sem(f"pairs_in{n}") for n in range(NT)]
        fin_a, fin_b, fin_c, out_stored = sem("fin_a"), sem("fin_b"), sem("fin_c"), sem("out_stored")
        eps_ready, consts_dve, lam_exp = sem("eps_ready"), sem("consts_dve"), sem("lam_exp")
        act_chain, dve_chain, pool_chain = sem("act_chain"), sem("dve_chain"), sem("pool_chain")

        x_rows = x.rearrange("b (t p) d -> (b p) t d", p=P)
        out_rows = out.rearrange("b (t p) d -> (b p) t d", p=P)
        ada_v = w_ada.rearrange("l (p k) n -> (l p) k n", k=KD)
        in_v = w_in.rearrange("l (p k) n -> (l p) k n", k=KD)
        out_v = w_out.rearrange("l (k p) n -> (l p) k n", p=P)
        w1_v = w1.rearrange("l g e (p k) f -> (l g e) p (k f)", k=KD)
        w3_v = w3.rearrange("l g e (p k) f -> (l g e) p (k f)", k=KD)
        w2_v = w2.rearrange("l g e (f p) n -> (l g e) p f n", p=P)
        b_cols_v = b_ada.rearrange("l (v p k) -> (l p) v k", v=6, k=KD)
        w2_dst = [s[2].rearrange("p (f n) -> p f n", f=FC) for s in slots]

        def piece_at(p):
            n = PIECE_AT[p]
            return stage[:, n % NSTAGE, :], stage_in[n % NSTAGE], 16 * (n // NSTAGE + 1)

        def row(v):
            return v.rearrange("l n -> (l n)").partition_broadcast(P)

        params = [
            (c_col, c.rearrange("b (p k) -> (b p) k", k=KD)),
            (b_col[:, 0:2, :], b_cols_v[:, SHIFT_A:SCALE_A + 1, :]),
            (b_col[:, 2:4, :], b_cols_v[:, SHIFT_F:SCALE_F + 1, :]),
            (g_col[:, 0, :], g_attn.rearrange("l (p k) -> (l p) k", k=KD)),
            (g_col[:, 1, :], g_ffn.rearrange("l (p k) -> (l p) k", k=KD)),
            (out_g[:, 0:1], diff_out_g.rearrange("l (p o) -> (l p) o", o=1)),
            (gates[:, 0, :], row(b_ada[:, GATE_A * D:(GATE_A + 1) * D])),
            (gates[:, 1, :], row(b_ada[:, GATE_F * D:(GATE_F + 1) * D])),
            (wr[:, :, 0:G], w_group.rearrange("l (p k) g -> (l p) k g", k=KD)),
            (router_row[0:1, 0, 0:G], b_group),
            (router_row[0:1, 0, G:NR], b_expert.rearrange("l g e -> l (g e)")),
        ]
        for g in range(G):
            params.append((wr[:, :, G + g * EG:G + (g + 1) * EG], w_erouter[:, g].rearrange("l (p k) e -> (l p) k e", k=KD)))
        for n, v in enumerate((lambda_q1, lambda_k1, lambda_q2, lambda_k2)):
            params.append((lam_in[:, n, :], row(v)))
        for m in range(2):
            part = slice(m * HD, (m + 1) * HD)
            params.append((gqk[part, 0:1], q_norm_g.rearrange("l (p o) -> (l p) o", o=1)))
            params.append((gqk[part, 1:2], k_norm_g.rearrange("l (p o) -> (l p) o", o=1)))
            params.append((out_g[part, 1:2], sb_out_g.rearrange("l (p o) -> (l p) o", o=1)))
        N_PARAMS = len(params)

        IN_LAST = {0: ("qk", 3), 1: ("qk", 7), 2: ("v", 3, 0), 3: ("sq", 3), 4: ("sk", 3), 5: ("v", 3, 1)}

        block = ctx.enter_context(nc.Block())

        @block.sync
        def _(sp):
            sp.dma_start(xr[:], x_rows).then_inc(x_in, 16)
            for n, piece in enumerate(PIECES):
                dst, arrived, _ = piece_at(piece)
                if n >= NSTAGE:
                    old = PIECES[n - NSTAGE]
                    if old[0] == "ada":
                        sp.wait_ge(ada_used, 2 * ADA_ORDER.index(old[1]) + old[2] + 1)
                    else:
                        sp.wait_ge(job_done, job_no[IN_LAST[old[1]]] + 1)
                if piece[0] == "ada":
                    v, half = piece[1:]
                    src = ada_v[:, 4 * half:4 * half + 4, v * D:(v + 1) * D]
                    dst = dst.rearrange("p (k n) -> p k n", k=4)
                elif piece[0] == "in":
                    src = in_v[:, :, piece[1] * 512:(piece[1] + 1) * 512]
                    dst = dst.rearrange("p (k n) -> p k n", k=KD)
                else:
                    src = out_v[:, 4 * piece[1]:4 * piece[1] + 4, :]
                    dst = dst.rearrange("p (k n) -> p k n", k=4)
                sp.dma_start(dst, src).then_inc(arrived, 16)

            def load_expert(e, s):
                sp.dma_start(slots[s][0], w1_v[e]).then_inc(w_in_slot[s], 16)
                sp.dma_start(slots[s][1], w3_v[e]).then_inc(w_in_slot[s], 16)
                sp.dma_start(w2_dst[s], w2_v[e]).then_inc(w_in_slot[s], 16)

            sp.wait_ge(job_done, job_no[("v", 3, 1)] + 1)
            sp.wait_ge(ada_used, 12)
            load_expert(0, 0)
            sp.wait_ge(spv_done, SH)
            load_expert(1, 1)
            load_expert(2, 2)
            sp.wait_ge(y_done, 2 * NT)
            load_expert(3, 3)
            with sp.Fori(1, E // 4) as it:
                for s in range(4):
                    sp.wait_ge(ye_done, it * 4 + (s - 3))
                    load_expert(it * 4 + s, s)
            sp.wait_ge(plan_ready, 1)
            nb = sp.value_load(plan[0:1, MAXOV + 1:MAXOV + 2], min_val=0, max_val=MAXOV)
            with sp.If(nb > 0):
                with sp.Fori(0, nb) as b:
                    sp.wait_ge(ye_done, b + E)
                    e = sp.value_load(plan[0:1, bass.ds(b, 1)], min_val=0, max_val=E - 1)
                    load_expert(e, 0)
            sp.wait_ge(y_stored[1], 16 * (E // 4))
            sp.wait_ge(y_stored[0], nb * 16 + 16 * (E // 4))
            for t in range(NT):
                dst = fin_pair(t)
                sp.dma_start(dst, y_dram.rearrange("(k t p) n -> t p k n", k=2, p=P)[t]).then_inc(pairs_in[t], 16)
            for t in range(NT):
                sp.wait_ge(fin_c, t + 1)
                sp.dma_start(out_rows[:, t, :], xr[:, t, :]).then_inc(out_stored, 16)
            sp.wait_ge(out_stored, 16 * NT)
            sp.wait_ge(xn_stored, 16 * NT)

        @block.gpsimd
        def _(pool):
            chain = [0]

            def link(ins):
                chain[0] += 1
                ins.then_inc(pool_chain, 1)
                pool.wait_ge(pool_chain, chain[0])

            g = nc.gpsimd
            link(g.memset(consts[:, 0, :], 1.0))
            g.affine_select(out=ident, in_=ident, pattern=[[-1, P]], compare_op=ALU.is_equal, fill=0.0,
                            base=0, channel_multiplier=1).then_inc(consts_ready, 1)
            link(g.memset(negtri, -1.0))
            g.affine_select(out=negtri, in_=negtri, pattern=[[-1, P]], compare_op=ALU.is_ge, fill=0.0,
                            base=0, channel_multiplier=1).then_inc(consts_ready, 1)
            g.memset(negones, -1.0).then_inc(consts_ready, 1)
            link(g.memset(tri_bf[:], 1.0))
            g.affine_select(out=tri_bf[:], in_=tri_bf[:], pattern=[[1, P]], compare_op=ALU.is_gt, fill=0.0,
                            base=0, channel_multiplier=-1).then_inc(consts_ready, 1)
            link(g.iota(ramp, pattern=[[-1, T]], base=3 * P, channel_multiplier=1))
            for h in range(DH):
                slope = 2.0 ** (-8.0 * (h + 1) / DH)
                link(g.tensor_scalar(alibi[:, h, :], ramp, -slope, None, ALU.mult))
                g.affine_select(out=alibi[:, h, :], in_=alibi[:, h, :], pattern=[[-1, T]], compare_op=ALU.is_ge,
                                fill=-1e30, base=3 * P, channel_multiplier=1).then_inc(alibi_ready, 1)
            g.memset(fill, SKIP).then_inc(memset_ready, 1)
            g.iota(records[:, :, :, 0], pattern=[[P, NT], [0, 2]], base=0, channel_multiplier=1).then_inc(memset_ready, 1)
            g.iota(records[:, :, :, 1], pattern=[[P, NT], [T, 2]], base=0, channel_multiplier=1).then_inc(memset_ready, 1)
            link(g.iota(ints[:, 0:32], pattern=[[C, E]], base=0, channel_multiplier=0))
            g.tensor_copy(e64, ints[:, 0:32]).then_inc(memset_ready, 1)
            link(g.iota(ints[:, 32:32 + MAXOV + 1], pattern=[[1, MAXOV + 1]], base=0, channel_multiplier=0))
            g.tensor_copy(b_iota, ints[:, 32:32 + MAXOV + 1]).then_inc(memset_ready, 1)
            link(g.iota(ints[:, 72:80], pattern=[[-1, 8]], base=8, channel_multiplier=0))
            g.tensor_copy(rev, ints[:, 72:80]).then_inc(memset_ready, 1)
            pool.wait_ge(memset_ready, 6)
            g.dma_start(table_dram.rearrange("(p n) two -> p (n two)", p=P), fill).then_inc(fill_in, 16)

            def mask_tiles(v, r, ready):
                v0 = v[:, r, :]
                a = v0[:, 0:1024].rearrange("p (b k) -> p b k", b=2)[:, :, 0:P]
                g.affine_select(out=a, in_=a, pattern=[[0, 2], [1, P]], compare_op=ALU.is_gt, fill=0.0,
                                base=0, channel_multiplier=-1)
                a = v0[:, 896:1152].rearrange("p (b k) -> p b k", b=2)
                g.affine_select(out=a, in_=a, pattern=[[0, 2], [1, P]], compare_op=ALU.is_gt, fill=0.0,
                                base=0, channel_multiplier=-1).then_inc(ready, 1)

            pool.wait_ge(fill_in, 16)
            for n in range(SH + 1):
                if n < SH:
                    pool.wait_ge(soft_raw, n + 1)
                    mask_tiles(soft, n % 2, soft_ready)
                if n >= 1:
                    pool.wait_ge(stick_raw, n)
                    mask_tiles(stick, (n - 1) % 2, stick_ready)

            for w in range(2 * NT):
                pool.wait_ge(y_scaled, w + 1)
                xh = xr[:, w // 2, (w % 2) * 512:(w % 2) * 512 + 512]
                g.tensor_tensor(xh, xh, obuf[:, w % 2, :], ALU.add).then_inc(x2_ready, 1)
                if w == 1:
                    g.memset(rows, 0.0).then_inc(rows_zero, 1)

            pool.wait_ge(pos_ready, 1)
            for t in range(NT):
                for k in range(2):
                    g.indirect_dma_start(
                        table_dram, bass.IndirectOffsetOnAxis(ap=ints[:, 80 + k * NT + t:81 + k * NT + t], axis=0),
                        records[:, t, k, :], None).then_inc(scattered, 16)
            pool.wait_ge(scattered, 16 * 2 * NT)
            g.dma_start(table_sb[:], table_dram[0:C * E, :].rearrange("(b p) two -> p b two", p=P)).then_inc(table_in, 16)
            pool.wait_ge(table_in, 16)
            pool.wait_ge(xn_stored, 16 * NT)
            pool.wait_ge(rows_zero, 1)

            def gather(q):
                if q >= 2:
                    pool.wait_ge(eT_done, q - 1)
                g.indirect_dma_start(rows[:, q % 2, :], None, xn_dram,
                                     bass.IndirectOffsetOnAxis(ap=table_sb[:, q, 0:1], axis=0),
                                     bounds_check=T - 1, oob_is_err=False).then_inc(rows_in[q % 2], 16)

            gather(0)
            for q in range(E // 2):
                if q + 1 < E // 2:
                    gather(q + 1)
                pool.wait_ge(ysb_ready, q + 1)
                g.indirect_dma_start(y_dram, bass.IndirectOffsetOnAxis(ap=table_sb[:, q, 1:2], axis=0),
                                     ysb[:, q % 2, :], None,
                                     bounds_check=2 * T - 1, oob_is_err=False).then_inc(y_stored[q % 2], 16)
            pool.wait_ge(plan_ready, 1)
            nb = pool.value_load(plan[0:1, MAXOV + 1:MAXOV + 2], min_val=0, max_val=MAXOV)
            for b in range(MAXOV):
                with pool.If(nb > b):
                    pool.wait_ge(y_stored[0], 16 * (E // 4 + b))
                    g.dma_start(table_ov[:], table_dram[C * (E + b):C * (E + b + 1), :]).then_inc(ov_table, 16)
                    pool.wait_ge(ov_table, 16 * (b + 1))
                    g.indirect_dma_start(rows[0:C, 0, :], None, xn_dram,
                                         bass.IndirectOffsetOnAxis(ap=table_ov[:, 0:1], axis=0),
                                         bounds_check=T - 1, oob_is_err=False).then_inc(rows_in[0], 16)
                    pool.wait_ge(ysb_ready, E // 2 + b + 1)
                    g.indirect_dma_start(y_dram, bass.IndirectOffsetOnAxis(ap=table_ov[:, 1:2], axis=0),
                                         ysb[0:C, 0, :], None,
                                         bounds_check=2 * T - 1, oob_is_err=False).then_inc(y_stored[0], 16)

        @block.scalar
        def _(act):
            chain = [0]

            def link(ins):
                chain[0] += 1
                ins.then_inc(act_chain, 1)
                act.wait_ge(act_chain, chain[0])

            a = nc.scalar
            for dst, src in params:
                act.dma_start(dst, src).then_inc(params_in, 16)
            act.wait_ge(params_in, 16 * N_PARAMS)
            a.activation(cs, c_col, ACT.Silu).then_inc(silu_c, 1)
            a.preload_act_table_set("natural_log_exp_and_others")
            act.wait_ge(x_in, 16)
            act.wait_ge(eps_ready, 1)
            for t in range(NT):
                link(a.activation(hT_f[:, 0:D], xr[:, t, :], ACT.Square, accum_out=ssx[:, t:t + 1]))
            link(a.activation(rx, ssx, ACT.Ln, bias=eps, scale=1.0 / D))
            link(a.activation(rx, rx, ACT.Exp, scale=-0.5))
            for t in range(NT):
                a.activation(xn[:, t, :].rearrange("p (k j) -> p k j", k=KD),
                             xr[:, t, :].rearrange("p (j k) -> p k j", k=KD), ACT.Copy,
                             scale=rx[:, t:t + 1]).then_inc(xn_ready, 1)
            act.wait_ge(lam_ready, 1)
            a.activation(lam[:, 2:4], lam[:, 0:2], ACT.Exp).then_inc(lam_exp, 1)
            act.wait_ge(mod_a, 1)
            for k in range(1, KD, 2):
                act.wait_ge(xT_done, k + 1)
                a.activation(hT[:, k, :], banks[:, 2 + k % 4, :], ACT.Identity,
                             bias=mod[:, 0, k:k + 1], scale=mod[:, 1, k:k + 1]).then_inc(hT_act, 1)

            def qk_square(n):
                act.wait_ge(job_done, job_no[("qk", n)] + 1)
                if n >= 2:
                    act.wait_ge(norm_done, n - 1)
                a.activation(sqb[:, n % 2, :], banks[:, job_no[("qk", n)] % 2, :], ACT.Square).then_inc(sq_ready, 1)

            def qk_rstd(n):
                act.wait_ge(norm_done, n + 1)
                if n >= 2:
                    act.wait_ge(qk_dve, n - 1)
                link(a.activation(rqk[:, n % 2, :], banks[:, 2 + n % 2, :], ACT.Ln, bias=eps, scale=1.0 / HD))
                a.activation(rqk[:, n % 2, :], rqk[:, n % 2, :], ACT.Exp, scale=-0.5).then_inc(rqk_ready, 1)

            def job_evac(job):
                n = job_no[job]
                src = banks[:, n % 2, :]
                if job[0] == "v":
                    act.wait_ge(job_done, n + 1)
                    a.activation(val[:, job[1], job[2] * 512:job[2] * 512 + 512], src, ACT.Copy).then_inc(bank_free[n % 2], 1)
                elif job[0] == "sq":
                    act.wait_ge(job_done, n + 1)
                    a.activation(qkT[:, 8 + job[1], :], src, ACT.Copy, scale=HD ** -0.5).then_inc(bank_free[n % 2], 1)
                elif job[0] == "sk":
                    act.wait_ge(job_done, n + 1)
                    a.activation(qkT[:, 12 + job[1], :], src, ACT.Copy).then_inc(bank_free[n % 2], 1)

            for n in range(8):
                qk_square(n)
                if n >= 1:
                    qk_rstd(n - 1)
            qk_rstd(7)
            for job in head_jobs:
                job_evac(job)

            def exp_unit(u):
                h, i = u // NT, u % NT
                act.wait_ge(max_ready, u + 1)
                for m in range(2):
                    v = prob[:, u % 2, m, 0:(i + 1) * P]
                    ins = a.activation(v, v, ACT.Exp, bias=nmx[:, u % 2, m:m + 1], accum_out=lsum[:, u % 2, m:m + 1])
                ins.then_inc(exp_ready, 1)

            def probT_evac(u):
                i = u % NT
                act.wait_ge(T_done, T_no[("unit", u)] + 1)
                if u >= 2:
                    act.wait_ge(pv_done, u - 1)
                a.activation(probT[:, u % 2, 0:(i + 1) * P], banks[:, 6, 0:(i + 1) * P], ACT.Copy).then_inc(probT_ready, 1)

            def out_rstd(f):
                n = 4 if f < DH else 8
                act.wait_ge(o_sums, f + 1)
                link(a.activation(ro[:, f % 2, 0:n], sso[:, f % 2, 0:n], ACT.Ln, bias=eps, scale=n / 512.0))
                a.activation(ro[:, f % 2, 0:n], ro[:, f % 2, 0:n], ACT.Exp, scale=-0.5).then_inc(o_rstd, 1)

            def mix_evac(f):
                act.wait_ge(T_done, T_no[("fin", f)] + 1)
                if f == DH:
                    act.wait_ge(job_done, job_no[("gate", 1, 1)] + 1)
                a.activation(mixT[:, f, :], banks[:, 6, :], ACT.Copy,
                             scale=out_g[:, f // DH:f // DH + 1]).then_inc(mix_ready, 1)

            for s in range(DIFF_STEPS):
                if s >= 1:
                    for job in step_jobs.get(s - 1, ()):
                        job_evac(job)
                if s < 16:
                    exp_unit(s)
                if 1 <= s <= 16:
                    probT_evac(s - 1)
                for f in range(DH):
                    if s == fin_step(f):
                        out_rstd(f)
                    if s == fin_step(f) + 2:
                        mix_evac(f)

            for s in range(STICK_STEPS):
                for f in range(DH):
                    if DIFF_STEPS + s == fin_step(f) + 2:
                        mix_evac(f)
                if s < SH:
                    act.wait_ge(z_done, s + 1)
                    if s >= 2:
                        act.wait_ge(tri_done, s - 1)
                    v = soft[:, s % 2, :]
                    link(a.activation(v, zps[s % 2][:, 0:ZCOLS], ACT.Abs))
                    link(a.activation(v, v, ACT.Exp, scale=-1.0))
                    a.activation(v, v, ACT.Ln, bias=1.0).then_inc(ln_ready, 1)
                if 1 <= s <= SH:
                    act.wait_ge(tri_done, s)
                    if s >= 3:
                        act.wait_ge(spv_done, s - 2)
                    a.activation(stick[:, (s - 1) % 2, :], zps[(s - 1) % 2][:, 0:ZCOLS], ACT.Exp).then_inc(stick_raw, 1)
                for f in range(DH, 2 * DH):
                    if DIFF_STEPS + s == fin_step(f):
                        out_rstd(f)
                    if DIFF_STEPS + s == fin_step(f) + 2:
                        mix_evac(f)

            for t in range(NT):
                act.wait_ge(x2_ready, 2 * t + 2)
                link(a.activation(obuf[:, 2:4, :].rearrange("p a b -> p (a b)"), xr[:, t, :], ACT.Square,
                                  accum_out=ss2[:, t:t + 1]))
                link(a.activation(r2[:, t:t + 1], ss2[:, t:t + 1], ACT.Ln, bias=eps, scale=1.0 / D))
                link(a.activation(r2[:, t:t + 1], r2[:, t:t + 1], ACT.Exp, scale=-0.5))
                if t >= 2:
                    act.wait_ge(fT_done, t - 1)
                    act.wait_ge(xn_stored, 16 * t)
                a.activation(xnb[:, t % 2, :].rearrange("p (k j) -> p k j", k=KD),
                             xr[:, t, :].rearrange("p (j k) -> p k j", k=KD), ACT.Copy,
                             scale=r2[:, t:t + 1]).then_inc(xnb_ready, 1)
                act.wait_ge(xnb_ready, t + 1)
                act.dma_start(xn_dram[t * P:(t + 1) * P, :], xnb[:, t % 2, :]).then_inc(xn_stored, 16)
            act.wait_ge(g_exp_in, 1)
            a.activation(exp_g, exp_g, ACT.Exp).then_inc(g_exp, 1)
            act.wait_ge(d_in, 1)
            a.activation(exp_d, exp_d, ACT.Exp).then_inc(d_exp, 1)
            a.preload_act_table(ACT.Silu)

            def silu(n, r):
                act.wait_ge(h_done, n)
                a.activation(gact[:, r, :], banks[:, 2 + r, 0:P], ACT.Silu).then_inc(silu_ready, 1)

            with act.Fori(0, E // 4) as it:
                for s in range(4):
                    silu(it * 4 + (s + 1), s % 2)
            act.wait_ge(plan_ready, 1)
            nb = act.value_load(plan[0:1, MAXOV + 1:MAXOV + 2], min_val=0, max_val=MAXOV)
            with act.If(nb > 0):
                with act.Fori(0, nb) as b:
                    silu(b + (E + 1), 0)
            for t in range(NT):
                act.wait_ge(pairs_in[t], 16)
                a.activation(fin_pair(t)[:, 1, :], fin_pair(t)[:, 1, :], ACT.Copy,
                             scale=wpair[:, 1, t:t + 1]).then_inc(fin_a, 1)

        @block.vector
        def _(dve):
            chain = [0]

            def link(ins):
                chain[0] += 1
                ins.then_inc(dve_chain, 1)
                dve.wait_ge(dve_chain, chain[0])

            v = nc.vector
            v.memset(eps, EPS).then_inc(eps_ready, 1)
            v.memset(ones, 1.0).then_inc(consts_dve, 1)
            v.memset(ones_bf[:], 1.0).then_inc(consts_dve, 1)
            v.memset(zero32, 0.0).then_inc(consts_dve, 1)
            link(v.memset(halves, 0.0))
            v.memset(halves[0:HD, 0:HD], 1.0).then_inc(consts_dve, 1)
            v.memset(halves[HD:P, HD:P], 1.0).then_inc(consts_dve, 1)
            dve.wait_ge(params_in, 16 * N_PARAMS)
            for m in range(2):
                ins = v.tensor_tensor_reduce(out=obuf[:, m, 0:HD], in0=lam_in[:, 2 * m, :], in1=lam_in[:, 2 * m + 1, :],
                                             scale=1.0, scalar=0.0, op0=ALU.mult, op1=ALU.add,
                                             accum_out=lam[:, m:m + 1])
            ins.then_inc(lam_ready, 1)
            link(v.tensor_scalar(gqk[:, 0:1], gqk[:, 0:1], HD ** -0.5, None, ALU.mult))
            link(v.tensor_scalar(out_g[:, 0:1], out_g[:, 0:1], 1.0 - LAMBDA_INIT, None, ALU.mult))

            def ada(n):
                vec = ADA_ORDER[n]
                if n in (2, 3):
                    dve.wait_ge(col_a, 1)
                if n == 4:
                    dve.wait_ge(job_done, job_no[("gate", 0, 1)] + 1)
                if n == 5:
                    dve.wait_ge(job_done, job_no[("col", 2)] + 1)
                dst = acc[:, n % 2, :]
                for half in range(2):
                    src, arrived, value = piece_at(("ada", vec, half))
                    src = src.rearrange("p (k n) -> p k n", k=4)
                    dve.wait_ge(arrived, value)
                    for k in range(4):
                        s = cs[:, 4 * half + k:4 * half + k + 1]
                        if half == 0 and k == 0:
                            link(v.tensor_scalar(dst, src[:, k, :], s, None, ALU.mult))
                            continue
                        ins = v.scalar_tensor_tensor(out=dst, in0=src[:, k, :], scalar=s, in1=dst,
                                                     op0=ALU.mult, op1=ALU.add)
                        if k < 3:
                            link(ins)
                        else:
                            ins.then_inc(ada_used, 1)
                            dve.wait_ge(ada_used, 2 * n + half + 1)

            dve.wait_ge(silu_c, 1)
            ada(0)
            ada(1)
            dve.wait_ge(col_a, 1)
            v.tensor_tensor(mod[:, 0, :], banks[:, 0, 0:8], b_col[:, 0, :], ALU.add)
            link(v.tensor_tensor(mod[:, 1, :], banks[:, 0, 8:16], b_col[:, 1, :], ALU.add))
            v.scalar_tensor_tensor(out=mod[:, 1, :], in0=mod[:, 1, :], scalar=1.0, in1=g_col[:, 0, :],
                                   op0=ALU.add, op1=ALU.mult).then_inc(mod_a, 1)
            dve.wait_ge(mod_a, 1)
            for k in range(0, KD, 2):
                dve.wait_ge(xT_done, k + 1)
                v.tensor_scalar(hT[:, k, :], banks[:, 2 + k % 4, :], mod[:, 1, k:k + 1], mod[:, 0, k:k + 1],
                                ALU.mult, ALU.add).then_inc(hT_dve, 1)
            dve.wait_ge(lam_exp, 1)
            link(v.tensor_tensor(neglam, lam[:, 3:4], lam[:, 2:3], ALU.subtract))
            link(v.tensor_scalar(neglam, neglam, -LAMBDA_INIT, None, ALU.add))

            for n in range(8):
                dve.wait_ge(rqk_ready, n + 1)
                b = job_no[("qk", n)] % 2
                v.scalar_tensor_tensor(out=qkT[:, n, :], in0=banks[:, b, :], scalar=gqk[:, n // 4:n // 4 + 1],
                                       in1=rqk[:, n % 2, :], op0=ALU.mult, op1=ALU.mult).then_inc(qk_dve, 1)

            def job_evac(job):
                n = job_no[job]
                src = banks[:, n % 2, :]
                if job[0] == "gate":
                    dve.wait_ge(job_done, n + 1)
                    dst = gates[:, job[1], job[2] * 512:job[2] * 512 + 512]
                    v.tensor_tensor(dst, src, dst, ALU.add).then_inc(bank_free[n % 2], 1)
                elif job[0] == "col":
                    dve.wait_ge(job_done, n + 1)
                    w = job[1]
                    v.tensor_tensor(mod[:, w, :], src[:, 0:8], b_col[:, w, :], ALU.add).then_inc(bank_free[n % 2], 1)
                    dve.wait_ge(bank_free[n % 2], freed[job][1])
                    if w == 3:
                        link(v.scalar_tensor_tensor(out=mod[:, 3, :], in0=mod[:, 3, :], scalar=1.0,
                                                    in1=g_col[:, 1, :], op0=ALU.add, op1=ALU.mult))
                        v.tensor_tensor(wrA[:], wr[:], mod[:, 3, :].unsqueeze(2).to_broadcast([P, KD, NR]),
                                        ALU.mult).then_inc(wrA_ready, 1)
                elif job[0] == "shift_router":
                    dve.wait_ge(job_done, n + 1)
                    v.tensor_tensor(router_row[0:1, 1, :], src[0:1, 0:NR], router_row[0:1, 0, :],
                                    ALU.add).then_inc(bank_free[n % 2], 1)

            ada(2)
            for job in head_jobs:
                job_evac(job)
            ada(3)

            def max_unit(u):
                h, i = u // NT, u % NT
                if u == 0:
                    dve.wait_ge(alibi_ready, DH)
                dve.wait_ge(score_done, u + 1)
                W = (i + 1) * P
                if u >= 2:
                    dve.wait_ge(T_done, T_no[("unit", u - 2)] + 1)
                for m in range(2):
                    ins = v.tensor_tensor_reduce(out=prob[:, u % 2, m, 0:W], in0=banks[:, 2 + 2 * (u % 2) + m, 0:W],
                                                 in1=alibi[:, h, T - W:T], scale=1.0, scalar=-3e38,
                                                 op0=ALU.add, op1=ALU.max, accum_out=mx[:, u % 2, m:m + 1])
                link(ins)
                v.tensor_scalar(nmx[:, u % 2, :], mx[:, u % 2, :], -1.0, None, ALU.mult).then_inc(max_ready, 1)

            def combine_unit(u):
                i = u % NT
                W = (i + 1) * P
                dve.wait_ge(exp_ready, u + 1)
                link(v.reciprocal(rl[:, u % 2, :], lsum[:, u % 2, :]))
                link(v.tensor_scalar(rl[:, u % 2, 1:2], rl[:, u % 2, 1:2], neglam, None, ALU.mult))
                p0, p1 = prob[:, u % 2, 0, 0:W], prob[:, u % 2, 1, 0:W]
                link(v.tensor_scalar(p1, p1, rl[:, u % 2, 1:2], None, ALU.mult))
                v.scalar_tensor_tensor(out=p0, in0=p0, scalar=rl[:, u % 2, 0:1], in1=p1,
                                       op0=ALU.mult, op1=ALU.add).then_inc(prob_ready, 1)

            def out_sums(f):
                n = 4 if f < DH else 8
                if f < DH:
                    dve.wait_ge(pv_done, NT * (f + 1))
                else:
                    dve.wait_ge(spv_done, 2 * (f - DH) + 2)
                o = obuf[:, f % 2, :]
                v.tensor_copy(o, banks[:, 7, :]).then_inc(o_copied, 1)
                dve.wait_ge(o_copied, f + 1)
                if f >= 2:
                    dve.wait_ge(T_done, T_no[("fin", f - 2)] + 1)
                sq = obuf[:, 2 + f % 2, :]
                link(v.tensor_tensor(sq, o, o, ALU.mult))
                v.tensor_reduce(sso[:, f % 2, 0:n], sq.rearrange("p (g w) -> p g w", g=n), X,
                                ALU.add).then_inc(o_sums, 1)

            def out_scale(f):
                n = 4 if f < DH else 8
                dve.wait_ge(o_rstd, f + 1)
                w = 512 // n
                v.tensor_tensor(obuf[:, 2 + f % 2, :].rearrange("p (g w) -> p g w", g=n),
                                obuf[:, f % 2, :].rearrange("p (g w) -> p g w", g=n),
                                ro[:, f % 2, 0:n].unsqueeze(2).to_broadcast([P, n, w]), ALU.mult).then_inc(o_ready, 1)

            for s in range(DIFF_STEPS):
                if s >= 1:
                    for job in step_jobs.get(s - 1, ()):
                        job_evac(job)
                if 1 <= s <= 16:
                    combine_unit(s - 1)
                if s < 16:
                    max_unit(s)
                if s == 4:
                    ada(4)
                if s == 9:
                    ada(5)
                for f in range(DH):
                    if s == fin_step(f):
                        out_sums(f)
                    if s == fin_step(f) + 1:
                        out_scale(f)

            for s in range(STICK_STEPS):
                for f in range(DH):
                    if DIFF_STEPS + s == fin_step(f) + 1:
                        out_scale(f)
                if s < SH:
                    dve.wait_ge(ln_ready, s + 1)
                    v.scalar_tensor_tensor(out=soft[:, s % 2, :], in0=zps[s % 2][:, 0:ZCOLS], scalar=0.0,
                                           in1=soft[:, s % 2, :], op0=ALU.max, op1=ALU.add).then_inc(soft_raw, 1)
                for f in range(DH, 2 * DH):
                    if DIFF_STEPS + s == fin_step(f):
                        out_sums(f)
                        out_scale(f)

            def copy_x2T(t):
                dve.wait_ge(fT_done, t + 1)
                if t >= 2:
                    dve.wait_ge(logits_done, t - 1)
                v.tensor_copy(x2T[:, t % 2, :], banks[:, 6:8, :].rearrange("p b k -> p (b k)")).then_inc(x2T_ready, 1)

            for w in range(2 * NT):
                dve.wait_ge(y_done, w + 1)
                if w >= 2:
                    dve.wait_ge(x2_ready, w - 1)
                else:
                    dve.wait_ge(T_done, T_no[("fin", 7)] + 1)
                v.tensor_tensor(obuf[:, w % 2, :], banks[:, w % 5, :], gates[:, 0, (w % 2) * 512:(w % 2) * 512 + 512],
                                ALU.mult).then_inc(y_scaled, 1)
                if w >= 5 and w % 2 == 1:
                    copy_x2T((w - 5) // 2)
            for t in range(2, NT):
                copy_x2T(t)

            n32 = NT * 32
            lg = rt[:, 0:NT * NR].rearrange("p (t r) -> p t r", t=NT)
            o1 = NT * NR
            gsel = rt[:, o1:o1 + 16].rearrange("p (t g) -> p t g", t=NT)
            gkey = rt[:, o1 + 16:o1 + 32].rearrange("p (t g) -> p t g", t=NT)
            ge = exp_g.rearrange("p (t g) -> p t g", t=NT)
            prod = rt[:, o1 + 64:o1 + 64 + n32].rearrange("p (t g j) -> p t g j", t=NT, g=G)
            o2 = o1 + 64 + n32
            esel = rt[:, o2:o2 + 32].rearrange("p (t j) -> p t j", t=NT)
            key = rt[:, o2 + 32:o2 + 64].rearrange("p (t j) -> p t j", t=NT)
            oh = [rt[:, o2 + 64 + 32 * k:o2 + 96 + 32 * k].rearrange("p (t j) -> p t j", t=NT) for k in range(2)]
            o3 = o2 + 128
            sc = [rt[:, o3 + 4 * n:o3 + 4 * n + 4] for n in range(10)]
            gmax, kmax, gsum, ggate, m1, m2, den = sc[:7]
            dlt = exp_d
            o4 = o3 + 40
            rank = rt[:, o4:o4 + n32].rearrange("p (t e) -> p t e", t=NT)
            ov = rt[:, o4 + n32:o4 + 2 * n32].rearrange("p (t e) -> p t e", t=NT)
            sel = rt[:, o4 + 2 * n32:o4 + 3 * n32].rearrange("p (t e) -> p t e", t=NT)
            o5 = o4 + 3 * n32
            cnt, extra, incl, obase = (rt[:, o5 + 32 * n:o5 + 32 * n + 32] for n in range(4))
            posf = rt[:, o5 + 128:o5 + 136].rearrange("p (k t) -> p k t", k=2)
            assert o5 + 136 <= 1536 - 8

            def b3(ap, n):
                return ap.unsqueeze(2).to_broadcast([P, NT, n])

            def first_max(src, n, keybuf, onehot):
                link(v.tensor_reduce(kmax, src, X, ALU.max))
                link(v.tensor_tensor(keybuf, src, b3(kmax, n), ALU.is_equal))
                link(v.tensor_tensor(keybuf, keybuf, rev[:, 8 - n:8].unsqueeze(1).to_broadcast([P, NT, n]), ALU.mult))
                link(v.tensor_reduce(den, keybuf, X, ALU.max))
                link(v.tensor_tensor(onehot, keybuf, b3(den, n), ALU.is_equal))

            dve.wait_ge(memset_ready, 6)
            dve.wait_ge(logits_done, NT)
            link(v.tensor_copy(lg, banks[:, 5, 0:NT * NR].rearrange("p (t r) -> p t r", t=NT)))
            first_max(lg[:, :, 0:G], G, gkey, gsel)
            v.tensor_tensor(ge, lg[:, :, 0:G], b3(kmax, G), ALU.subtract).then_inc(g_exp_in, 1)
            link(v.tensor_tensor(prod, lg[:, :, G:NR].rearrange("p t (g j) -> p t g j", g=G),
                                 gsel.unsqueeze(3).to_broadcast([P, NT, G, EG]), ALU.mult))
            link(v.tensor_reduce(esel, prod.rearrange("p t g j -> p t j g"), X, ALU.add))
            first_max(esel, EG, key, oh[0])
            link(v.tensor_copy(m1, kmax))
            link(v.scalar_tensor_tensor(out=esel, in0=oh[0], scalar=-1e30, in1=esel, op0=ALU.mult, op1=ALU.add))
            first_max(esel, EG, key, oh[1])
            v.tensor_tensor(dlt, kmax, m1, ALU.subtract).then_inc(d_in, 1)
            for k in range(2):
                for t in range(NT):
                    link(v.tensor_tensor(masks[:, k, t, :].rearrange("p (g j) -> p g j", g=G),
                                         gsel[:, t, :].unsqueeze(2).to_broadcast([P, G, EG]),
                                         oh[k][:, t, :].unsqueeze(1).to_broadcast([P, G, EG]), ALU.mult))
            v.tensor_tensor(masks[:, 2, :, :], masks[:, 0, :, :], masks[:, 1, :, :], ALU.add).then_inc(masks_ready, 1)
            dve.wait_ge(rank_done, 1)
            link(v.tensor_copy(rank, banks[:, 0, 0:n32].rearrange("p (t e) -> p t e", t=NT)))
            link(v.tensor_scalar(ints[:, 0:32], banks[:, 0, n32:n32 + 32], float(C - 1), None, ALU.add))
            link(v.tensor_scalar(ints[:, 0:32], ints[:, 0:32], C.bit_length() - 1, None, ALU.arith_shift_right))
            link(v.tensor_copy(cnt, ints[:, 0:32]))
            link(v.tensor_scalar(extra, cnt, -1.0, 0.0, ALU.add, ALU.max))
            link(v.tensor_tensor_scan(incl, extra, zero32, 0.0, ALU.add, ALU.add))
            link(v.tensor_tensor(obase, incl, extra, ALU.subtract))
            link(v.tensor_scalar(obase, obase, float(E - 1), float(C), ALU.add, ALU.mult))
            link(v.tensor_tensor(obase, obase, e64, ALU.subtract))
            link(v.tensor_scalar(ov, rank, float(C), None, ALU.is_ge))
            link(v.tensor_tensor(ov, ov, obase.unsqueeze(1).to_broadcast([P, NT, E]), ALU.mult))
            link(v.tensor_tensor(rank, rank, e64.unsqueeze(1).to_broadcast([P, NT, E]), ALU.add))
            link(v.tensor_tensor(rank, rank, ov, ALU.add))
            for k in range(2):
                link(v.tensor_tensor(sel, rank, masks[:, k, :, :], ALU.mult))
                link(v.tensor_reduce(posf[:, k, :], sel, X, ALU.add))
            v.tensor_copy(ints[:, 80:88].rearrange("p (k t) -> p k t", k=2), posf).then_inc(pos_ready, 1)
            over = rt[0:1, 0:(MAXOV + 1) * E].rearrange("p (b e) -> p b e", b=MAXOV + 1)
            nover = sel[0:1, 0, 0:MAXOV + 1]
            link(v.tensor_tensor(over, incl[0:1, :].unsqueeze(1).to_broadcast([1, MAXOV + 1, E]),
                                 b_iota[0:1, :].unsqueeze(2).to_broadcast([1, MAXOV + 1, E]), ALU.is_le))
            link(v.tensor_reduce(nover, over, X, ALU.add))
            link(v.tensor_copy(plan[0:1, 0:MAXOV + 1], nover))
            v.tensor_copy(plan[0:1, MAXOV + 1:MAXOV + 2], incl[0:1, 31:32]).then_inc(plan_ready, 1)
            dve.wait_ge(g_exp, 1)
            link(v.tensor_reduce(gsum, ge, X, ALU.add))
            link(v.reciprocal(ggate, gsum))
            dve.wait_ge(d_exp, 1)
            link(v.tensor_scalar(den, dlt, 1.0, None, ALU.add))
            link(v.reciprocal(den, den))
            link(v.tensor_tensor(wpair[:, 0, :], den, ggate, ALU.mult))
            link(v.tensor_tensor(wpair[:, 1, :], wpair[:, 0, :], dlt, ALU.mult))

            def modulate(n, r):
                dve.wait_ge(eT_done, n)
                dst = heT[:, r, :].rearrange("p (k t) -> p k t", k=KD)
                src = banks[:, 0:2, :].rearrange("p b (k t) -> p (b k) t", t=P)
                v.tensor_tensor(dst, src, mod[:, 3, :].unsqueeze(2).to_broadcast([P, KD, P]), ALU.mult).then_inc(he_mul, 1)
                dve.wait_ge(he_mul, n)
                v.tensor_tensor(dst, dst, mod[:, 2, :].unsqueeze(2).to_broadcast([P, KD, P]), ALU.add).then_inc(heT_ready, 1)

            def gated(n, r):
                dve.wait_ge(silu_ready, n)
                v.tensor_tensor(geT[:, r, :], gact[:, r, :], banks[:, 2 + r, P:2 * P], ALU.mult).then_inc(ge_ready, 1)

            def y_evac(n_experts, r, w):
                dve.wait_ge(ye_done, n_experts)
                v.tensor_tensor(ysb[0:w, r, :], banks[0:w, 4 + 2 * r:6 + 2 * r, :].rearrange("p b k -> p (b k)"),
                                gates[0:w, 1, :], ALU.mult).then_inc(ysb_ready, 1)

            dve.wait_ge(fT_done, NT)
            dve.wait_ge(xn_stored, 16 * NT)
            modulate(1, 0)

            def two_pairs(it, first, last):
                for a in range(2):
                    gated(it * 4 + (2 * a + 1), 0)
                    if not (last and a == 1):
                        modulate(it * 2 + (a + 2), 1 - a)
                    gated(it * 4 + (2 * a + 2), 1)
                    if not first:
                        dve.wait_ge(y_stored[a], it * 16)
                    y_evac(it * 4 + (2 * a + 2), a, P)

            two_pairs(0, True, False)
            with dve.Fori(1, E // 4 - 1) as it:
                two_pairs(it, False, False)
            two_pairs(E // 4 - 1, False, True)
            dve.wait_ge(plan_ready, 1)
            nb = dve.value_load(plan[0:1, MAXOV + 1:MAXOV + 2], min_val=0, max_val=MAXOV)
            with dve.If(nb > 0):
                dve.wait_ge(y_stored[0], 16 * (E // 4))
                with dve.Fori(0, nb) as b:
                    modulate(b + (E // 2 + 1), 0)
                    gated(b + (E + 1), 0)
                    y_evac(b + (E + 1), 0, C)
            for t in range(NT):
                dve.wait_ge(pairs_in[t], 16)
                v.scalar_tensor_tensor(out=xr[:, t, :], in0=fin_pair(t)[:, 0, :], scalar=wpair[:, 0, t:t + 1],
                                       in1=xr[:, t, :], op0=ALU.mult, op1=ALU.add).then_inc(fin_b, 1)
                dve.wait_ge(fin_b, t + 1)
                dve.wait_ge(fin_a, t + 1)
                v.tensor_tensor(xr[:, t, :], xr[:, t, :], fin_pair(t)[:, 1, :], ALU.add).then_inc(fin_c, 1)

        @block.tensor
        def _(pe):
            mm = nc.tensor.matmul
            pe.wait_ge(consts_ready, 4)
            pe.wait_ge(consts_dve, 5)

            for n in range(2):
                pe.wait_ge(ada_used, 2 * n + 2)
                for k in range(KD):
                    ins = mm(banks[:, 0, 8 * n + k:8 * n + k + 1],
                             acc[:, n, :].rearrange("p (j k) -> p k j", k=KD)[:, k, :], ones[:, 0:1],
                             start=(n == 0 and k == 0), stop=True, skip_group_check=True)
            ins.then_inc(col_a, 1)
            pe.wait_ge(xn_ready, NT)
            for k in range(KD):
                if k >= 4:
                    if k % 2:
                        pe.wait_ge(hT_act, (k - 4) // 2 + 1)
                    else:
                        pe.wait_ge(hT_dve, (k - 4) // 2 + 1)
                for t in range(NT):
                    ins = nc.tensor.transpose(banks[:, 2 + k % 4, t * P:(t + 1) * P], xn[:, t, k * P:(k + 1) * P], ident)
                ins.then_inc(xT_done, 1)
            pe.wait_ge(hT_act, KD // 2)
            pe.wait_ge(hT_dve, KD // 2)

            def wait_freed(job):
                which, value = freed[job]
                pe.wait_ge(qk_dve if which == "qk" else bank_free[which], value)

            def run(job):
                n = job_no[job]
                bank = banks[:, n % 2, :]
                if n >= 2:
                    wait_freed(job_at[n - 2])
                kind = job[0]
                if kind in ("qk", "sq", "sk"):
                    piece, ch = {"qk": (job[1] // 4, job[1] % 4), "sq": (3, job[1]), "sk": (4, job[1])}[kind]
                    w, arrived, value = piece_at(("in", piece))
                    w = w.rearrange("p (k n) -> p k n", k=KD)
                    pe.wait_ge(arrived, value)
                    for k in range(KD):
                        ins = mm(bank, w[:, k, ch * P:(ch + 1) * P], hT[:, k, :], start=(k == 0), stop=(k == KD - 1))
                elif kind == "v":
                    w, arrived, value = piece_at(("in", 2 if job[2] == 0 else 5))
                    w = w.rearrange("p (k n) -> p k n", k=KD)
                    pe.wait_ge(arrived, value)
                    for k in range(KD):
                        ins = mm(bank, hT[:, k, job[1] * P:(job[1] + 1) * P], w[:, k, :], start=(k == 0), stop=(k == KD - 1))
                elif kind == "gate":
                    v = 2 if job[1] == 0 else 5
                    pe.wait_ge(ada_used, 2 * v + 2)
                    ins = mm(bank, ones, acc[:, v % 2, job[2] * 512:job[2] * 512 + 512], start=True, stop=True)
                elif kind == "col":
                    v = job[1] + 1
                    pe.wait_ge(ada_used, 2 * v + 2)
                    for k in range(KD):
                        ins = mm(bank[:, k:k + 1], acc[:, v % 2, :].rearrange("p (j k) -> p k j", k=KD)[:, k, :],
                                 ones[:, 0:1], start=(k == 0), stop=True, skip_group_check=True)
                elif kind == "shift_router":
                    wait_freed(("col", 2))
                    for k in range(KD):
                        ins = mm(bank[0:1, 0:NR], mod[:, 2, k:k + 1], wr[:, k, :], start=(k == 0), stop=(k == KD - 1))
                ins.then_inc(job_done, 1)

            def qk_norm(n):
                pe.wait_ge(sq_ready, n + 1)
                if n >= 2:
                    pe.wait_ge(rqk_ready, n - 1)
                mm(banks[:, 2 + n % 2, :], halves, sqb[:, n % 2, :], start=True, stop=True).then_inc(norm_done, 1)

            for i, job in enumerate(head_jobs):
                run(job)
                if 1 <= i <= 8:
                    qk_norm(i - 1)

            def scores(u):
                h, i = u // NT, u % NT
                W = (i + 1) * P
                if u == 0:
                    pe.wait_ge(qk_dve, 8)
                    pe.wait_ge(rqk_ready, 8)
                if u >= 2:
                    pe.wait_ge(max_ready, u - 1)
                for m in range(2):
                    q = qkT[m * HD:(m + 1) * HD, h, i * P:(i + 1) * P]
                    k = qkT[m * HD:(m + 1) * HD, 4 + h, 0:W]
                    ins = mm(banks[:, 2 + 2 * (u % 2) + m, 0:W], q, k, start=True, stop=True)
                ins.then_inc(score_done, 1)

            def T_free(n):
                if n >= 1:
                    kind, w = T_order[n - 1]
                    pe.wait_ge(probT_ready if kind == "unit" else mix_ready, w + 1)

            def probT_make(u):
                i = u % NT
                pe.wait_ge(prob_ready, u + 1)
                T_free(T_no[("unit", u)])
                for kb in range(i + 1):
                    ins = nc.tensor.transpose(banks[:, 6, kb * P:(kb + 1) * P], prob[:, u % 2, 0, kb * P:(kb + 1) * P], ident)
                ins.then_inc(T_done, 1)

            def pv(u):
                h, i = u // NT, u % NT
                pe.wait_ge(probT_ready, u + 1)
                if i == 0 and h == 0:
                    wait_freed(("v", NT - 2, 0))
                    wait_freed(("v", NT - 1, 0))
                if i == 0 and h >= 1:
                    pe.wait_ge(o_copied, h)
                for kb in range(i + 1):
                    ins = mm(banks[:, 7, i * P:(i + 1) * P], probT[:, u % 2, kb * P:(kb + 1) * P],
                             val[:, kb, h * P:(h + 1) * P], start=(i == 0 and kb == 0), stop=(kb == i),
                             skip_group_check=True)
                ins.then_inc(pv_done, 1)

            def fin_T(f):
                pe.wait_ge(o_ready, f + 1)
                T_free(T_no[("fin", f)])
                o = obuf[:, 2 + f % 2, :]
                for i in range(NT):
                    ins = nc.tensor.transpose(banks[:, 6, i * P:(i + 1) * P], o[:, i * P:(i + 1) * P], ident)
                ins.then_inc(T_done, 1)

            for s in range(DIFF_STEPS):
                if s < 16:
                    scores(s)
                if 1 <= s <= 16:
                    probT_make(s - 1)
                if 2 <= s <= 17:
                    pv(s - 2)
                for f in range(DH):
                    if s == fin_step(f) + 2:
                        fin_T(f)
                for job in step_jobs.get(s, ()):
                    run(job)

            def stick_scores(n):
                pair, s = n // 2, n % 2
                if n == 0:
                    wait_freed(job_at[len(job_no) - 2])
                    wait_freed(job_at[len(job_no) - 1])
                    pe.wait_ge(max_ready, 16)
                if n >= 2:
                    pe.wait_ge(stick_raw, n - 1)
                for kb in (0, 1, 3, 2):
                    W = T - kb * P
                    k = qkT[s * HD:(s + 1) * HD, 12 + pair, kb * P:(kb + 1) * P]
                    q = qkT[s * HD:(s + 1) * HD, 8 + pair, kb * P:T]
                    ins = mm(zps[n % 2][:, ZOFF[kb]:ZOFF[kb] + W], k, q, start=(kb != 3), stop=True,
                             skip_group_check=True)
                ins.then_inc(z_done, 1)

            def stick_sums(n):
                pe.wait_ge(soft_ready, n + 1)
                for kb in range(NT):
                    for j in range(kb, NT):
                        W = T - j * P
                        o = ZOFF[kb] + (j - kb) * P
                        ins = mm(zps[n % 2][:, o:o + W], negtri if j == kb else negones,
                                 soft[:, n % 2, ZOFF[j]:ZOFF[j] + W], start=False, stop=True, skip_group_check=True)
                ins.then_inc(tri_done, 1)

            def stick_pv(n):
                pair, s = n // 2, n % 2
                pe.wait_ge(stick_ready, n + 1)
                if s == 0:
                    pe.wait_ge(o_copied, DH + pair)
                for i in range(NT):
                    for kb in range(i + 1):
                        o = ZOFF[kb] + (i - kb) * P
                        ins = mm(banks[:, 7, i * P + s * HD:i * P + (s + 1) * HD], stick[:, n % 2, o:o + P],
                                 val[:, kb, 512 + n * HD:512 + (n + 1) * HD],
                                 start=(s == 0 and i == 0 and kb == 0), stop=(kb == i), skip_group_check=True)
                ins.then_inc(spv_done, 1)

            for s in range(STICK_STEPS):
                for f in range(DH):
                    if DIFF_STEPS + s == fin_step(f) + 2:
                        fin_T(f)
                if s < SH:
                    stick_scores(s)
                if 1 <= s <= SH:
                    stick_sums(s - 1)
                if 2 <= s <= SH + 1:
                    stick_pv(s - 2)
                for f in range(DH, 2 * DH):
                    if DIFF_STEPS + s == fin_step(f) + 2:
                        fin_T(f)

            def out_proj(w):
                t, half = w // 2, w % 2
                if w == 0:
                    for p in range(2):
                        _, arrived, value = piece_at(("out", p))
                        pe.wait_ge(arrived, value)
                    pe.wait_ge(mix_ready, 8)
                    pe.wait_ge(stick_raw, SH)
                if w >= 5:
                    pe.wait_ge(y_scaled, w - 4)
                for k in range(KD):
                    wv = piece_at(("out", k // 4))[0].rearrange("p (k n) -> p k n", k=4)
                    ins = mm(banks[:, w % 5, :], mixT[:, k, t * P:(t + 1) * P],
                             wv[:, k % 4, half * 512:(half + 1) * 512], start=(k == 0), stop=(k == KD - 1))
                ins.then_inc(y_done, 1)

            def rows_T(t):
                pe.wait_ge(xnb_ready, t + 1)
                if t >= 1:
                    pe.wait_ge(x2T_ready, t)
                for k in range(KD):
                    ins = nc.tensor.transpose(banks[:, 6 + k // 4, (k % 4) * P:(k % 4 + 1) * P],
                                              xnb[:, t % 2, k * P:(k + 1) * P], ident)
                ins.then_inc(fT_done, 1)

            def logits(t):
                pe.wait_ge(x2T_ready, t + 1)
                for k in range(KD):
                    mm(banks[:, 5, t * NR:(t + 1) * NR], x2T[:, t % 2, k * P:(k + 1) * P], wrA[:, k, :],
                       start=(t == 0 and k == 0), stop=False, skip_group_check=True)
                mm(banks[:, 5, t * NR:(t + 1) * NR], ones[0:1, :], router_row[0:1, 1, :], start=False, stop=True,
                   skip_group_check=True).then_inc(logits_done, 1)

            pe.wait_ge(wrA_ready, 1)
            for w in range(4):
                out_proj(w)
            rows_T(0)
            out_proj(4)
            out_proj(5)
            rows_T(1)
            logits(0)
            out_proj(6)
            out_proj(7)
            rows_T(2)
            logits(1)
            rows_T(3)
            logits(2)
            logits(3)

            pe.wait_ge(masks_ready, 1)
            for t in range(NT):
                for j in range(t + 1):
                    mm(banks[:, 0, t * E:(t + 1) * E], tri_bf[:] if j == t else ones_bf[:], masks[:, 2, j, :],
                       start=(t == 0), stop=(j == t), skip_group_check=True)
            for j in range(NT):
                ins = mm(banks[:, 0, NT * E:NT * E + E], ones_bf[:], masks[:, 2, j, :], start=False, stop=(j == NT - 1),
                         skip_group_check=True)
            ins.then_inc(rank_done, 1)

            def expert_T(first_wait, arrived, r):
                pe.wait_ge(arrived[0], arrived[1])
                if first_wait is not None:
                    pe.wait_ge(he_mul, first_wait)
                for k in range(KD):
                    ins = nc.tensor.transpose(banks[:, k // 4, (k % 4) * P:(k % 4 + 1) * P],
                                              rows[:, r, k * P:(k + 1) * P], ident)
                ins.then_inc(eT_done, 1)

            def expert_h(n_h, n_pairs, s, r, half):
                pe.wait_ge(heT_ready, n_pairs)
                if n_h is not None:
                    pe.wait_ge(ge_ready, n_h)
                first = True
                for which, ws in enumerate((w1s[s], w3s[s])):
                    for fc in range(FC):
                        o = which * P + fc * C
                        for k in range(KD):
                            ins = mm(banks[:, 2 + half, o:o + C], ws[:, k, fc * P:(fc + 1) * P],
                                     heT[:, r, k * P + half * C:k * P + (half + 1) * C],
                                     start=first, stop=(k == KD - 1), skip_group_check=True)
                            first = False
                ins.then_inc(h_done, 1)

            def expert_y(n_e, n_free, s, r, half):
                pe.wait_ge(ge_ready, n_e)
                if n_free is not None:
                    pe.wait_ge(ysb_ready, n_free)
                for col in range(2):
                    for fc in range(FC):
                        ins = mm(banks[half * C:(half + 1) * C, 4 + 2 * r + col, :], geT[:, half, fc * C:(fc + 1) * C],
                                 w2s[s][:, fc, col * 512:(col + 1) * 512], start=(fc == 0), stop=(fc == FC - 1))
                ins.then_inc(ye_done, 1)

            def two_pairs(it, first, last):
                for a in range(2):
                    for half in range(2):
                        s = 2 * a + half
                        pe.wait_ge(w_in_slot[s], it * 48 + 48)
                        free = None if (first and s < 2) else it * 4 + (s - 1)
                        expert_h(free, it * 2 + (a + 1), s, a, half)
                        if half == 0 and not (last and a == 1):
                            expert_T(it * 2 + (a + 1), (rows_in[1 - a], it * 16 + 16 * (a + 1)), 1 - a)
                    for half in range(2):
                        s = 2 * a + half
                        free = None if first or half else it * 2 + (a - 1)
                        expert_y(it * 4 + (s + 1), free, s, a, half)

            expert_T(None, (rows_in[0], 16), 0)
            two_pairs(0, True, False)
            with pe.Fori(1, E // 4 - 1) as it:
                two_pairs(it, False, False)
            two_pairs(E // 4 - 1, False, True)
            pe.wait_ge(plan_ready, 1)
            nb = pe.value_load(plan[0:1, MAXOV + 1:MAXOV + 2], min_val=0, max_val=MAXOV)
            with pe.If(nb > 0):
                with pe.Fori(0, nb) as b:
                    expert_T(b + E // 2, (rows_in[0], b * 16 + 16 * (E // 4 + 1)), 0)
                    pe.wait_ge(w_in_slot[0], b * 48 + 48 * (E // 4 + 1))
                    expert_h(b + E, b + (E // 2 + 1), 0, 0, 0)
                    expert_y(b + (E + 1), b + E // 2, 0, 0, 0)


_INS = ["x", "c", "w_ada", "b_ada", "g_attn", "w_in", "q_norm_g", "k_norm_g", "lambda_q1", "lambda_k1",
        "lambda_q2", "lambda_k2", "diff_out_g", "sb_out_g", "w_out", "g_ffn", "w_group", "b_group",
        "w_erouter", "b_expert", "w1", "w3", "w2"]


def kernel(**inputs):
    import numpy as _np
    import concourse.bacc as _bacc
    from concourse import mybir as _mybir
    from concourse.bass_utils import run_bass_kernel_spmd as _run

    nc = _bacc.Bacc("TRN2", target_bir_lowering=False, num_devices=1)
    arrays, args = {}, []
    for name in _INS:
        a = _np.ascontiguousarray(inputs[name])
        arrays[f"in_{name}_dram"] = a
        args.append(nc.dram_tensor(f"in_{name}_dram", a.shape, _mybir.dt.from_np(a.dtype), kind="ExternalInput").ap())
    args.append(nc.dram_tensor("out_0_dram", (1, T, D), _mybir.dt.float32, kind="ExternalOutput").ap())
    hymba_block(nc, *args)
    r = _run(nc, [arrays], core_ids=[0])
    return r.results[0]["out_0_dram"]
```

```python
from contextlib import ExitStack

import concourse.bass as bass
from concourse import mybir

F32 = mybir.dt.float32
BF16 = mybir.dt.bfloat16
I32 = mybir.dt.int32
ALU = mybir.AluOpType
ACT = mybir.ActivationFunctionType
X = mybir.AxisListType.X

P = 128
T = 512
D = 1024
NT = T // P
KD = D // P
HD = 64
DH = 4
SH = 8
G = 4
EG = 8
E = G * EG
F = 256
FC = F // P
NR = G + G * EG
C = 64
MAXOV = 2 * T // (C + 1)
NQ = E // 2
NQOV = (MAXOV + 1) // 2
NCOL = NQ + NQOV
SKIP = 60000
EPS = 1e-6
LAMBDA_INIT = 0.2

ZOFF = {0: 0, 1: 512, 3: 896, 2: 1024}
ZCOLS = 1280


def plan_jobs():
    head = [("qk", n) for n in range(8)] + [("v", t, 0) for t in range(NT)] + [("gate", 0, 0), ("gate", 0, 1)]
    steps = {s: [] for s in range(20)}
    for n in range(4):
        steps[n].append(("sq", n))
        steps[4 + n].append(("sk", n))
        steps[8 + n].append(("v", n, 1))
    steps[2].insert(0, ("col", 2))
    steps[7].insert(0, ("col", 3))
    steps[8].insert(0, ("shift_router",))
    steps[12].append(("gate", 1, 0))
    steps[13].append(("gate", 1, 1))
    order = head + [j for s in range(20) for j in steps[s]]
    return head, steps, {j: n for n, j in enumerate(order)}


SHIFT_A, SCALE_A, GATE_A, SHIFT_F, SCALE_F, GATE_F = range(6)


DIFF_STEPS, STICK_STEPS = NT * DH + 2, SH + 4


def fin_step(f):
    return 4 * f + 5 if f < DH else DIFF_STEPS + 2 * (f - DH) + 3


def plan_transposes():
    order = []
    for s in range(DIFF_STEPS + STICK_STEPS):
        if s >= DIFF_STEPS:
            order += [("fin", f) for f in range(DH) if s == fin_step(f) + 2]
        if 1 <= s <= NT * DH:
            order.append(("unit", s - 1))
        if s < DIFF_STEPS:
            order += [("fin", f) for f in range(DH) if s == fin_step(f) + 2]
        order += [("fin", f) for f in range(DH, 2 * DH) if s == fin_step(f) + 2]
    return order, {w: n for n, w in enumerate(order)}


def plan_releases(job_no):
    freed, count = {}, [0, 0]
    for job, n in sorted(job_no.items(), key=lambda kv: kv[1]):
        if job[0] == "qk":
            freed[job] = ("qk", job[1] + 1)
            continue
        count[n % 2] += 1
        freed[job] = (n % 2, count[n % 2])
    return freed


def hymba_block(nc, x, c, w_ada, b_ada, g_attn, w_in, q_norm_g, k_norm_g, lambda_q1, lambda_k1,
                lambda_q2, lambda_k2, diff_out_g, sb_out_g, w_out, g_ffn, w_group, b_group,
                w_erouter, b_expert, w1, w3, w2, out):
    head_jobs, step_jobs, job_no = plan_jobs()
    job_at = {n: job for job, n in job_no.items()}
    T_order, T_no = plan_transposes()
    freed = plan_releases(job_no)

    xn_dram = nc.dram_tensor("xn_rows", (T, D), F32, kind="Internal").ap()
    y_dram = nc.dram_tensor("pair_rows", (2 * T, D), F32, kind="Internal").ap()

    with ExitStack() as ctx:
        def sb(name, shape, dt=F32):
            return ctx.enter_context(nc.sbuf_tensor(name, shape, dt))

        def sem(name):
            return ctx.enter_context(nc.semaphore(name))

        xr = sb("xr", [P, NT, D])
        stage = sb("stage", [P, 3, 4096])
        hT = sb("hT", [P, KD, T])
        qkT = sb("qkT", [P, 16, T])
        val = sb("val", [P, NT, 1024])
        mixT = sb("mixT", [P, KD, T])
        gates = sb("gates", [P, 2, D])
        alibi = sb("alibi", [P, DH, T])
        work = sb("work", [P, 8192])
        obuf = sb("obuf", [P, 4, T])
        consts = sb("consts", [P, 6, P])
        wr = sb("wr", [P, KD, NR])
        wrA = sb("wrA", [P, KD, NR])
        small = sb("small", [P, 296])
        router_row = sb("router_row", [1, 2, NR])
        tri_bf = sb("tri_bf", [P, P], BF16)
        ones_bf = sb("ones_bf", [P, P], BF16)
        tables = sb("tables", [P, 2, NCOL], I32)
        ints = sb("ints", [P, 96], I32)
        plan = sb("plan", [1, 2 * NQOV + 2], I32)

        ident, negtri, negones, ones, halves, slot_iota = (consts[:, n, :] for n in range(6))
        acc = mixT[:, 4:8, :].rearrange("p (v a) t -> p v (a t)", v=2)
        xn = qkT[:, 0:8, :].rearrange("p (t a) c -> p t (a c)", t=NT)
        prob = work[:, 0:2048].rearrange("p (r m k) -> p r m k", r=2, m=2)
        probT = work[:, 2048:3072].rearrange("p (r k) -> p r k", r=2)
        sqb = work[:, 3072:4096].rearrange("p (r k) -> p r k", r=2)
        rqk = work[:, 4096:5120].rearrange("p (r k) -> p r k", r=2)
        soft = work[:, 3072:3072 + 2 * ZCOLS].rearrange("p (r k) -> p r k", r=2)
        stick = work[:, 5632:5632 + 2 * ZCOLS].rearrange("p (r k) -> p r k", r=2)
        xnb = work[:, 0:2048].rearrange("p (r k) -> p r k", r=2)
        x2T = work[:, 2048:4096].rearrange("p (r k) -> p r k", r=2)
        onehot = work[:, 2048:3072].rearrange("p (c s) -> p c s", c=2 * NT)
        rows = work[:, 4096:6144].rearrange("p (r k) -> p r k", r=2)
        heT = work[:, 0:2048].rearrange("p (r k) -> p r k", r=2)
        ysb = work[:, 2048:4096].rearrange("p (r k) -> p r k", r=2)
        gact = work[:, 6144:6400].rearrange("p (r k) -> p r k", r=2)
        geT = work[:, 6400:6656].rearrange("p (r k) -> p r k", r=2)
        rt = work[:, 6656:8192]
        hT_f = hT[:].rearrange("p a b -> p (a b)")
        qk_f = qkT[:].rearrange("p a b -> p (a b)")
        val_f = val[:].rearrange("p a b -> p (a b)")
        mix_f = mixT[:].rearrange("p a b -> p (a b)")
        slots = [
            (hT_f[:, 0:2048], hT_f[:, 2048:4096], stage[:, 2, 0:2048]),
            (qk_f[:, 0:2048], qk_f[:, 2048:4096], qk_f[:, 4096:6144]),
            (qk_f[:, 6144:8192], val_f[:, 0:2048], val_f[:, 2048:4096]),
            (stage[:, 0, 0:2048], stage[:, 0, 2048:4096], stage[:, 1, 0:2048]),
            (mix_f[:, 0:2048], mix_f[:, 2048:4096], stage[:, 1, 2048:4096]),
            (alibi[:].rearrange("p a b -> p (a b)"), obuf[:].rearrange("p a b -> p (a b)"), stage[:, 2, 2048:4096]),
        ]
        w1s = [s[0].rearrange("p (k f) -> p k f", k=KD) for s in slots]
        w3s = [s[1].rearrange("p (k f) -> p k f", k=KD) for s in slots]
        w2s = [s[2].rearrange("p (f n) -> p f n", f=FC) for s in slots]

        ramp = work[:, 7168:7680].bitcast(I32)
        lam_in = work[:, 7936:8192].rearrange("p (v d) -> p v d", v=4)
        masks = rt[:, 1200:1392].bitcast(BF16).rearrange("p (k t e) -> p k t e", k=3, t=NT)
        exp_g = rt[:, 1400:1416]
        exp_d = rt[:, 1416:1420]

        def fin_pair(t):
            n = t * 2048
            return stage[:].rearrange("p a b -> p (a b)")[:, n:n + 2048].rearrange("p (k n) -> p k n", k=2)

        at = [0]

        def cols(n):
            at[0] += n
            return small[:, at[0] - n:at[0]]

        c_col, cs = cols(8), cols(8)
        b_col = cols(32).rearrange("p (v k) -> p v k", v=4)
        g_col = cols(16).rearrange("p (v k) -> p v k", v=2)
        mod = cols(32).rearrange("p (v k) -> p v k", v=4)
        gqk, out_g = cols(2), cols(2)
        eps = cols(1)
        ssx, rx, ss2, r2 = cols(4), cols(4), cols(4), cols(4)
        lam, neglam = cols(4), cols(1)
        mx, nmx, lsum, rl = (cols(4).rearrange("p (r m) -> p r m", r=2) for _ in range(4))
        sso, ro = cols(16).rearrange("p (r k) -> p r k", r=2), cols(16).rearrange("p (r k) -> p r k", r=2)
        wpair = cols(8).rearrange("p (k t) -> p k t", k=2)
        rev = cols(8)
        e64 = cols(32)
        zero32 = cols(32)
        pair_id = cols(8)
        b_iota = cols(2 * NQOV)
        assert at[0] <= 296

        banks = ctx.enter_context(nc.psum_tensor("banks", [P, 8, 512], F32))
        zps = [banks[:, 3 * r:3 * r + 3, :].rearrange("p b k -> p (b k)") for r in range(2)]

        x_in, c_in, params_in, gate_bias_in = sem("x_in"), sem("c_in"), sem("params_in"), sem("gate_bias_in")
        first_in = [sem(f"first_in{n}") for n in range(4)]
        piece_in = [sem("piece_in0"), sem("piece_in1")]
        quarter_in = [sem("quarter_in0"), sem("quarter_in1")]
        scale_used = sem("scale_used")
        consts_ready, memset_ready = sem("consts_ready"), sem("memset_ready")
        silu_c, shift_used, ada_used = sem("silu_c"), sem("shift_used"), sem("ada_used")
        col_a, mod_a = sem("col_a"), sem("mod_a")
        xn_ready, xT_done = sem("xn_ready"), sem("xT_done")
        hT_act, hT_dve = sem("hT_act"), sem("hT_dve")
        job_done = sem("job_done")
        bank_free = [sem("bank_free0"), sem("bank_free1")]
        qk_raw, sq_ready, norm_done, rqk_ready = sem("qk_raw"), sem("sq_ready"), sem("norm_done"), sem("rqk_ready")
        qk_act, qk_dve, v_ready = sem("qk_act"), sem("qk_dve"), sem("v_ready")
        alibi_ready, lam_ready = sem("alibi_ready"), sem("lam_ready")
        score_done, max_ready, exp_ready, prob_ready = (sem(n) for n in (
            "score_done", "max_ready", "exp_ready", "prob_ready"))
        T_done, probT_ready, pv_done = sem("T_done"), sem("probT_ready"), sem("pv_done")
        o_copied, o_sums, o_rstd, o_ready, oT_done, mix_ready = (sem(n) for n in (
            "o_copied", "o_sums", "o_rstd", "o_ready", "oT_done", "mix_ready"))
        z_done, ln_ready, soft_raw, soft_ready, tri_done, stick_raw, stick_ready, spv_done = (sem(n) for n in (
            "z_done", "ln_ready", "soft_raw", "soft_ready", "tri_done", "stick_raw", "stick_ready", "spv_done"))
        y_done, y_scaled, x2_ready = sem("y_done"), sem("y_scaled"), sem("x2_ready")
        xnb_ready, xn_stored, fT_done, x2T_ready, logits_done = (sem(n) for n in (
            "xnb_ready", "xn_stored", "fT_done", "x2T_ready", "logits_done"))
        wrA_ready, row_ready, gate_ready = sem("wrA_ready"), sem("row_ready"), sem("gate_ready")
        g_exp_in, g_exp, d_in, d_exp = sem("g_exp_in"), sem("g_exp"), sem("d_in"), sem("d_exp")
        masks_ready, rank_done, onehot_ready, table_done, table_ready = (sem(n) for n in (
            "masks_ready", "rank_done", "onehot_ready", "table_done", "table_ready"))
        plan_ready = sem("plan_ready")
        w_in_slot = [sem(f"w_slot{n}") for n in range(6)]
        rows_in = [sem("rows_in0"), sem("rows_in1")]
        rows_zero = sem("rows_zero")
        eT_done, he_mul, heT_ready, h_done, silu_ready, ge_ready, ye_done, ysb_ready = (sem(n) for n in (
            "eT_done", "he_mul", "heT_ready", "h_done", "silu_ready", "ge_ready", "ye_done", "ysb_ready"))
        y_stored = [sem("y_stored0"), sem("y_stored1")]
        pairs_in = [sem(f"pairs_in{n}") for n in range(NT)]
        fin_a, fin_b, fin_c, out_stored = sem("fin_a"), sem("fin_b"), sem("fin_c"), sem("out_stored")
        eps_ready, consts_dve, lam_exp = sem("eps_ready"), sem("consts_dve"), sem("lam_exp")
        act_chain, dve_chain, pool_chain = sem("act_chain"), sem("dve_chain"), sem("pool_chain")

        x_rows = x.rearrange("b (t p) d -> (b p) t d", p=P)
        out_rows = out.rearrange("b (t p) d -> (b p) t d", p=P)
        ada_v = w_ada.rearrange("l (p k) n -> (l p) k n", k=KD)
        in_v = w_in.rearrange("l (p k) n -> (l p) k n", k=KD)
        out_v = w_out.rearrange("l (k p) n -> (l p) k n", p=P)
        w1_v = w1.rearrange("l g e (p k) f -> (l g e) p (k f)", k=KD)
        w3_v = w3.rearrange("l g e (p k) f -> (l g e) p (k f)", k=KD)
        w2_v = w2.rearrange("l g e (f p) n -> (l g e) p f n", p=P)
        b_cols_v = b_ada.rearrange("l (v p k) -> (l p) v k", v=6, k=KD)
        w2_dst = [s[2].rearrange("p (f n) -> p f n", f=FC) for s in slots]

        def piece(n):
            w = stage[:, n % 2, :].rearrange("p (k n) -> p k n", k=KD if n < 6 else 4)
            return w, piece_in[n % 2], 16 * (n // 2 + 1)

        def quarter(v, i):
            n = 4 * (v - 2) + i
            w = stage[:, 2, (n % 2) * 2048:(n % 2 + 1) * 2048].rearrange("p (k n) -> p k n", k=2)
            return n, w, quarter_in[n % 2], 16 * (n // 2 + 1)

        shift_w = [val_f.rearrange("p (k n) -> p k n", k=4),
                   qk_f[:, 4096:8192].rearrange("p (k n) -> p k n", k=4)]
        scale_w = [stage[:, 2, :].rearrange("p (k n) -> p k n", k=4),
                   stage[:, 1, :].rearrange("p (k n) -> p k n", k=4)]

        def row(v):
            return v.rearrange("l n -> (l n)").partition_broadcast(P)

        params = [
            (b_col[:, 0:2, :], b_cols_v[:, SHIFT_A:SCALE_A + 1, :]),
            (b_col[:, 2:4, :], b_cols_v[:, SHIFT_F:SCALE_F + 1, :]),
            (g_col[:, 0, :], g_attn.rearrange("l (p k) -> (l p) k", k=KD)),
            (g_col[:, 1, :], g_ffn.rearrange("l (p k) -> (l p) k", k=KD)),
            (out_g[:, 0:1], diff_out_g.rearrange("l (p o) -> (l p) o", o=1)),
            (wr[:, :, 0:G], w_group.rearrange("l (p k) g -> (l p) k g", k=KD)),
            (router_row[0:1, 0, 0:G], b_group),
            (router_row[0:1, 0, G:NR], b_expert.rearrange("l g e -> l (g e)")),
        ]
        for g in range(G):
            params.append((wr[:, :, G + g * EG:G + (g + 1) * EG], w_erouter[:, g].rearrange("l (p k) e -> (l p) k e", k=KD)))
        for n, v in enumerate((lambda_q1, lambda_k1, lambda_q2, lambda_k2)):
            params.append((lam_in[:, n, :], row(v)))
        for m in range(2):
            part = slice(m * HD, (m + 1) * HD)
            params.append((gqk[part, 0:1], q_norm_g.rearrange("l (p o) -> (l p) o", o=1)))
            params.append((gqk[part, 1:2], k_norm_g.rearrange("l (p o) -> (l p) o", o=1)))
            params.append((out_g[part, 1:2], sb_out_g.rearrange("l (p o) -> (l p) o", o=1)))
        N_PARAMS = len(params)

        IN_LAST = {0: ("qk", 3), 1: ("qk", 7), 2: ("v", 3, 0), 3: ("sq", 3), 4: ("sk", 3), 5: ("v", 3, 1)}

        block = ctx.enter_context(nc.Block())

        @block.sync
        def _(sp):
            def ada_half(dst, v, half, arrived):
                sp.dma_start(dst, ada_v[:, 4 * half:4 * half + 4, v * D:(v + 1) * D]).then_inc(arrived, 16)

            sp.wait_ge(c_in, 16)
            ada_half(shift_w[0], SHIFT_A, 0, first_in[0])
            ada_half(shift_w[1], SHIFT_A, 1, first_in[1])
            sp.dma_start(xr[:], x_rows).then_inc(x_in, 16)
            ada_half(scale_w[0], SCALE_A, 0, first_in[2])
            ada_half(scale_w[1], SCALE_A, 1, first_in[3])
            for n in range(8):
                if n == 1:
                    sp.wait_ge(scale_used, 2)
                if n >= 2:
                    sp.wait_ge(job_done, job_no[IN_LAST[n - 2]] + 1)
                dst, arrived, _ = piece(n)
                src = in_v[:, :, n * 512:(n + 1) * 512] if n < 6 else out_v[:, 4 * (n - 6):4 * (n - 6) + 4, :]
                sp.dma_start(dst, src).then_inc(arrived, 16)

            def load_expert(e, s):
                sp.dma_start(slots[s][0], w1_v[e]).then_inc(w_in_slot[s], 16)
                sp.dma_start(slots[s][1], w3_v[e]).then_inc(w_in_slot[s], 16)
                sp.dma_start(w2_dst[s], w2_v[e]).then_inc(w_in_slot[s], 16)

            sp.wait_ge(job_done, job_no[("v", 3, 1)] + 1)
            sp.wait_ge(ada_used, 16)
            load_expert(0, 0)
            sp.wait_ge(spv_done, SH)
            load_expert(1, 1)
            load_expert(2, 2)
            sp.wait_ge(y_done, 2 * NT)
            load_expert(3, 3)
            load_expert(4, 4)
            sp.wait_ge(xnb_ready, NT)
            load_expert(5, 5)
            with sp.Fori(0, (E - 8) // 4) as it:
                for s in range(4):
                    sp.wait_ge(ye_done, it * 4 + (s + 3))
                    load_expert(it * 4 + (s + 6), 2 + s)
            for e in (E - 2, E - 1):
                sp.wait_ge(ye_done, e - 3)
                load_expert(e, 2 + (e - 2) % 4)
            sp.wait_ge(plan_ready, 1)
            nq = sp.value_load(plan[0:1, 2 * NQOV:2 * NQOV + 1], min_val=0, max_val=NQOV)
            with sp.If(nq > 0):
                with sp.Fori(0, nq) as m:
                    for s in range(2):
                        sp.wait_ge(ye_done, m * 2 + (E - 1 + s))
                        e = sp.value_load(plan[0:1, bass.ds(m * 2 + s, 1)], min_val=0, max_val=E - 1)
                        load_expert(e, 2 + s)
            sp.wait_ge(y_stored[1], 16 * (NQ // 2))
            sp.wait_ge(y_stored[0], nq * 16 + 16 * (NQ // 2))
            for t in range(NT):
                dst = fin_pair(t)
                sp.dma_start(dst, y_dram.rearrange("(k t p) n -> t p k n", k=2, p=P)[t]).then_inc(pairs_in[t], 16)
            for t in range(NT):
                sp.wait_ge(fin_c, t + 1)
                sp.dma_start(out_rows[:, t, :], xr[:, t, :]).then_inc(out_stored, 16)
            sp.wait_ge(out_stored, 16 * NT)
            sp.wait_ge(xn_stored, 16 * NT)

        @block.gpsimd
        def _(pool):
            chain = [0]

            def link(ins):
                chain[0] += 1
                ins.then_inc(pool_chain, 1)
                pool.wait_ge(pool_chain, chain[0])

            g = nc.gpsimd
            link(g.memset(consts[:, 0, :], 1.0))
            g.affine_select(out=ident, in_=ident, pattern=[[-1, P]], compare_op=ALU.is_equal, fill=0.0,
                            base=0, channel_multiplier=1).then_inc(consts_ready, 1)
            link(g.memset(negtri, -1.0))
            g.affine_select(out=negtri, in_=negtri, pattern=[[-1, P]], compare_op=ALU.is_ge, fill=0.0,
                            base=0, channel_multiplier=1).then_inc(consts_ready, 1)
            g.memset(negones, -1.0).then_inc(consts_ready, 1)
            link(g.memset(tri_bf[:], 1.0))
            g.affine_select(out=tri_bf[:], in_=tri_bf[:], pattern=[[1, P]], compare_op=ALU.is_gt, fill=0.0,
                            base=0, channel_multiplier=-1).then_inc(consts_ready, 1)
            link(g.iota(ramp, pattern=[[-1, T]], base=3 * P, channel_multiplier=1))
            for h in range(DH):
                slope = 2.0 ** (-8.0 * (h + 1) / DH)
                link(g.tensor_scalar(alibi[:, h, :], ramp, -slope, None, ALU.mult))
                g.affine_select(out=alibi[:, h, :], in_=alibi[:, h, :], pattern=[[-1, T]], compare_op=ALU.is_ge,
                                fill=-1e30, base=3 * P, channel_multiplier=1).then_inc(alibi_ready, 1)
            link(g.iota(ramp[:, 0:P], pattern=[[1, P]], base=0, channel_multiplier=0))
            g.tensor_copy(slot_iota, ramp[:, 0:P]).then_inc(memset_ready, 1)
            link(g.iota(ints[:, 0:32], pattern=[[C, E]], base=0, channel_multiplier=0))
            g.tensor_copy(e64, ints[:, 0:32]).then_inc(memset_ready, 1)
            link(g.iota(ints[:, 32:32 + 2 * NQOV], pattern=[[1, 2 * NQOV]], base=0, channel_multiplier=0))
            g.tensor_copy(b_iota, ints[:, 32:32 + 2 * NQOV]).then_inc(memset_ready, 1)
            link(g.iota(ints[:, 72:80], pattern=[[-1, 8]], base=8, channel_multiplier=0))
            g.tensor_copy(rev, ints[:, 72:80]).then_inc(memset_ready, 1)
            link(g.iota(ints[:, 48:56], pattern=[[T, 2], [P, NT]], base=1, channel_multiplier=1))
            g.tensor_copy(pair_id, ints[:, 48:56]).then_inc(memset_ready, 1)

            for n, v in enumerate((GATE_A, GATE_F)):
                g.dma_start(gates[:, n, :], row(b_ada[:, v * D:(v + 1) * D])).then_inc(gate_bias_in, 16)
            for v in range(GATE_A, GATE_F + 1):
                for i in range(4):
                    n, dst, arrived, _ = quarter(v, i)
                    if n == 0:
                        pool.wait_ge(scale_used, 1)
                    if n >= 2:
                        pool.wait_ge(ada_used, n - 1)
                    g.dma_start(dst, ada_v[:, 2 * i:2 * i + 2, v * D:(v + 1) * D]).then_inc(arrived, 16)

            def mask_tiles(v, r, ready):
                v0 = v[:, r, :]
                a = v0[:, 0:1024].rearrange("p (b k) -> p b k", b=2)[:, :, 0:P]
                g.affine_select(out=a, in_=a, pattern=[[0, 2], [1, P]], compare_op=ALU.is_gt, fill=0.0,
                                base=0, channel_multiplier=-1)
                a = v0[:, 896:1152].rearrange("p (b k) -> p b k", b=2)
                g.affine_select(out=a, in_=a, pattern=[[0, 2], [1, P]], compare_op=ALU.is_gt, fill=0.0,
                                base=0, channel_multiplier=-1).then_inc(ready, 1)

            for n in range(SH + 1):
                if n < SH:
                    pool.wait_ge(soft_raw, n + 1)
                    mask_tiles(soft, n % 2, soft_ready)
                if n >= 1:
                    pool.wait_ge(stick_raw, n)
                    mask_tiles(stick, (n - 1) % 2, stick_ready)

            for w in range(2 * NT):
                pool.wait_ge(y_scaled, w + 1)
                xh = xr[:, w // 2, (w % 2) * 512:(w % 2) * 512 + 512]
                g.tensor_tensor(xh, xh, obuf[:, w % 2, :], ALU.add).then_inc(x2_ready, 1)
            g.memset(rows, 0.0).then_inc(rows_zero, 1)
            pool.wait_ge(table_ready, 1)
            pool.wait_ge(xn_stored, 16 * NT)
            pool.wait_ge(rows_zero, 1)

            def gather(q, r):
                g.indirect_dma_start(rows[:, r, :], None, xn_dram,
                                     bass.IndirectOffsetOnAxis(ap=tables[:, 0, q:q + 1], axis=0),
                                     bounds_check=T - 1, oob_is_err=False).then_inc(rows_in[r], 16)

            def scatter(q, r):
                g.indirect_dma_start(y_dram, bass.IndirectOffsetOnAxis(ap=tables[:, 1, q:q + 1], axis=0),
                                     ysb[:, r, :], None,
                                     bounds_check=2 * T - 1, oob_is_err=False).then_inc(y_stored[r], 16)

            gather(0, 0)
            gather(1, 1)
            for q in range(NQ):
                if q + 2 < NQ:
                    pool.wait_ge(eT_done, q + 1)
                    gather(q + 2, q % 2)
                pool.wait_ge(ysb_ready, q + 1)
                scatter(q, q % 2)
            pool.wait_ge(plan_ready, 1)
            nq = pool.value_load(plan[0:1, 2 * NQOV:2 * NQOV + 1], min_val=0, max_val=NQOV)
            for m in range(NQOV):
                with pool.If(nq > m):
                    pool.wait_ge(y_stored[0], 16 * (NQ // 2 + m))
                    gather(NQ + m, 0)
                    pool.wait_ge(ysb_ready, NQ + m + 1)
                    scatter(NQ + m, 0)

        @block.scalar
        def _(act):
            chain = [0]

            def link(ins):
                chain[0] += 1
                ins.then_inc(act_chain, 1)
                act.wait_ge(act_chain, chain[0])

            a = nc.scalar
            act.dma_start(c_col, c.rearrange("b (p k) -> (b p) k", k=KD)).then_inc(c_in, 16)
            for dst, src in params:
                act.dma_start(dst, src).then_inc(params_in, 16)
            act.wait_ge(c_in, 16)
            a.activation(cs, c_col, ACT.Silu).then_inc(silu_c, 1)
            a.preload_act_table_set("natural_log_exp_and_others")
            act.wait_ge(x_in, 16)
            act.wait_ge(eps_ready, 1)
            for t in range(NT):
                link(a.activation(hT_f[:, 0:D], xr[:, t, :], ACT.Square, accum_out=ssx[:, t:t + 1]))
            link(a.activation(rx, ssx, ACT.Ln, bias=eps, scale=1.0 / D))
            link(a.activation(rx, rx, ACT.Exp, scale=-0.5))
            for t in range(NT):
                a.activation(xn[:, t, :].rearrange("p (k j) -> p k j", k=KD),
                             xr[:, t, :].rearrange("p (j k) -> p k j", k=KD), ACT.Copy,
                             scale=rx[:, t:t + 1]).then_inc(xn_ready, 1)
            act.wait_ge(lam_ready, 1)
            a.activation(lam[:, 2:4], lam[:, 0:2], ACT.Exp).then_inc(lam_exp, 1)
            act.wait_ge(mod_a, 1)
            for k in range(1, KD, 2):
                act.wait_ge(xT_done, k + 1)
                a.activation(hT[:, k, :], banks[:, 2 + k % 4, :], ACT.Identity,
                             bias=mod[:, 0, k:k + 1], scale=mod[:, 1, k:k + 1]).then_inc(hT_act, 1)

            def qk_square(n):
                act.wait_ge(qk_raw, n + 1)
                if n >= 2:
                    act.wait_ge(norm_done, n - 1)
                a.activation(sqb[:, n % 2, :], qkT[:, n, :], ACT.Square).then_inc(sq_ready, 1)

            def qk_rstd(n):
                act.wait_ge(norm_done, n + 1)
                if n >= 2:
                    act.wait_ge(qk_dve, n - 1)
                link(a.activation(rqk[:, n % 2, :], banks[:, 2 + n % 2, :], ACT.Ln, bias=eps, scale=1.0 / HD))
                a.activation(rqk[:, n % 2, :], rqk[:, n % 2, :], ACT.Exp, scale=-0.5).then_inc(rqk_ready, 1)

            def job_evac(job):
                n = job_no[job]
                src = banks[:, n % 2, :]
                if job[0] == "v":
                    act.wait_ge(job_done, n + 1)
                    a.activation(val[:, job[1], job[2] * 512:job[2] * 512 + 512], src, ACT.Copy).then_inc(bank_free[n % 2], 1)
                elif job[0] == "sq":
                    act.wait_ge(job_done, n + 1)
                    a.activation(qkT[:, 8 + job[1], :], src, ACT.Copy, scale=HD ** -0.5).then_inc(bank_free[n % 2], 1)
                elif job[0] == "sk":
                    act.wait_ge(job_done, n + 1)
                    a.activation(qkT[:, 12 + job[1], :], src, ACT.Copy).then_inc(bank_free[n % 2], 1)

            for n in range(8):
                qk_square(n)
                if n >= 1:
                    qk_rstd(n - 1)
            qk_rstd(7)
            for job in head_jobs:
                job_evac(job)

            def exp_unit(u):
                h, i = u // NT, u % NT
                act.wait_ge(max_ready, u + 1)
                for m in range(2):
                    v = prob[:, u % 2, m, 0:(i + 1) * P]
                    ins = a.activation(v, v, ACT.Exp, bias=nmx[:, u % 2, m:m + 1], accum_out=lsum[:, u % 2, m:m + 1])
                ins.then_inc(exp_ready, 1)

            def probT_evac(u):
                i = u % NT
                act.wait_ge(T_done, T_no[("unit", u)] + 1)
                if u >= 2:
                    act.wait_ge(pv_done, u - 1)
                a.activation(probT[:, u % 2, 0:(i + 1) * P], banks[:, 6, 0:(i + 1) * P], ACT.Copy).then_inc(probT_ready, 1)

            def out_rstd(f):
                n = 4 if f < DH else 8
                act.wait_ge(o_sums, f + 1)
                link(a.activation(ro[:, f % 2, 0:n], sso[:, f % 2, 0:n], ACT.Ln, bias=eps, scale=n / 512.0))
                a.activation(ro[:, f % 2, 0:n], ro[:, f % 2, 0:n], ACT.Exp, scale=-0.5).then_inc(o_rstd, 1)

            def mix_evac(f):
                act.wait_ge(T_done, T_no[("fin", f)] + 1)
                if f == DH:
                    act.wait_ge(job_done, job_no[("gate", 1, 1)] + 1)
                a.activation(mixT[:, f, :], banks[:, 6, :], ACT.Copy,
                             scale=out_g[:, f // DH:f // DH + 1]).then_inc(mix_ready, 1)

            for s in range(DIFF_STEPS):
                if s >= 1:
                    for job in step_jobs.get(s - 1, ()):
                        job_evac(job)
                if s < 16:
                    exp_unit(s)
                if 1 <= s <= 16:
                    probT_evac(s - 1)
                for f in range(DH):
                    if s == fin_step(f):
                        out_rstd(f)
                    if s == fin_step(f) + 2:
                        mix_evac(f)

            for s in range(STICK_STEPS):
                for f in range(DH):
                    if DIFF_STEPS + s == fin_step(f) + 2:
                        mix_evac(f)
                if s < SH:
                    act.wait_ge(z_done, s + 1)
                    if s >= 2:
                        act.wait_ge(tri_done, s - 1)
                    v = soft[:, s % 2, :]
                    link(a.activation(v, zps[s % 2][:, 0:ZCOLS], ACT.Abs))
                    link(a.activation(v, v, ACT.Exp, scale=-1.0))
                    a.activation(v, v, ACT.Ln, bias=1.0).then_inc(ln_ready, 1)
                if 1 <= s <= SH:
                    act.wait_ge(tri_done, s)
                    if s >= 3:
                        act.wait_ge(spv_done, s - 2)
                    a.activation(stick[:, (s - 1) % 2, :], zps[(s - 1) % 2][:, 0:ZCOLS], ACT.Exp).then_inc(stick_raw, 1)
                for f in range(DH, 2 * DH):
                    if DIFF_STEPS + s == fin_step(f):
                        out_rstd(f)
                    if DIFF_STEPS + s == fin_step(f) + 2:
                        mix_evac(f)

            for t in range(NT):
                act.wait_ge(x2_ready, 2 * t + 2)
                link(a.activation(obuf[:, 2:4, :].rearrange("p a b -> p (a b)"), xr[:, t, :], ACT.Square,
                                  accum_out=ss2[:, t:t + 1]))
                link(a.activation(r2[:, t:t + 1], ss2[:, t:t + 1], ACT.Ln, bias=eps, scale=1.0 / D))
                link(a.activation(r2[:, t:t + 1], r2[:, t:t + 1], ACT.Exp, scale=-0.5))
                if t >= 2:
                    act.wait_ge(fT_done, t - 1)
                    act.wait_ge(xn_stored, 16 * t)
                a.activation(xnb[:, t % 2, :].rearrange("p (k j) -> p k j", k=KD),
                             xr[:, t, :].rearrange("p (j k) -> p k j", k=KD), ACT.Copy,
                             scale=r2[:, t:t + 1]).then_inc(xnb_ready, 1)
                act.wait_ge(xnb_ready, t + 1)
                act.dma_start(xn_dram[t * P:(t + 1) * P, :], xnb[:, t % 2, :]).then_inc(xn_stored, 16)
            act.wait_ge(g_exp_in, 1)
            a.activation(exp_g, exp_g, ACT.Exp).then_inc(g_exp, 1)
            act.wait_ge(d_in, 1)
            a.activation(exp_d, exp_d, ACT.Exp).then_inc(d_exp, 1)
            a.preload_act_table(ACT.Silu)

            def silu(n, r):
                act.wait_ge(h_done, n)
                a.activation(gact[:, r, :], banks[:, 2 + r, 0:P], ACT.Silu).then_inc(silu_ready, 1)

            with act.Fori(0, NQ) as q:
                for half in range(2):
                    silu(q * 2 + (half + 1), half)
            act.wait_ge(plan_ready, 1)
            nq = act.value_load(plan[0:1, 2 * NQOV:2 * NQOV + 1], min_val=0, max_val=NQOV)
            with act.If(nq > 0):
                with act.Fori(0, nq) as m:
                    for half in range(2):
                        silu(m * 2 + (E + half + 1), half)
            for t in range(NT):
                act.wait_ge(pairs_in[t], 16)
                a.activation(fin_pair(t)[:, 1, :], fin_pair(t)[:, 1, :], ACT.Copy,
                             scale=wpair[:, 1, t:t + 1]).then_inc(fin_a, 1)

        @block.vector
        def _(dve):
            chain = [0]

            def link(ins):
                chain[0] += 1
                ins.then_inc(dve_chain, 1)
                dve.wait_ge(dve_chain, chain[0])

            v = nc.vector
            def accumulate(dst, src, k, first):
                s = cs[:, k:k + 1]
                if first:
                    return v.tensor_scalar(dst, src, s, None, ALU.mult)
                return v.scalar_tensor_tensor(out=dst, in0=src, scalar=s, in1=dst, op0=ALU.mult, op1=ALU.add)

            def shift_sums():
                for half in range(2):
                    dve.wait_ge(first_in[half], 16)
                    for k in range(4):
                        accumulate(acc[:, 0, :], shift_w[half][:, k, :], 4 * half + k,
                                   half + k == 0).then_inc(shift_used, 1)
                        dve.wait_ge(shift_used, 4 * half + k + 1)

            v.memset(eps, EPS).then_inc(eps_ready, 1)
            v.memset(ones, 1.0).then_inc(consts_dve, 1)
            v.memset(ones_bf[:], 1.0).then_inc(consts_dve, 1)
            v.memset(zero32, 0.0).then_inc(consts_dve, 1)
            link(v.memset(halves, 0.0))
            v.memset(halves[0:HD, 0:HD], 1.0).then_inc(consts_dve, 1)
            v.memset(halves[HD:P, HD:P], 1.0).then_inc(consts_dve, 1)
            dve.wait_ge(silu_c, 1)
            shift_sums()
            dve.wait_ge(params_in, 16 * N_PARAMS)
            for m in range(2):
                ins = v.tensor_tensor_reduce(out=obuf[:, m, 0:HD], in0=lam_in[:, 2 * m, :], in1=lam_in[:, 2 * m + 1, :],
                                             scale=1.0, scalar=0.0, op0=ALU.mult, op1=ALU.add,
                                             accum_out=lam[:, m:m + 1])
            ins.then_inc(lam_ready, 1)
            link(v.tensor_scalar(gqk[:, 0:1], gqk[:, 0:1], HD ** -0.5, None, ALU.mult))
            link(v.tensor_scalar(out_g[:, 0:1], out_g[:, 0:1], 1.0 - LAMBDA_INIT, None, ALU.mult))

            def ada_quarter(vec, i):
                if i == 0 and vec in (2, 3):
                    dve.wait_ge(col_a, 1)
                if i == 0 and vec == 4:
                    dve.wait_ge(job_done, job_no[("gate", 0, 1)] + 1)
                if i == 0 and vec == 5:
                    dve.wait_ge(job_done, job_no[("col", 2)] + 1)
                n, src, arrived, value = quarter(vec, i)
                dve.wait_ge(arrived, value)
                link(accumulate(acc[:, vec % 2, :], src[:, 0, :], 2 * i, i == 0))
                accumulate(acc[:, vec % 2, :], src[:, 1, :], 2 * i + 1, False).then_inc(ada_used, 1)
                dve.wait_ge(ada_used, n + 1)

            dve.wait_ge(col_a, 1)
            v.tensor_tensor(mod[:, 0, :], banks[:, 0, 0:8], b_col[:, 0, :], ALU.add)
            link(v.tensor_tensor(mod[:, 1, :], banks[:, 0, 8:16], b_col[:, 1, :], ALU.add))
            v.scalar_tensor_tensor(out=mod[:, 1, :], in0=mod[:, 1, :], scalar=1.0, in1=g_col[:, 0, :],
                                   op0=ALU.add, op1=ALU.mult).then_inc(mod_a, 1)
            dve.wait_ge(mod_a, 1)
            for k in range(0, KD, 2):
                dve.wait_ge(xT_done, k + 1)
                v.tensor_scalar(hT[:, k, :], banks[:, 2 + k % 4, :], mod[:, 1, k:k + 1], mod[:, 0, k:k + 1],
                                ALU.mult, ALU.add).then_inc(hT_dve, 1)
            dve.wait_ge(lam_exp, 1)
            link(v.tensor_tensor(neglam, lam[:, 3:4], lam[:, 2:3], ALU.subtract))
            link(v.tensor_scalar(neglam, neglam, -LAMBDA_INIT, None, ALU.add))

            def qk_scale(n):
                dve.wait_ge(rqk_ready, n + 1)
                v.scalar_tensor_tensor(out=qkT[:, n, :], in0=qkT[:, n, :], scalar=gqk[:, n // 4:n // 4 + 1],
                                       in1=rqk[:, n % 2, :], op0=ALU.mult, op1=ALU.mult).then_inc(qk_dve, 1)

            for n in range(8):
                b = job_no[("qk", n)] % 2
                dve.wait_ge(job_done, n + 1)
                v.tensor_copy(qkT[:, n, :], banks[:, b, :]).then_inc(qk_raw, 1)
                if n >= 1:
                    qk_scale(n - 1)
                ada_quarter(GATE_A + n // 4, n % 4)
            qk_scale(7)

            def job_evac(job):
                n = job_no[job]
                src = banks[:, n % 2, :]
                if job[0] == "gate":
                    dve.wait_ge(gate_bias_in, 32)
                    dve.wait_ge(job_done, n + 1)
                    dst = gates[:, job[1], job[2] * 512:job[2] * 512 + 512]
                    v.tensor_tensor(dst, src, dst, ALU.add).then_inc(bank_free[n % 2], 1)
                elif job[0] == "col":
                    dve.wait_ge(job_done, n + 1)
                    w = job[1]
                    v.tensor_tensor(mod[:, w, :], src[:, 0:8], b_col[:, w, :], ALU.add).then_inc(bank_free[n % 2], 1)
                    dve.wait_ge(bank_free[n % 2], freed[job][1])
                    if w == 3:
                        link(v.scalar_tensor_tensor(out=mod[:, 3, :], in0=mod[:, 3, :], scalar=1.0,
                                                    in1=g_col[:, 1, :], op0=ALU.add, op1=ALU.mult))
                        v.tensor_tensor(wrA[:], wr[:], mod[:, 3, :].unsqueeze(2).to_broadcast([P, KD, NR]),
                                        ALU.mult).then_inc(wrA_ready, 1)
                elif job[0] == "shift_router":
                    dve.wait_ge(job_done, n + 1)
                    v.tensor_tensor(router_row[0:1, 1, :], src[0:1, 0:NR], router_row[0:1, 0, :],
                                    ALU.add).then_inc(bank_free[n % 2], 1)

            for job in head_jobs:
                job_evac(job)

            def max_unit(u):
                h, i = u // NT, u % NT
                if u == 0:
                    dve.wait_ge(alibi_ready, DH)
                dve.wait_ge(score_done, u + 1)
                W = (i + 1) * P
                if u >= 2:
                    dve.wait_ge(T_done, T_no[("unit", u - 2)] + 1)
                for m in range(2):
                    ins = v.tensor_tensor_reduce(out=prob[:, u % 2, m, 0:W], in0=banks[:, 2 + 2 * (u % 2) + m, 0:W],
                                                 in1=alibi[:, h, T - W:T], scale=1.0, scalar=-3e38,
                                                 op0=ALU.add, op1=ALU.max, accum_out=mx[:, u % 2, m:m + 1])
                link(ins)
                v.tensor_scalar(nmx[:, u % 2, :], mx[:, u % 2, :], -1.0, None, ALU.mult).then_inc(max_ready, 1)

            def combine_unit(u):
                i = u % NT
                W = (i + 1) * P
                dve.wait_ge(exp_ready, u + 1)
                link(v.reciprocal(rl[:, u % 2, :], lsum[:, u % 2, :]))
                link(v.tensor_scalar(rl[:, u % 2, 1:2], rl[:, u % 2, 1:2], neglam, None, ALU.mult))
                p0, p1 = prob[:, u % 2, 0, 0:W], prob[:, u % 2, 1, 0:W]
                link(v.tensor_scalar(p1, p1, rl[:, u % 2, 1:2], None, ALU.mult))
                v.scalar_tensor_tensor(out=p0, in0=p0, scalar=rl[:, u % 2, 0:1], in1=p1,
                                       op0=ALU.mult, op1=ALU.add).then_inc(prob_ready, 1)

            def out_sums(f):
                n = 4 if f < DH else 8
                if f < DH:
                    dve.wait_ge(pv_done, NT * (f + 1))
                else:
                    dve.wait_ge(spv_done, 2 * (f - DH) + 2)
                o = obuf[:, f % 2, :]
                v.tensor_copy(o, banks[:, 7, :]).then_inc(o_copied, 1)
                dve.wait_ge(o_copied, f + 1)
                if f >= 2:
                    dve.wait_ge(T_done, T_no[("fin", f - 2)] + 1)
                sq = obuf[:, 2 + f % 2, :]
                link(v.tensor_tensor(sq, o, o, ALU.mult))
                v.tensor_reduce(sso[:, f % 2, 0:n], sq.rearrange("p (g w) -> p g w", g=n), X,
                                ALU.add).then_inc(o_sums, 1)

            def out_scale(f):
                n = 4 if f < DH else 8
                dve.wait_ge(o_rstd, f + 1)
                w = 512 // n
                v.tensor_tensor(obuf[:, 2 + f % 2, :].rearrange("p (g w) -> p g w", g=n),
                                obuf[:, f % 2, :].rearrange("p (g w) -> p g w", g=n),
                                ro[:, f % 2, 0:n].unsqueeze(2).to_broadcast([P, n, w]), ALU.mult).then_inc(o_ready, 1)

            for s in range(DIFF_STEPS):
                if s >= 1:
                    for job in step_jobs.get(s - 1, ()):
                        job_evac(job)
                if 1 <= s <= 16:
                    combine_unit(s - 1)
                if s < 16:
                    max_unit(s)
                if s < 8:
                    ada_quarter(SCALE_F + s // 4, s % 4)
                for f in range(DH):
                    if s == fin_step(f):
                        out_sums(f)
                    if s == fin_step(f) + 1:
                        out_scale(f)

            for s in range(STICK_STEPS):
                for f in range(DH):
                    if DIFF_STEPS + s == fin_step(f) + 1:
                        out_scale(f)
                if s < SH:
                    dve.wait_ge(ln_ready, s + 1)
                    v.scalar_tensor_tensor(out=soft[:, s % 2, :], in0=zps[s % 2][:, 0:ZCOLS], scalar=0.0,
                                           in1=soft[:, s % 2, :], op0=ALU.max, op1=ALU.add).then_inc(soft_raw, 1)
                for f in range(DH, 2 * DH):
                    if DIFF_STEPS + s == fin_step(f):
                        out_sums(f)
                        out_scale(f)

            def copy_x2T(t):
                dve.wait_ge(fT_done, t + 1)
                if t >= 2:
                    dve.wait_ge(logits_done, t - 1)
                v.tensor_copy(x2T[:, t % 2, :], banks[:, 6:8, :].rearrange("p b k -> p (b k)")).then_inc(x2T_ready, 1)

            for w in range(2 * NT):
                dve.wait_ge(y_done, w + 1)
                if w >= 2:
                    dve.wait_ge(x2_ready, w - 1)
                else:
                    dve.wait_ge(T_done, T_no[("fin", 7)] + 1)
                v.tensor_tensor(obuf[:, w % 2, :], banks[:, w % 5, :], gates[:, 0, (w % 2) * 512:(w % 2) * 512 + 512],
                                ALU.mult).then_inc(y_scaled, 1)
                if w >= 5 and w % 2 == 1:
                    copy_x2T((w - 5) // 2)
            for t in range(2, NT):
                copy_x2T(t)

            n32 = NT * 32
            lg = rt[:, 0:NT * NR].rearrange("p (t r) -> p t r", t=NT)
            o1 = NT * NR
            gsel = rt[:, o1:o1 + 16].rearrange("p (t g) -> p t g", t=NT)
            gkey = rt[:, o1 + 16:o1 + 32].rearrange("p (t g) -> p t g", t=NT)
            ge = exp_g.rearrange("p (t g) -> p t g", t=NT)
            prod = rt[:, o1 + 64:o1 + 64 + n32].rearrange("p (t g j) -> p t g j", t=NT, g=G)
            o2 = o1 + 64 + n32
            esel = rt[:, o2:o2 + 32].rearrange("p (t j) -> p t j", t=NT)
            key = rt[:, o2 + 32:o2 + 64].rearrange("p (t j) -> p t j", t=NT)
            oh = [rt[:, o2 + 64 + 32 * k:o2 + 96 + 32 * k].rearrange("p (t j) -> p t j", t=NT) for k in range(2)]
            o3 = o2 + 128
            sc = [rt[:, o3 + 4 * n:o3 + 4 * n + 4] for n in range(10)]
            gmax, kmax, gsum, ggate, m1, m2, den = sc[:7]
            dlt = exp_d
            o4 = o3 + 40
            rank = rt[:, o4:o4 + n32].rearrange("p (t e) -> p t e", t=NT)
            ov = rt[:, o4 + n32:o4 + 2 * n32].rearrange("p (t e) -> p t e", t=NT)
            sel = rt[:, o4 + 2 * n32:o4 + 3 * n32].rearrange("p (t e) -> p t e", t=NT)
            o5 = o4 + 3 * n32
            cnt, extra, incl, obase = (rt[:, o5 + 32 * n:o5 + 32 * n + 32] for n in range(4))
            posf = rt[:, o5 + 128:o5 + 136].rearrange("p (k t) -> p k t", k=2)
            assert o5 + 136 <= 1536 - 8

            def b3(ap, n):
                return ap.unsqueeze(2).to_broadcast([P, NT, n])

            def first_max(src, n, keybuf, onehot):
                link(v.tensor_reduce(kmax, src, X, ALU.max))
                link(v.tensor_tensor(keybuf, src, b3(kmax, n), ALU.is_equal))
                link(v.tensor_tensor(keybuf, keybuf, rev[:, 8 - n:8].unsqueeze(1).to_broadcast([P, NT, n]), ALU.mult))
                link(v.tensor_reduce(den, keybuf, X, ALU.max))
                link(v.tensor_tensor(onehot, keybuf, b3(den, n), ALU.is_equal))

            dve.wait_ge(memset_ready, 5)
            dve.wait_ge(logits_done, NT)
            link(v.tensor_copy(lg, banks[:, 5, 0:NT * NR].rearrange("p (t r) -> p t r", t=NT)))
            first_max(lg[:, :, 0:G], G, gkey, gsel)
            v.tensor_tensor(ge, lg[:, :, 0:G], b3(kmax, G), ALU.subtract).then_inc(g_exp_in, 1)
            link(v.tensor_tensor(prod, lg[:, :, G:NR].rearrange("p t (g j) -> p t g j", g=G),
                                 gsel.unsqueeze(3).to_broadcast([P, NT, G, EG]), ALU.mult))
            link(v.tensor_reduce(esel, prod.rearrange("p t g j -> p t j g"), X, ALU.add))
            first_max(esel, EG, key, oh[0])
            link(v.tensor_copy(m1, kmax))
            link(v.scalar_tensor_tensor(out=esel, in0=oh[0], scalar=-1e30, in1=esel, op0=ALU.mult, op1=ALU.add))
            first_max(esel, EG, key, oh[1])
            v.tensor_tensor(dlt, kmax, m1, ALU.subtract).then_inc(d_in, 1)
            for k in range(2):
                for t in range(NT):
                    link(v.tensor_tensor(masks[:, k, t, :].rearrange("p (g j) -> p g j", g=G),
                                         gsel[:, t, :].unsqueeze(2).to_broadcast([P, G, EG]),
                                         oh[k][:, t, :].unsqueeze(1).to_broadcast([P, G, EG]), ALU.mult))
            v.tensor_tensor(masks[:, 2, :, :], masks[:, 0, :, :], masks[:, 1, :, :], ALU.add).then_inc(masks_ready, 1)
            dve.wait_ge(rank_done, 1)
            link(v.tensor_copy(rank, banks[:, 0, 0:n32].rearrange("p (t e) -> p t e", t=NT)))
            link(v.tensor_scalar(ints[:, 0:32], banks[:, 0, n32:n32 + 32], float(C - 1), None, ALU.add))
            link(v.tensor_scalar(ints[:, 0:32], ints[:, 0:32], C.bit_length() - 1, None, ALU.arith_shift_right))
            link(v.tensor_copy(cnt, ints[:, 0:32]))
            link(v.tensor_scalar(extra, cnt, -1.0, 0.0, ALU.add, ALU.max))
            link(v.tensor_tensor_scan(incl, extra, zero32, 0.0, ALU.add, ALU.add))
            link(v.tensor_tensor(obase, incl, extra, ALU.subtract))
            link(v.tensor_scalar(obase, obase, float(E - 1), float(C), ALU.add, ALU.mult))
            link(v.tensor_tensor(obase, obase, e64, ALU.subtract))
            link(v.tensor_scalar(ov, rank, float(C), None, ALU.is_ge))
            link(v.tensor_tensor(ov, ov, obase.unsqueeze(1).to_broadcast([P, NT, E]), ALU.mult))
            link(v.tensor_tensor(rank, rank, e64.unsqueeze(1).to_broadcast([P, NT, E]), ALU.add))
            link(v.tensor_tensor(rank, rank, ov, ALU.add))
            for k in range(2):
                link(v.tensor_tensor(sel, rank, masks[:, k, :, :], ALU.mult))
                link(v.tensor_reduce(posf[:, k, :], sel, X, ALU.add))
            posi, lo_i = ints[:, 80:88], ints[:, 88:96]
            pos2 = rt[:, o5 + 128:o5 + 136]
            link(v.tensor_copy(posi, pos2))
            link(v.tensor_scalar(lo_i, posi, P - 1, None, ALU.bitwise_and))
            link(v.tensor_scalar(posi, posi, P.bit_length() - 1, None, ALU.logical_shift_right))
            lof, hif = cnt[:, 0:8], cnt[:, 8:16]
            link(v.tensor_copy(lof, lo_i))
            link(v.tensor_copy(hif, posi))
            dve.wait_ge(logits_done, NT)
            v.tensor_tensor(onehot, slot_iota.unsqueeze(1).to_broadcast([P, 2 * NT, P]),
                            lof.unsqueeze(2).to_broadcast([P, 2 * NT, P]), ALU.is_equal)
            hot_col = rt[:, 0:2 * NT * NCOL].rearrange("p (c q) -> p c q", c=2 * NT)
            link(v.tensor_tensor(hot_col, slot_iota[:, 0:NCOL].unsqueeze(1).to_broadcast([P, 2 * NT, NCOL]),
                                 hif.unsqueeze(2).to_broadcast([P, 2 * NT, NCOL]), ALU.is_equal))
            v.tensor_tensor(hot_col, hot_col, pair_id.unsqueeze(2).to_broadcast([P, 2 * NT, NCOL]),
                            ALU.mult).then_inc(onehot_ready, 1)
            dve.wait_ge(onehot_ready, 1)
            dve.wait_ge(table_done, 1)
            found, free = onehot[:, 0, 0:NCOL], onehot[:, 1, 0:NCOL]
            link(v.tensor_copy(found, banks[:, 1, 0:NCOL]))
            link(v.tensor_scalar(free, found, 0.0, float(SKIP), ALU.is_equal, ALU.mult))
            link(v.scalar_tensor_tensor(out=found, in0=found, scalar=-1.0, in1=free, op0=ALU.add, op1=ALU.add))
            v.tensor_copy(tables[:, 1, :], found)
            link(v.tensor_scalar(free, found, float(T), float(-T), ALU.is_ge, ALU.mult))
            v.tensor_tensor(tables[:, 0, :], found, free, ALU.add).then_inc(table_ready, 1)
            dve.wait_ge(table_ready, 1)
            over = rt[0:1, 0:2 * NQOV * E].rearrange("p (b e) -> p b e", e=E)
            nover = sel[0:1, 0, 0:2 * NQOV]
            link(v.tensor_tensor(over, incl[0:1, :].unsqueeze(1).to_broadcast([1, 2 * NQOV, E]),
                                 b_iota[0:1, :].unsqueeze(2).to_broadcast([1, 2 * NQOV, E]), ALU.is_le))
            link(v.tensor_reduce(nover, over, X, ALU.add))
            link(v.tensor_scalar(plan[0:1, 0:2 * NQOV], nover, float(E - 1), None, ALU.min))
            last = plan[0:1, 2 * NQOV:2 * NQOV + 1]
            link(v.tensor_scalar(last, incl[0:1, E - 1:E], 1.0, None, ALU.add))
            v.tensor_scalar(last, last, 1, None, ALU.logical_shift_right).then_inc(plan_ready, 1)
            dve.wait_ge(g_exp, 1)
            link(v.tensor_reduce(gsum, ge, X, ALU.add))
            link(v.reciprocal(ggate, gsum))
            dve.wait_ge(d_exp, 1)
            link(v.tensor_scalar(den, dlt, 1.0, None, ALU.add))
            link(v.reciprocal(den, den))
            link(v.tensor_tensor(wpair[:, 0, :], den, ggate, ALU.mult))
            link(v.tensor_tensor(wpair[:, 1, :], wpair[:, 0, :], dlt, ALU.mult))

            def modulate(n, r):
                dve.wait_ge(eT_done, n)
                dst = heT[:, r, :].rearrange("p (k t) -> p k t", k=KD)
                src = banks[:, 0:2, :].rearrange("p b (k t) -> p (b k) t", t=P)
                v.tensor_tensor(dst, src, mod[:, 3, :].unsqueeze(2).to_broadcast([P, KD, P]), ALU.mult).then_inc(he_mul, 1)
                dve.wait_ge(he_mul, n)
                v.tensor_tensor(dst, dst, mod[:, 2, :].unsqueeze(2).to_broadcast([P, KD, P]), ALU.add).then_inc(heT_ready, 1)

            def gated(n, r):
                dve.wait_ge(silu_ready, n)
                v.tensor_tensor(geT[:, r, :], gact[:, r, :], banks[:, 2 + r, P:2 * P], ALU.mult).then_inc(ge_ready, 1)

            def y_evac(n_experts, r, w):
                dve.wait_ge(ye_done, n_experts)
                v.tensor_tensor(ysb[0:w, r, :], banks[0:w, 4 + 2 * r:6 + 2 * r, :].rearrange("p b k -> p (b k)"),
                                gates[0:w, 1, :], ALU.mult).then_inc(ysb_ready, 1)

            dve.wait_ge(fT_done, NT)
            dve.wait_ge(xn_stored, 16 * NT)
            modulate(1, 0)

            def pair(q, r, stored, last):
                gated(q * 2 + 1, 0)
                if not last:
                    modulate(q + 2, 1 - r)
                gated(q * 2 + 2, 1)
                if stored is not None:
                    dve.wait_ge(y_stored[r], stored)
                y_evac(q * 2 + 2, r, P)

            pair(0, 0, None, False)
            pair(1, 1, None, False)
            pair(2, 0, 16, False)
            with dve.Fori(1, NQ // 2 - 1) as it:
                pair(it * 2 + 1, 1, it * 16, False)
                pair(it * 2 + 2, 0, it * 16 + 16, False)
            pair(NQ - 1, 1, 16 * (NQ // 2 - 1), True)
            dve.wait_ge(plan_ready, 1)
            nq = dve.value_load(plan[0:1, 2 * NQOV:2 * NQOV + 1], min_val=0, max_val=NQOV)
            with dve.If(nq > 0):
                with dve.Fori(0, nq) as m:
                    modulate(m + (NQ + 1), 0)
                    pair(m + NQ, 0, m * 16 + 16 * (NQ // 2), True)
            for t in range(NT):
                dve.wait_ge(pairs_in[t], 16)
                v.scalar_tensor_tensor(out=xr[:, t, :], in0=fin_pair(t)[:, 0, :], scalar=wpair[:, 0, t:t + 1],
                                       in1=xr[:, t, :], op0=ALU.mult, op1=ALU.add).then_inc(fin_b, 1)
                dve.wait_ge(fin_b, t + 1)
                dve.wait_ge(fin_a, t + 1)
                v.tensor_tensor(xr[:, t, :], xr[:, t, :], fin_pair(t)[:, 1, :], ALU.add).then_inc(fin_c, 1)

        @block.tensor
        def _(pe):
            mm = nc.tensor.matmul
            pe.wait_ge(consts_ready, 4)
            pe.wait_ge(consts_dve, 5)

            pe.wait_ge(silu_c, 1)
            for half in range(2):
                pe.wait_ge(first_in[2 + half], 16)
                for k in range(4):
                    w = scale_w[half][:, k, :].rearrange("p (j k) -> p k j", k=KD)
                    for c_out in range(KD):
                        ins = mm(banks[:, 0, 8 + c_out:9 + c_out], w[:, c_out, :], cs[:, 4 * half + k:4 * half + k + 1],
                                 start=(half + k + c_out == 0), stop=(half + k == 4), skip_group_check=True)
                ins.then_inc(scale_used, 1)
            pe.wait_ge(shift_used, KD)
            for k in range(KD):
                ins = mm(banks[:, 0, k:k + 1], acc[:, 0, :].rearrange("p (j k) -> p k j", k=KD)[:, k, :], ones[:, 0:1],
                         start=False, stop=True, skip_group_check=True)
            ins.then_inc(col_a, 1)
            pe.wait_ge(xn_ready, NT)
            for k in range(KD):
                if k >= 4:
                    if k % 2:
                        pe.wait_ge(hT_act, (k - 4) // 2 + 1)
                    else:
                        pe.wait_ge(hT_dve, (k - 4) // 2 + 1)
                for t in range(NT):
                    ins = nc.tensor.transpose(banks[:, 2 + k % 4, t * P:(t + 1) * P], xn[:, t, k * P:(k + 1) * P], ident)
                ins.then_inc(xT_done, 1)
            pe.wait_ge(hT_act, KD // 2)
            pe.wait_ge(hT_dve, KD // 2)

            def wait_freed(job):
                which, value = freed[job]
                pe.wait_ge(qk_raw if which == "qk" else bank_free[which], value)

            def run(job):
                n = job_no[job]
                bank = banks[:, n % 2, :]
                if n >= 2:
                    wait_freed(job_at[n - 2])
                kind = job[0]
                if kind in ("qk", "sq", "sk"):
                    n_in, ch = {"qk": (job[1] // 4, job[1] % 4), "sq": (3, job[1]), "sk": (4, job[1])}[kind]
                    w, arrived, value = piece(n_in)
                    pe.wait_ge(arrived, value)
                    for k in range(KD):
                        ins = mm(bank, w[:, k, ch * P:(ch + 1) * P], hT[:, k, :], start=(k == 0), stop=(k == KD - 1))
                elif kind == "v":
                    w, arrived, value = piece(2 if job[2] == 0 else 5)
                    pe.wait_ge(arrived, value)
                    for k in range(KD):
                        ins = mm(bank, hT[:, k, job[1] * P:(job[1] + 1) * P], w[:, k, :], start=(k == 0), stop=(k == KD - 1))
                elif kind == "gate":
                    v = 2 if job[1] == 0 else 5
                    pe.wait_ge(ada_used, 4 * (v - 1))
                    ins = mm(bank, ones, acc[:, v % 2, job[2] * 512:job[2] * 512 + 512], start=True, stop=True)
                elif kind == "col":
                    v = job[1] + 1
                    pe.wait_ge(ada_used, 4 * (v - 1))
                    for k in range(KD):
                        ins = mm(bank[:, k:k + 1], acc[:, v % 2, :].rearrange("p (j k) -> p k j", k=KD)[:, k, :],
                                 ones[:, 0:1], start=(k == 0), stop=True, skip_group_check=True)
                elif kind == "shift_router":
                    wait_freed(("col", 2))
                    for k in range(KD):
                        ins = mm(bank[0:1, 0:NR], mod[:, 2, k:k + 1], wr[:, k, :], start=(k == 0), stop=(k == KD - 1))
                ins.then_inc(job_done, 1)

            def qk_norm(n):
                pe.wait_ge(sq_ready, n + 1)
                if n >= 2:
                    pe.wait_ge(rqk_ready, n - 1)
                mm(banks[:, 2 + n % 2, :], halves, sqb[:, n % 2, :], start=True, stop=True).then_inc(norm_done, 1)

            for i, job in enumerate(head_jobs):
                run(job)
                if 1 <= i <= 8:
                    qk_norm(i - 1)

            def scores(u):
                h, i = u // NT, u % NT
                W = (i + 1) * P
                if u == 0:
                    pe.wait_ge(qk_dve, 8)
                    pe.wait_ge(rqk_ready, 8)
                if u >= 2:
                    pe.wait_ge(max_ready, u - 1)
                for m in range(2):
                    q = qkT[m * HD:(m + 1) * HD, h, i * P:(i + 1) * P]
                    k = qkT[m * HD:(m + 1) * HD, 4 + h, 0:W]
                    ins = mm(banks[:, 2 + 2 * (u % 2) + m, 0:W], q, k, start=True, stop=True)
                ins.then_inc(score_done, 1)

            def T_free(n):
                if n >= 1:
                    kind, w = T_order[n - 1]
                    pe.wait_ge(probT_ready if kind == "unit" else mix_ready, w + 1)

            def probT_make(u):
                i = u % NT
                pe.wait_ge(prob_ready, u + 1)
                T_free(T_no[("unit", u)])
                for kb in range(i + 1):
                    ins = nc.tensor.transpose(banks[:, 6, kb * P:(kb + 1) * P], prob[:, u % 2, 0, kb * P:(kb + 1) * P], ident)
                ins.then_inc(T_done, 1)

            def pv(u):
                h, i = u // NT, u % NT
                pe.wait_ge(probT_ready, u + 1)
                if i == 0 and h == 0:
                    wait_freed(("v", NT - 2, 0))
                    wait_freed(("v", NT - 1, 0))
                if i == 0 and h >= 1:
                    pe.wait_ge(o_copied, h)
                for kb in range(i + 1):
                    ins = mm(banks[:, 7, i * P:(i + 1) * P], probT[:, u % 2, kb * P:(kb + 1) * P],
                             val[:, kb, h * P:(h + 1) * P], start=(i == 0 and kb == 0), stop=(kb == i),
                             skip_group_check=True)
                ins.then_inc(pv_done, 1)

            def fin_T(f):
                pe.wait_ge(o_ready, f + 1)
                T_free(T_no[("fin", f)])
                o = obuf[:, 2 + f % 2, :]
                for i in range(NT):
                    ins = nc.tensor.transpose(banks[:, 6, i * P:(i + 1) * P], o[:, i * P:(i + 1) * P], ident)
                ins.then_inc(T_done, 1)

            for s in range(DIFF_STEPS):
                if s < 16:
                    scores(s)
                if 1 <= s <= 16:
                    probT_make(s - 1)
                if 2 <= s <= 17:
                    pv(s - 2)
                for f in range(DH):
                    if s == fin_step(f) + 2:
                        fin_T(f)
                for job in step_jobs.get(s, ()):
                    run(job)

            def stick_scores(n):
                pair, s = n // 2, n % 2
                if n == 0:
                    wait_freed(job_at[len(job_no) - 2])
                    wait_freed(job_at[len(job_no) - 1])
                    pe.wait_ge(max_ready, 16)
                if n >= 2:
                    pe.wait_ge(stick_raw, n - 1)
                for kb in (0, 1, 3, 2):
                    W = T - kb * P
                    k = qkT[s * HD:(s + 1) * HD, 12 + pair, kb * P:(kb + 1) * P]
                    q = qkT[s * HD:(s + 1) * HD, 8 + pair, kb * P:T]
                    ins = mm(zps[n % 2][:, ZOFF[kb]:ZOFF[kb] + W], k, q, start=(kb != 3), stop=True,
                             skip_group_check=True)
                ins.then_inc(z_done, 1)

            def stick_sums(n):
                pe.wait_ge(soft_ready, n + 1)
                for kb in range(NT):
                    for j in range(kb, NT):
                        W = T - j * P
                        o = ZOFF[kb] + (j - kb) * P
                        ins = mm(zps[n % 2][:, o:o + W], negtri if j == kb else negones,
                                 soft[:, n % 2, ZOFF[j]:ZOFF[j] + W], start=False, stop=True, skip_group_check=True)
                ins.then_inc(tri_done, 1)

            def stick_pv(n):
                pair, s = n // 2, n % 2
                pe.wait_ge(stick_ready, n + 1)
                if s == 0:
                    pe.wait_ge(o_copied, DH + pair)
                for i in range(NT):
                    for kb in range(i + 1):
                        o = ZOFF[kb] + (i - kb) * P
                        ins = mm(banks[:, 7, i * P + s * HD:i * P + (s + 1) * HD], stick[:, n % 2, o:o + P],
                                 val[:, kb, 512 + n * HD:512 + (n + 1) * HD],
                                 start=(s == 0 and i == 0 and kb == 0), stop=(kb == i), skip_group_check=True)
                ins.then_inc(spv_done, 1)

            for s in range(STICK_STEPS):
                for f in range(DH):
                    if DIFF_STEPS + s == fin_step(f) + 2:
                        fin_T(f)
                if s < SH:
                    stick_scores(s)
                if 1 <= s <= SH:
                    stick_sums(s - 1)
                if 2 <= s <= SH + 1:
                    stick_pv(s - 2)
                for f in range(DH, 2 * DH):
                    if DIFF_STEPS + s == fin_step(f) + 2:
                        fin_T(f)

            def out_proj(w):
                t, half = w // 2, w % 2
                if w == 0:
                    for n in (6, 7):
                        _, arrived, value = piece(n)
                        pe.wait_ge(arrived, value)
                    pe.wait_ge(mix_ready, 8)
                    pe.wait_ge(stick_raw, SH)
                if w >= 5:
                    pe.wait_ge(y_scaled, w - 4)
                for k in range(KD):
                    wv = piece(6 + k // 4)[0]
                    ins = mm(banks[:, w % 5, :], mixT[:, k, t * P:(t + 1) * P],
                             wv[:, k % 4, half * 512:(half + 1) * 512], start=(k == 0), stop=(k == KD - 1))
                ins.then_inc(y_done, 1)

            def rows_T(t):
                pe.wait_ge(xnb_ready, t + 1)
                if t >= 1:
                    pe.wait_ge(x2T_ready, t)
                for k in range(KD):
                    ins = nc.tensor.transpose(banks[:, 6 + k // 4, (k % 4) * P:(k % 4 + 1) * P],
                                              xnb[:, t % 2, k * P:(k + 1) * P], ident)
                ins.then_inc(fT_done, 1)

            def logits(t):
                pe.wait_ge(x2T_ready, t + 1)
                for k in range(KD):
                    mm(banks[:, 5, t * NR:(t + 1) * NR], x2T[:, t % 2, k * P:(k + 1) * P], wrA[:, k, :],
                       start=(t == 0 and k == 0), stop=False, skip_group_check=True)
                mm(banks[:, 5, t * NR:(t + 1) * NR], ones[0:1, :], router_row[0:1, 1, :], start=False, stop=True,
                   skip_group_check=True).then_inc(logits_done, 1)

            pe.wait_ge(wrA_ready, 1)
            for w in range(4):
                out_proj(w)
            rows_T(0)
            out_proj(4)
            out_proj(5)
            rows_T(1)
            logits(0)
            out_proj(6)
            out_proj(7)
            rows_T(2)
            logits(1)
            rows_T(3)
            logits(2)
            logits(3)

            pe.wait_ge(masks_ready, 1)
            for t in range(NT):
                for j in range(t + 1):
                    mm(banks[:, 0, t * E:(t + 1) * E], tri_bf[:] if j == t else ones_bf[:], masks[:, 2, j, :],
                       start=(t == 0), stop=(j == t), skip_group_check=True)
            for j in range(NT):
                ins = mm(banks[:, 0, NT * E:NT * E + E], ones_bf[:], masks[:, 2, j, :], start=False, stop=(j == NT - 1),
                         skip_group_check=True)
            ins.then_inc(rank_done, 1)
            pe.wait_ge(onehot_ready, 1)
            for n in range(2 * NT):
                ins = mm(banks[:, 1, 0:NCOL], onehot[:, n, :], rt[:, n * NCOL:(n + 1) * NCOL],
                         start=(n == 0), stop=(n == 2 * NT - 1))
            ins.then_inc(table_done, 1)

            def expert_T(first_wait, arrived, r):
                pe.wait_ge(arrived[0], arrived[1])
                if first_wait is not None:
                    pe.wait_ge(he_mul, first_wait)
                for k in range(KD):
                    ins = nc.tensor.transpose(banks[:, k // 4, (k % 4) * P:(k % 4 + 1) * P],
                                              rows[:, r, k * P:(k + 1) * P], ident)
                ins.then_inc(eT_done, 1)

            def expert_h(n_h, n_pairs, s, r, half):
                pe.wait_ge(heT_ready, n_pairs)
                if n_h is not None:
                    pe.wait_ge(ge_ready, n_h)
                first = True
                for which, ws in enumerate((w1s[s], w3s[s])):
                    for fc in range(FC):
                        o = which * P + fc * C
                        for k in range(KD):
                            ins = mm(banks[:, 2 + half, o:o + C], ws[:, k, fc * P:(fc + 1) * P],
                                     heT[:, r, k * P + half * C:k * P + (half + 1) * C],
                                     start=first, stop=(k == KD - 1), skip_group_check=True)
                            first = False
                ins.then_inc(h_done, 1)

            def expert_y(n_e, n_free, s, r, half):
                pe.wait_ge(ge_ready, n_e)
                if n_free is not None:
                    pe.wait_ge(ysb_ready, n_free)
                for col in range(2):
                    for fc in range(FC):
                        ins = mm(banks[half * C:(half + 1) * C, 4 + 2 * r + col, :], geT[:, half, fc * C:(fc + 1) * C],
                                 w2s[s][:, fc, col * 512:(col + 1) * 512], start=(fc == 0), stop=(fc == FC - 1))
                ins.then_inc(ye_done, 1)

            def pair(q, r, weights, h_free, y_free, next_rows):
                for half in range(2):
                    slot, value = weights[half]
                    pe.wait_ge(w_in_slot[slot], value)
                    expert_h(q * 2 + (half - 1) if h_free else None, q + 1, slot, r, half)
                    if half == 0 and next_rows is not None:
                        expert_T(q + 1, next_rows, 1 - r)
                for half in range(2):
                    expert_y(q * 2 + (half + 1), q - 1 if y_free and not half else None, weights[half][0], r, half)

            def ring(a, it):
                return [(2 + 2 * a + half, it * 48 + 48) for half in range(2)]

            expert_T(None, (rows_in[0], 16), 0)
            pair(0, 0, [(0, 48), (1, 48)], False, False, (rows_in[1], 16))
            pair(1, 1, ring(0, 0), True, False, (rows_in[0], 32))
            pair(2, 0, ring(1, 0), True, True, (rows_in[1], 32))
            with pe.Fori(1, NQ // 2 - 1) as it:
                pair(it * 2 + 1, 1, ring(0, it), True, True, (rows_in[0], it * 16 + 32))
                pair(it * 2 + 2, 0, ring(1, it), True, True, (rows_in[1], it * 16 + 32))
            pair(NQ - 1, 1, ring(0, NQ // 2 - 1), True, True, None)
            pe.wait_ge(plan_ready, 1)
            nq = pe.value_load(plan[0:1, 2 * NQOV:2 * NQOV + 1], min_val=0, max_val=NQOV)
            with pe.If(nq > 0):
                with pe.Fori(0, nq) as m:
                    expert_T(m + NQ, (rows_in[0], m * 16 + 16 * (NQ // 2 + 1)), 0)
                    pair(m + NQ, 0, ring(0, m + NQ // 2), True, True, None)


_INS = ["x", "c", "w_ada", "b_ada", "g_attn", "w_in", "q_norm_g", "k_norm_g", "lambda_q1", "lambda_k1",
        "lambda_q2", "lambda_k2", "diff_out_g", "sb_out_g", "w_out", "g_ffn", "w_group", "b_group",
        "w_erouter", "b_expert", "w1", "w3", "w2"]


def kernel(**inputs):
    import numpy as _np
    import concourse.bacc as _bacc
    from concourse import mybir as _mybir
    from concourse.bass_utils import run_bass_kernel_spmd as _run

    nc = _bacc.Bacc("TRN2", target_bir_lowering=False, num_devices=1)
    arrays, args = {}, []
    for name in _INS:
        a = _np.ascontiguousarray(inputs[name])
        arrays[f"in_{name}_dram"] = a
        args.append(nc.dram_tensor(f"in_{name}_dram", a.shape, _mybir.dt.from_np(a.dtype), kind="ExternalInput").ap())
    args.append(nc.dram_tensor("out_0_dram", (1, T, D), _mybir.dt.float32, kind="ExternalOutput").ap())
    hymba_block(nc, *args)
    r = _run(nc, [arrays], core_ids=[0])
    return r.results[0]["out_0_dram"]
```

```python
from contextlib import ExitStack

import concourse.bass as bass
from concourse import mybir

F32 = mybir.dt.float32
F32R = mybir.dt.float32r
BF16 = mybir.dt.bfloat16
I32 = mybir.dt.int32
ALU = mybir.AluOpType
ACT = mybir.ActivationFunctionType
X = mybir.AxisListType.X

P = 128
T = 512
D = 1024
NT = T // P
KD = D // P
HD = 64
DH = 4
SH = 8
G = 4
EG = 8
E = G * EG
F = 256
FC = F // P
NR = G + G * EG
C = 64
MAXOV = 2 * T // (C + 1)
NQ = E // 2
NQOV = (MAXOV + 1) // 2
NCOL = NQ + NQOV
R = 3
SKIP = 60000
EPS = 1e-6
LAMBDA_INIT = 0.2

ZOFF = {0: 0, 1: 512, 3: 896, 2: 1024}
ZCOLS = 1280
XT_BANK = (2, 3, 4, 5, 6, 7, 1, 2)


def plan_jobs():
    head = [("qk", n) for n in range(8)] + [("v", t, 0) for t in range(NT)] + [("gate", 0, 0), ("gate", 0, 1)]
    steps = {s: [] for s in range(20)}
    halves = [(job, part) for job in [("sq", n) for n in range(4)] + [("sk", n) for n in range(4)]
              + [("v", n, 1) for n in range(NT)] for part in range(2)]
    for s in range(16):
        for _ in range(2 if s < 8 else 1):
            steps[s].append(halves.pop(0))
    steps[3].append((("col", 2), None))
    steps[7].append((("col", 3), None))
    steps[9] += [(("gate", 1, 0), None), (("shift_router",), None)]
    steps[11].append((("gate", 1, 1), None))
    ended = {s: [job for job, part in steps[s] if part != 0] for s in range(20)}
    order = head + [job for s in range(20) for job in ended[s]]
    return head, steps, ended, {j: n for n, j in enumerate(order)}


SHIFT_A, SCALE_A, GATE_A, SHIFT_F, SCALE_F, GATE_F = range(6)


DIFF_STEPS, STICK_0 = NT * DH + 2, NT * DH
STEPS = STICK_0 + SH + 4


def fin_step(f):
    return 4 * f + 5 if f < DH else STICK_0 + 2 * (f - DH) + 3


def plan_transposes():
    order = []
    for s in range(STEPS):
        if 1 <= s <= NT * DH:
            order.append(("unit", s - 1))
        order += [("fin", f) for f in range(2 * DH) if s == fin_step(f) + 2]
    return order, {w: n for n, w in enumerate(order)}


def plan_releases(job_no):
    freed, count = {}, [0, 0]
    for job, n in sorted(job_no.items(), key=lambda kv: kv[1]):
        if job[0] == "qk":
            freed[job] = ("qk", job[1] + 1)
            continue
        count[n % 2] += 1
        freed[job] = (n % 2, count[n % 2])
    return freed


def hymba_block(nc, x, c, w_ada, b_ada, g_attn, w_in, q_norm_g, k_norm_g, lambda_q1, lambda_k1,
                lambda_q2, lambda_k2, diff_out_g, sb_out_g, w_out, g_ffn, w_group, b_group,
                w_erouter, b_expert, w1, w3, w2, out):
    head_jobs, step_parts, step_jobs, job_no = plan_jobs()
    job_at = {n: job for job, n in job_no.items()}
    T_order, T_no = plan_transposes()
    freed = plan_releases(job_no)

    xn_dram = nc.dram_tensor("xn_rows", (T, D), F32, kind="Internal").ap()
    y_dram = nc.dram_tensor("pair_rows", (2 * T, D), F32, kind="Internal").ap()

    with ExitStack() as ctx:
        def sb(name, shape, dt=F32):
            return ctx.enter_context(nc.sbuf_tensor(name, shape, dt))

        placed = {}

        def placed_sb(name, shape):
            placed[name] = (nc.sbuf_base + 31) // 32 * 32
            return sb(name, shape)

        def rounded(name, shape, over, column=0):
            return nc.alloc_sbuf_tensor_at(name, shape, F32R, offset=placed[over] + 4 * column)

        def sem(name):
            return ctx.enter_context(nc.semaphore(name))

        xr = sb("xr", [P, NT, D])
        stage = placed_sb("stage", [P, 3, 4096])
        hT = sb("hT", [P, KD, T])
        qkT = placed_sb("qkT", [P, 16, T])
        val = sb("val", [P, NT, 1024])
        mixT = placed_sb("mixT", [P, KD, T])
        gates = sb("gates", [P, 2, D])
        alibi = sb("alibi", [P, DH, T])
        work = placed_sb("work", [P, 8192])
        obuf = placed_sb("obuf", [P, 4, T])
        consts = sb("consts", [P, 6, P])
        wr = sb("wr", [P, KD, NR])
        wrA = sb("wrA", [P, KD, NR])
        small = sb("small", [P, 296])
        router_row = sb("router_row", [1, 2, NR])
        tri_bf = sb("tri_bf", [P, P], BF16)
        ones_bf = sb("ones_bf", [P, P], BF16)
        tables = sb("tables", [P, 2, NCOL], I32)
        ints = sb("ints", [P, 96], I32)
        plan = sb("plan", [1, 2 * NQOV + 2], I32)

        hT_hi = rounded("hT_hi", [P, KD, T], "qkT", 8 * T)
        hT_lo_parts = [rounded("hT_lo0", [P, 4, T], "mixT"), rounded("hT_lo1", [P, 4, T], "obuf")]
        w_hi = rounded("w_hi", [P, KD, 512], "work", 4096)
        w_lo_parts = rounded("w_lo", [P, 2, 4096], "stage")

        def hT_lo(k):
            return hT_lo_parts[k // 4][:, k % 4, :]

        ident, negtri, negones, ones, halves, slot_iota = (consts[:, n, :] for n in range(6))
        acc = mixT[:, 4:8, :].rearrange("p (v a) t -> p v (a t)", v=2)
        xn = qkT[:, 0:8, :].rearrange("p (t a) c -> p t (a c)", t=NT)
        prob = work[:, 0:2048].rearrange("p (r m k) -> p r m k", r=2, m=2)
        probT = work[:, 2048:3072].rearrange("p (r k) -> p r k", r=2)
        sqb = work[:, 3072:4096].rearrange("p (r k) -> p r k", r=2)
        rqk = work[:, 0:1024].rearrange("p (r k) -> p r k", r=2)
        soft = work[:, 3072:3072 + 2 * ZCOLS].rearrange("p (r k) -> p r k", r=2)
        stick = work[:, 5632:5632 + 2 * ZCOLS].rearrange("p (r k) -> p r k", r=2)
        xnb = work[:, 0:2048].rearrange("p (r k) -> p r k", r=2)
        x2T = work[:, 2048:4096].rearrange("p (r k) -> p r k", r=2)
        onehot = work[:, 2048:3072].rearrange("p (c s) -> p c s", c=2 * NT)
        rows = work[:, 4096:6144].rearrange("p (r k) -> p r k", r=2)
        heT = work[:, 0:2048].rearrange("p (r k) -> p r k", r=2)
        ysb = work[:, 2048:4096].rearrange("p (r k) -> p r k", r=2)
        gact, ge_act = work[:, 6144:6144 + F], work[:, 6144 + F:6144 + 2 * F]
        rt = work[:, 6656:8192]
        geT = rt[:, 0:FC * P]
        hT_f = hT[:].rearrange("p a b -> p (a b)")
        qk_f = qkT[:].rearrange("p a b -> p (a b)")
        val_f = val[:].rearrange("p a b -> p (a b)")
        mix_f = mixT[:].rearrange("p a b -> p (a b)")
        slots = [
            (hT_f[:, 0:2048], hT_f[:, 2048:4096], stage[:, 2, 0:2048]),
            (qk_f[:, 0:2048], qk_f[:, 2048:4096], qk_f[:, 4096:6144]),
            (qk_f[:, 6144:8192], val_f[:, 0:2048], val_f[:, 2048:4096]),
            (stage[:, 0, 0:2048], stage[:, 0, 2048:4096], stage[:, 1, 0:2048]),
            (mix_f[:, 0:2048], mix_f[:, 2048:4096], stage[:, 1, 2048:4096]),
            (alibi[:].rearrange("p a b -> p (a b)"), obuf[:].rearrange("p a b -> p (a b)"), stage[:, 2, 2048:4096]),
        ]
        w1s = [s[0].rearrange("p (k f) -> p k f", k=KD) for s in slots]
        w3s = [s[1].rearrange("p (k f) -> p k f", k=KD) for s in slots]
        w2s = [s[2].rearrange("p (f n) -> p f n", f=FC) for s in slots]

        ramp = work[:, 1280:1792].bitcast(I32)
        lam_in = work[:, 1024:1280].rearrange("p (v d) -> p v d", v=4)
        masks = rt[:, 1200:1392].bitcast(BF16).rearrange("p (k t e) -> p k t e", k=3, t=NT)
        exp_g = rt[:, 1400:1416]
        exp_d = rt[:, 1416:1420]

        def fin_pair(t):
            n = t * 2048
            return stage[:].rearrange("p a b -> p (a b)")[:, n:n + 2048].rearrange("p (k n) -> p k n", k=2)

        at = [0]

        def cols(n):
            at[0] += n
            return small[:, at[0] - n:at[0]]

        c_col, cs = cols(8), cols(8)
        b_col = cols(32).rearrange("p (v k) -> p v k", v=4)
        g_col = cols(16).rearrange("p (v k) -> p v k", v=2)
        mod = cols(32).rearrange("p (v k) -> p v k", v=4)
        gqk, out_g = cols(2), cols(2)
        eps = cols(1)
        ssx, rx, ss2, r2 = cols(4), cols(4), cols(4), cols(4)
        lam, neglam = cols(4), cols(1)
        mx, nmx, lsum, rl = (cols(4).rearrange("p (r m) -> p r m", r=2) for _ in range(4))
        sso, ro = cols(16).rearrange("p (r k) -> p r k", r=2), cols(16).rearrange("p (r k) -> p r k", r=2)
        wpair = cols(8).rearrange("p (k t) -> p k t", k=2)
        rev = cols(8)
        e64 = cols(32)
        zero32 = cols(32)
        pair_id = cols(8)
        b_iota = cols(2 * NQOV)
        assert at[0] <= 296

        banks = ctx.enter_context(nc.psum_tensor("banks", [P, 8, 512], F32))
        zps = [banks[:, 3 * r:3 * r + 3, :].rearrange("p b k -> p (b k)") for r in range(2)]

        x_in, c_in, params_in, gate_bias_in = sem("x_in"), sem("c_in"), sem("params_in"), sem("gate_bias_in")
        first_in = [sem(f"first_in{n}") for n in range(8)]
        mod_params_in = sem("mod_params_in")
        piece_in = [sem("piece_in0"), sem("piece_in1")]
        quarter_in = [sem("quarter_in0"), sem("quarter_in1")]
        scale_used = sem("scale_used")
        consts_ready, memset_ready = sem("consts_ready"), sem("memset_ready")
        silu_c, shift_used, ada_used = sem("silu_c"), sem("shift_used"), sem("ada_used")
        col_a, mod_a = sem("col_a"), sem("mod_a")
        xn_ready, xT_done = sem("xn_ready"), sem("xT_done")
        hT_raw, hT_hi_ready, hT_lo_dve, hT_lo_pool = (sem(n) for n in ("hT_raw", "hT_hi_ready", "hT_lo_dve", "hT_lo_pool"))
        w_hi_ready, w_split = sem("w_hi_ready"), sem("w_split")
        job_done = sem("job_done")
        bank_free = [sem("bank_free0"), sem("bank_free1")]
        qk_raw, sq_ready, norm_done, rqk_ready = sem("qk_raw"), sem("sq_ready"), sem("norm_done"), sem("rqk_ready")
        qk_dve = sem("qk_dve")
        alibi_ready, lam_ready = sem("alibi_ready"), sem("lam_ready")
        score_done, max_ready, exp_ready, prob_ready = (sem(n) for n in (
            "score_done", "max_ready", "exp_ready", "prob_ready"))
        T_done, probT_ready, pv_done = sem("T_done"), sem("probT_ready"), sem("pv_done")
        o_copied, o_sums, o_rstd, o_ready, mix_ready = (sem(n) for n in (
            "o_copied", "o_sums", "o_rstd", "o_ready", "mix_ready"))
        z_done, ln_ready, soft_raw, soft_ready, tri_done, stick_raw, stick_ready, spv_done = (sem(n) for n in (
            "z_done", "ln_ready", "soft_raw", "soft_ready", "tri_done", "stick_raw", "stick_ready", "spv_done"))
        y_done, y_scaled, x2_ready = sem("y_done"), sem("y_scaled"), sem("x2_ready")
        xnb_ready, xn_stored, fT_done, x2T_ready, logits_done = (sem(n) for n in (
            "xnb_ready", "xn_stored", "fT_done", "x2T_ready", "logits_done"))
        wrA_ready = sem("wrA_ready")
        g_exp_in, g_exp, d_in, d_exp = sem("g_exp_in"), sem("g_exp"), sem("d_in"), sem("d_exp")
        masks_ready, rank_done, onehot_ready, table_done, table_ready = (sem(n) for n in (
            "masks_ready", "rank_done", "onehot_ready", "table_done", "table_ready"))
        plan_ready = sem("plan_ready")
        w1_in, w3_in, w2_in = ([sem(f"w{k}_in{n}") for n in range(R)] for k in (1, 3, 2))
        rows_in = [sem("rows_in0"), sem("rows_in1")]
        rows_zero = sem("rows_zero")
        h1_done = sem("h1_done")
        eT_done, he_mul, heT_ready, h_done, silu_ready, ge_ready, geT_done, geT_ready, ye_done, ysb_ready = (
            sem(n) for n in ("eT_done", "he_mul", "heT_ready", "h_done", "silu_ready", "ge_ready", "geT_done",
                             "geT_ready", "ye_done", "ysb_ready"))
        y_stored = [sem("y_stored0"), sem("y_stored1")]
        pairs_in = [sem(f"pairs_in{n}") for n in range(NT)]
        fin_a, fin_b, fin_c, out_stored = sem("fin_a"), sem("fin_b"), sem("fin_c"), sem("out_stored")
        eps_ready, consts_dve, lam_exp = sem("eps_ready"), sem("consts_dve"), sem("lam_exp")
        act_chain, dve_chain, pool_chain = sem("act_chain"), sem("dve_chain"), sem("pool_chain")

        x_rows = x.rearrange("b (t p) d -> (b p) t d", p=P)
        out_rows = out.rearrange("b (t p) d -> (b p) t d", p=P)
        ada_v = w_ada.rearrange("l (p k) n -> (l p) k n", k=KD)
        in_v = w_in.rearrange("l (p k) n -> (l p) k n", k=KD)
        out_v = w_out.rearrange("l (k p) n -> (l p) k n", p=P)
        w1_v = w1.rearrange("l g e (p k) f -> (l g e) p (k f)", k=KD)
        w3_v = w3.rearrange("l g e (p k) f -> (l g e) p (k f)", k=KD)
        w2_v = w2.rearrange("l g e (f p) n -> (l g e) p f n", p=P)
        b_cols_v = b_ada.rearrange("l (v p k) -> (l p) v k", v=6, k=KD)
        w2_dst = [s[2].rearrange("p (f n) -> p f n", f=FC) for s in slots]

        def piece(n):
            w = stage[:, n % 2, :].rearrange("p (k n) -> p k n", k=KD if n < 6 else 4)
            return w, piece_in[n % 2], 16 * (n // 2 + 1)

        def quarter(v, i):
            n = 4 * (v - 2) + i
            w = stage[:, 2, (n % 2) * 2048:(n % 2 + 1) * 2048].rearrange("p (k n) -> p k n", k=2)
            return n, w, quarter_in[n % 2], 16 * (n // 2 + 1)

        shift_w = [val_f.rearrange("p (k n) -> p k n", k=4),
                   qk_f[:, 4096:8192].rearrange("p (k n) -> p k n", k=4)]
        scale_w = [stage[:, 2, :].rearrange("p (k n) -> p k n", k=4),
                   stage[:, 1, :].rearrange("p (k n) -> p k n", k=4)]

        def row(v):
            return v.rearrange("l n -> (l n)").partition_broadcast(P)

        params = [
            (b_col[:, 2:4, :], b_cols_v[:, SHIFT_F:SCALE_F + 1, :]),
            (g_col[:, 1, :], g_ffn.rearrange("l (p k) -> (l p) k", k=KD)),
            (out_g[:, 0:1], diff_out_g.rearrange("l (p o) -> (l p) o", o=1)),
            (wr[:, :, 0:G], w_group.rearrange("l (p k) g -> (l p) k g", k=KD)),
            (router_row[0:1, 0, 0:G], b_group),
            (router_row[0:1, 0, G:NR], b_expert.rearrange("l g e -> l (g e)")),
        ]
        for g in range(G):
            params.append((wr[:, :, G + g * EG:G + (g + 1) * EG], w_erouter[:, g].rearrange("l (p k) e -> (l p) k e", k=KD)))
        for n, v in enumerate((lambda_q1, lambda_k1, lambda_q2, lambda_k2)):
            params.append((lam_in[:, n, :], row(v)))
        for m in range(2):
            part = slice(m * HD, (m + 1) * HD)
            params.append((gqk[part, 0:1], q_norm_g.rearrange("l (p o) -> (l p) o", o=1)))
            params.append((gqk[part, 1:2], k_norm_g.rearrange("l (p o) -> (l p) o", o=1)))
            params.append((out_g[part, 1:2], sb_out_g.rearrange("l (p o) -> (l p) o", o=1)))
        N_PARAMS = len(params)

        def split_chunk(n):
            raw, arrived, value = piece(n // 4)
            lo = w_lo_parts[:, (n // 4) % 2, :].rearrange("p (k n) -> p k n", k=KD)
            part = slice((n % 4) * P, (n % 4 + 1) * P)
            return raw[:, :, part], w_hi[:, :, part], lo[:, :, part], arrived, value

        IN_LAST = {0: ("qk", 3), 1: ("qk", 7), 2: ("v", 3, 0), 3: ("sq", 3), 4: ("sk", 3), 5: ("v", 3, 1)}

        block = ctx.enter_context(nc.Block())

        @block.sync
        def _(sp):
            def ada_quarter(dst, v, i):
                sp.dma_start(dst[i // 2][:, 2 * (i % 2):2 * (i % 2) + 2, :],
                             ada_v[:, 2 * i:2 * i + 2, v * D:(v + 1) * D]).then_inc(first_in[4 * v + i], 16)

            sp.wait_ge(c_in, 16)
            for i in range(4):
                ada_quarter(shift_w, SHIFT_A, i)
            sp.dma_start(xr[:], x_rows).then_inc(x_in, 16)
            for i in range(4):
                ada_quarter(scale_w, SCALE_A, i)
            for n in range(8):
                if n == 1:
                    sp.wait_ge(scale_used, KD)
                if n >= 2:
                    sp.wait_ge(job_done, job_no[IN_LAST[n - 2]] + 1)
                dst, arrived, _ = piece(n)
                src = in_v[:, :, n * 512:(n + 1) * 512] if n < 6 else out_v[:, 4 * (n - 6):4 * (n - 6) + 4, :]
                sp.dma_start(dst, src).then_inc(arrived, 16)

            def load_expert(e, s):
                sp.dma_start(slots[s][0], w1_v[e]).then_inc(w1_in[s // 2], 16)
                sp.dma_start(slots[s][1], w3_v[e]).then_inc(w3_in[s // 2], 16)
                sp.dma_start(w2_dst[s], w2_v[e]).then_inc(w2_in[s // 2], 16)

            def load_pair(e0, e1, place, up_free, down_free):
                sp.wait_ge(h1_done, up_free)
                sp.dma_start(slots[2 * place][0], w1_v[e0]).then_inc(w1_in[place], 16)
                sp.dma_start(slots[2 * place + 1][0], w1_v[e1]).then_inc(w1_in[place], 16)
                sp.wait_ge(h_done, up_free)
                sp.dma_start(slots[2 * place][1], w3_v[e0]).then_inc(w3_in[place], 16)
                sp.dma_start(slots[2 * place + 1][1], w3_v[e1]).then_inc(w3_in[place], 16)
                sp.wait_ge(ye_done, down_free)
                sp.dma_start(w2_dst[2 * place], w2_v[e0]).then_inc(w2_in[place], 16)
                sp.dma_start(w2_dst[2 * place + 1], w2_v[e1]).then_inc(w2_in[place], 16)

            sp.wait_ge(job_done, job_no[("v", 3, 1)] + 1)
            sp.wait_ge(ada_used, 16)
            load_expert(0, 0)
            sp.wait_ge(spv_done, SH)
            load_expert(1, 1)
            load_expert(2, 2)
            sp.wait_ge(max_ready, NT * DH)
            sp.dma_start(slots[5][0], w1_v[5]).then_inc(w1_in[2], 16)
            sp.dma_start(w2_dst[5], w2_v[5]).then_inc(w2_in[2], 16)
            sp.wait_ge(y_done, 2 * NT)
            load_expert(3, 3)
            load_expert(4, 4)
            sp.wait_ge(xnb_ready, NT)
            sp.wait_ge(xn_stored, 16 * NT)
            sp.dma_start(slots[5][1], w3_v[5]).then_inc(w3_in[2], 16)
            with sp.Fori(0, NQ // R - 1) as it:
                for n in range(R):
                    e = it * (2 * R) + 2 * (n + R)
                    load_pair(e, e + 1, n, it * R + (n + 1), it * R + (n + 1))
            for q in range(NQ // R * R, NQ):
                load_pair(2 * q, 2 * q + 1, q % R, q - R + 1, q - R + 1)
            sp.wait_ge(plan_ready, 1)
            nq = sp.value_load(plan[0:1, 2 * NQOV:2 * NQOV + 1], min_val=0, max_val=NQOV)
            with sp.If(nq > 0):
                with sp.Fori(0, nq) as m:
                    e0, e1 = (sp.value_load(plan[0:1, bass.ds(m * 2 + n, 1)], min_val=0, max_val=E - 1) for n in range(2))
                    load_pair(e0, e1, 1, m + NQ, m + NQ)
            sp.wait_ge(y_stored[1], 16 * (NQ // 2))
            sp.wait_ge(y_stored[0], nq * 16 + 16 * (NQ // 2))
            for t in range(NT):
                dst = fin_pair(t)
                sp.dma_start(dst, y_dram.rearrange("(k t p) n -> t p k n", k=2, p=P)[t]).then_inc(pairs_in[t], 16)
            for t in range(NT):
                sp.wait_ge(fin_c, t + 1)
                sp.dma_start(out_rows[:, t, :], xr[:, t, :]).then_inc(out_stored, 16)
            sp.wait_ge(out_stored, 16 * NT)
            sp.wait_ge(xn_stored, 16 * NT)

        @block.gpsimd
        def _(pool):
            chain = [0]

            def link(ins):
                chain[0] += 1
                ins.then_inc(pool_chain, 1)
                pool.wait_ge(pool_chain, chain[0])

            g = nc.gpsimd
            link(g.memset(consts[:, 0, :], 1.0))
            g.affine_select(out=ident, in_=ident, pattern=[[-1, P]], compare_op=ALU.is_equal, fill=0.0,
                            base=0, channel_multiplier=1).then_inc(consts_ready, 1)
            link(g.memset(negtri, -1.0))
            g.affine_select(out=negtri, in_=negtri, pattern=[[-1, P]], compare_op=ALU.is_ge, fill=0.0,
                            base=0, channel_multiplier=1).then_inc(consts_ready, 1)
            g.memset(negones, -1.0).then_inc(consts_ready, 1)
            link(g.memset(tri_bf[:], 1.0))
            g.affine_select(out=tri_bf[:], in_=tri_bf[:], pattern=[[1, P]], compare_op=ALU.is_gt, fill=0.0,
                            base=0, channel_multiplier=-1).then_inc(consts_ready, 1)
            link(g.iota(ramp, pattern=[[-1, T]], base=3 * P, channel_multiplier=1))
            for h in range(DH):
                slope = 2.0 ** (-8.0 * (h + 1) / DH)
                link(g.tensor_scalar(alibi[:, h, :], ramp, -slope, None, ALU.mult))
                g.affine_select(out=alibi[:, h, :], in_=alibi[:, h, :], pattern=[[-1, T]], compare_op=ALU.is_ge,
                                fill=-1e30, base=3 * P, channel_multiplier=1).then_inc(alibi_ready, 1)
            link(g.iota(ramp[:, 0:P], pattern=[[1, P]], base=0, channel_multiplier=0))
            g.tensor_copy(slot_iota, ramp[:, 0:P]).then_inc(memset_ready, 1)
            link(g.iota(ints[:, 0:32], pattern=[[C, E]], base=0, channel_multiplier=0))
            g.tensor_copy(e64, ints[:, 0:32]).then_inc(memset_ready, 1)
            link(g.iota(ints[:, 32:32 + 2 * NQOV], pattern=[[1, 2 * NQOV]], base=0, channel_multiplier=0))
            g.tensor_copy(b_iota, ints[:, 32:32 + 2 * NQOV]).then_inc(memset_ready, 1)
            link(g.iota(ints[:, 72:80], pattern=[[-1, 8]], base=8, channel_multiplier=0))
            g.tensor_copy(rev, ints[:, 72:80]).then_inc(memset_ready, 1)
            link(g.iota(ints[:, 48:56], pattern=[[T, 2], [P, NT]], base=1, channel_multiplier=1))
            g.tensor_copy(pair_id, ints[:, 48:56]).then_inc(memset_ready, 1)

            for n, v in enumerate((GATE_A, GATE_F)):
                g.dma_start(gates[:, n, :], row(b_ada[:, v * D:(v + 1) * D])).then_inc(gate_bias_in, 16)
            for v in range(GATE_A, GATE_F + 1):
                for i in range(4):
                    n, dst, arrived, _ = quarter(v, i)
                    if n == 0:
                        pool.wait_ge(scale_used, KD // 2)
                    if n == 2:
                        for k in range(1, KD, 2):
                            pool.wait_ge(hT_hi_ready, k + 1)
                            g.tensor_tensor(hT_lo(k), hT[:, k, :], hT_hi[:, k, :].bitcast(F32),
                                            ALU.subtract).then_inc(hT_lo_pool, 1)
                    if n >= 2:
                        pool.wait_ge(ada_used, n - 1)
                    g.dma_start(dst, ada_v[:, 2 * i:2 * i + 2, v * D:(v + 1) * D]).then_inc(arrived, 16)

            def mask_tiles(v, r, ready):
                v0 = v[:, r, :]
                a = v0[:, 0:1024].rearrange("p (b k) -> p b k", b=2)[:, :, 0:P]
                g.affine_select(out=a, in_=a, pattern=[[0, 2], [1, P]], compare_op=ALU.is_gt, fill=0.0,
                                base=0, channel_multiplier=-1)
                a = v0[:, 896:1152].rearrange("p (b k) -> p b k", b=2)
                g.affine_select(out=a, in_=a, pattern=[[0, 2], [1, P]], compare_op=ALU.is_gt, fill=0.0,
                                base=0, channel_multiplier=-1).then_inc(ready, 1)

            for n in range(SH + 1):
                if n < SH:
                    pool.wait_ge(soft_raw, n + 1)
                    mask_tiles(soft, n % 2, soft_ready)
                if n >= 1:
                    pool.wait_ge(stick_raw, n)
                    mask_tiles(stick, (n - 1) % 2, stick_ready)

            for w in range(2 * NT - 1):
                pool.wait_ge(y_scaled, w + 1)
                xh = xr[:, w // 2, (w % 2) * 512:(w % 2) * 512 + 512]
                g.tensor_tensor(xh, xh, obuf[:, w % 2, :], ALU.add).then_inc(x2_ready, 1)
            g.memset(rows, 0.0).then_inc(rows_zero, 1)
            pool.wait_ge(table_ready, 1)
            pool.wait_ge(xn_stored, 16 * NT)
            pool.wait_ge(rows_zero, 1)

            def gather(q, r):
                g.indirect_dma_start(rows[:, r, :], None, xn_dram,
                                     bass.IndirectOffsetOnAxis(ap=tables[:, 0, q:q + 1], axis=0),
                                     bounds_check=T - 1, oob_is_err=False).then_inc(rows_in[r], 16)

            def scatter(q, r):
                g.indirect_dma_start(y_dram, bass.IndirectOffsetOnAxis(ap=tables[:, 1, q:q + 1], axis=0),
                                     ysb[:, r, :], None,
                                     bounds_check=2 * T - 1, oob_is_err=False).then_inc(y_stored[r], 16)

            gather(0, 0)
            gather(1, 1)
            pool.wait_ge(eT_done, 1)
            gather(2, 0)
            for q in range(NQ):
                if q + 3 < NQ:
                    pool.wait_ge(eT_done, q + 2)
                    gather(q + 3, (q + 3) % 2)
                pool.wait_ge(ysb_ready, q + 1)
                scatter(q, q % 2)
            pool.wait_ge(plan_ready, 1)
            nq = pool.value_load(plan[0:1, 2 * NQOV:2 * NQOV + 1], min_val=0, max_val=NQOV)
            for m in range(NQOV):
                with pool.If(nq > m):
                    pool.wait_ge(y_stored[0], 16 * (NQ // 2 + m))
                    gather(NQ + m, 0)
                    pool.wait_ge(ysb_ready, NQ + m + 1)
                    scatter(NQ + m, 0)

        @block.scalar
        def _(act):
            chain = [0]

            def link(ins):
                chain[0] += 1
                ins.then_inc(act_chain, 1)
                act.wait_ge(act_chain, chain[0])

            a = nc.scalar
            act.dma_start(c_col, c.rearrange("b (p k) -> (b p) k", k=KD)).then_inc(c_in, 16)
            act.dma_start(b_col[:, 0:2, :], b_cols_v[:, SHIFT_A:SCALE_A + 1, :]).then_inc(mod_params_in, 16)
            act.dma_start(g_col[:, 0, :], g_attn.rearrange("l (p k) -> (l p) k", k=KD)).then_inc(mod_params_in, 16)
            act.wait_ge(c_in, 16)
            a.activation(cs, c_col, ACT.Silu).then_inc(silu_c, 1)
            for dst, src in params:
                act.dma_start(dst, src).then_inc(params_in, 16)
            a.preload_act_table_set("natural_log_exp_and_others")
            act.wait_ge(x_in, 16)
            act.wait_ge(eps_ready, 1)
            for t in range(NT):
                link(a.activation(hT_f[:, 0:D], xr[:, t, :], ACT.Square, accum_out=ssx[:, t:t + 1]))
            link(a.activation(rx, ssx, ACT.Ln, bias=eps, scale=1.0 / D))
            link(a.activation(rx, rx, ACT.Exp, scale=-0.5))
            for t in range(NT):
                a.activation(xn[:, t, :].rearrange("p (k j) -> p k j", k=KD),
                             xr[:, t, :].rearrange("p (j k) -> p k j", k=KD), ACT.Copy,
                             scale=rx[:, t:t + 1]).then_inc(xn_ready, 1)
            act.wait_ge(mod_a, 1)
            for k in range(KD):
                act.wait_ge(xT_done, k + 1)
                a.activation(hT[:, k, :], banks[:, XT_BANK[k], :], ACT.Identity,
                             bias=mod[:, 0, k:k + 1], scale=mod[:, 1, k:k + 1]).then_inc(hT_raw, 1)

            def w_round(n):
                raw, hi, _, arrived, value = split_chunk(n)
                act.wait_ge(arrived, value)
                if n >= 4:
                    act.wait_ge(job_done, n - 3)
                a.activation(hi, raw, ACT.Copy).then_inc(w_hi_ready, 1)

            w_round(1)
            w_round(2)
            act.wait_ge(lam_ready, 1)
            a.activation(lam[:, 2:4], lam[:, 0:2], ACT.Exp).then_inc(lam_exp, 1)

            def qk_evac(n):
                act.wait_ge(job_done, n + 1)
                if n >= 2:
                    act.wait_ge(norm_done, n - 1)
                src = banks[:, job_no[("qk", n)] % 2, :]
                a.activation(sqb[:, n % 2, :], src, ACT.Square).then_inc(sq_ready, 1)
                a.activation(qkT[:, n, :], src, ACT.Copy).then_inc(qk_raw, 1)

            def qk_rstd(n):
                act.wait_ge(norm_done, n + 1)
                if n >= 2:
                    act.wait_ge(qk_dve, n - 1)
                link(a.activation(rqk[:, n % 2, :], banks[:, 2 + n % 2, :], ACT.Ln, bias=eps, scale=1.0 / HD))
                a.activation(rqk[:, n % 2, :], rqk[:, n % 2, :], ACT.Exp, scale=-0.5).then_inc(rqk_ready, 1)

            def job_evac(job):
                n = job_no[job]
                src = banks[:, n % 2, :]
                if job[0] == "v":
                    act.wait_ge(job_done, n + 1)
                    a.activation(val[:, job[1], job[2] * 512:job[2] * 512 + 512], src, ACT.Copy).then_inc(bank_free[n % 2], 1)
                elif job[0] == "sq":
                    act.wait_ge(job_done, n + 1)
                    a.activation(qkT[:, 8 + job[1], :], src, ACT.Copy, scale=HD ** -0.5).then_inc(bank_free[n % 2], 1)
                elif job[0] == "sk":
                    act.wait_ge(job_done, n + 1)
                    a.activation(qkT[:, 12 + job[1], :], src, ACT.Copy).then_inc(bank_free[n % 2], 1)

            for n in range(8):
                if n >= 1:
                    w_round(n + 2)
                if n == 7:
                    w_round(10)
                    w_round(11)
                qk_evac(n)
                if n >= 1:
                    qk_rstd(n - 1)
            qk_rstd(7)
            for job in head_jobs:
                job_evac(job)

            def exp_unit(u):
                h, i = u // NT, u % NT
                act.wait_ge(max_ready, u + 1)
                for m in range(2):
                    v = prob[:, u % 2, m, 0:(i + 1) * P]
                    ins = a.activation(v, v, ACT.Exp, bias=nmx[:, u % 2, m:m + 1], accum_out=lsum[:, u % 2, m:m + 1])
                ins.then_inc(exp_ready, 1)

            def probT_evac(u):
                i = u % NT
                act.wait_ge(T_done, T_no[("unit", u)] + 1)
                if u >= 2:
                    act.wait_ge(pv_done, u - 1)
                a.activation(probT[:, u % 2, 0:(i + 1) * P], banks[:, 6, 0:(i + 1) * P], ACT.Copy).then_inc(probT_ready, 1)

            def out_rstd(f):
                n = 4 if f < DH else 8
                act.wait_ge(o_sums, f + 1)
                link(a.activation(ro[:, f % 2, 0:n], sso[:, f % 2, 0:n], ACT.Ln, bias=eps, scale=n / 512.0))
                a.activation(ro[:, f % 2, 0:n], ro[:, f % 2, 0:n], ACT.Exp, scale=-0.5).then_inc(o_rstd, 1)

            def mix_evac(f):
                act.wait_ge(T_done, T_no[("fin", f)] + 1)
                if f == DH:
                    act.wait_ge(job_done, job_no[("gate", 1, 1)] + 1)
                a.activation(mixT[:, f, :], banks[:, 6, :], ACT.Copy,
                             scale=out_g[:, f // DH:f // DH + 1]).then_inc(mix_ready, 1)

            def softplus_parts(n):
                act.wait_ge(z_done, n + 1)
                if n >= 2:
                    act.wait_ge(tri_done, n - 1)
                v = soft[:, n % 2, :]
                link(a.activation(v, zps[n % 2][:, 0:ZCOLS], ACT.Abs))
                link(a.activation(v, v, ACT.Exp, scale=-1.0))
                a.activation(v, v, ACT.Ln, bias=1.0).then_inc(ln_ready, 1)

            def stick_exp(n):
                act.wait_ge(tri_done, n + 1)
                if n >= 2:
                    act.wait_ge(spv_done, n - 1)
                a.activation(stick[:, n % 2, :], zps[n % 2][:, 0:ZCOLS], ACT.Exp).then_inc(stick_raw, 1)

            for s in range(STEPS):
                if 1 <= s < DIFF_STEPS:
                    for job in step_jobs.get(s - 1, ()):
                        job_evac(job)
                if 1 <= s <= NT * DH:
                    probT_evac(s - 1)
                if s < NT * DH:
                    exp_unit(s)
                n = s - STICK_0
                if 0 <= n < SH:
                    softplus_parts(n)
                for f in range(DH):
                    if s == fin_step(f):
                        out_rstd(f)
                    if s == fin_step(f) + 2:
                        mix_evac(f)
                if 1 <= n <= SH:
                    stick_exp(n - 1)
                for f in range(DH, 2 * DH):
                    if s == fin_step(f):
                        out_rstd(f)
                    if s == fin_step(f) + 2:
                        mix_evac(f)

            for t in range(NT):
                act.wait_ge(x2_ready, 2 * t + 2)
                link(a.activation(obuf[:, 2:4, :].rearrange("p a b -> p (a b)"), xr[:, t, :], ACT.Square,
                                  accum_out=ss2[:, t:t + 1]))
                link(a.activation(r2[:, t:t + 1], ss2[:, t:t + 1], ACT.Ln, bias=eps, scale=1.0 / D))
                link(a.activation(r2[:, t:t + 1], r2[:, t:t + 1], ACT.Exp, scale=-0.5))
                if t >= 2:
                    act.wait_ge(xn_stored, 16 * t)
                a.activation(xnb[:, t % 2, :].rearrange("p (k j) -> p k j", k=KD),
                             xr[:, t, :].rearrange("p (j k) -> p k j", k=KD), ACT.Copy,
                             scale=r2[:, t:t + 1]).then_inc(xnb_ready, 1)
                act.wait_ge(xnb_ready, t + 1)
                act.dma_start(xn_dram[t * P:(t + 1) * P, :], xnb[:, t % 2, :]).then_inc(xn_stored, 16)
            act.wait_ge(g_exp_in, 1)
            a.activation(exp_g, exp_g, ACT.Exp).then_inc(g_exp, 1)
            act.wait_ge(d_in, 1)
            a.activation(exp_d, exp_d, ACT.Exp).then_inc(d_exp, 1)
            a.preload_act_table(ACT.Silu)

            def gate_pair(n):
                act.wait_ge(h_done, n)
                a.activation(gact, banks[:, 2, 0:F], ACT.Silu).then_inc(silu_ready, 1)
                act.wait_ge(geT_done, n)
                a.activation(geT, banks[:, 3, 0:FC * P], ACT.Copy).then_inc(geT_ready, 1)

            with act.Fori(0, NQ) as q:
                gate_pair(q + 1)
            act.wait_ge(plan_ready, 1)
            nq = act.value_load(plan[0:1, 2 * NQOV:2 * NQOV + 1], min_val=0, max_val=NQOV)
            with act.If(nq > 0):
                with act.Fori(0, nq) as m:
                    gate_pair(m + (NQ + 1))
            for t in range(NT):
                act.wait_ge(pairs_in[t], 16)
                a.activation(fin_pair(t)[:, 1, :], fin_pair(t)[:, 1, :], ACT.Copy,
                             scale=wpair[:, 1, t:t + 1]).then_inc(fin_a, 1)

        @block.vector
        def _(dve):
            chain = [0]

            def link(ins):
                chain[0] += 1
                ins.then_inc(dve_chain, 1)
                dve.wait_ge(dve_chain, chain[0])

            v = nc.vector

            def accumulate(dst, src, k, first):
                s = cs[:, k:k + 1]
                if first:
                    return v.tensor_scalar(dst, src, s, None, ALU.mult)
                return v.scalar_tensor_tensor(out=dst, in0=src, scalar=s, in1=dst, op0=ALU.mult, op1=ALU.add)

            def first_sums(v, w, used):
                for k in range(KD):
                    if k % 2 == 0:
                        dve.wait_ge(first_in[4 * v + k // 2], 16)
                    accumulate(acc[:, v, :], w[k // 4][:, k % 4, :], k, k == 0).then_inc(used, 1)
                    dve.wait_ge(used, k + 1)

            v.memset(eps, EPS).then_inc(eps_ready, 1)
            v.memset(ones, 1.0).then_inc(consts_dve, 1)
            v.memset(ones_bf[:], 1.0).then_inc(consts_dve, 1)
            v.memset(zero32, 0.0).then_inc(consts_dve, 1)
            link(v.memset(halves, 0.0))
            v.memset(halves[0:HD, 0:HD], 1.0).then_inc(consts_dve, 1)
            v.memset(halves[HD:P, HD:P], 1.0).then_inc(consts_dve, 1)
            dve.wait_ge(silu_c, 1)
            first_sums(0, shift_w, shift_used)
            first_sums(1, scale_w, scale_used)

            def ada_quarter(vec, i):
                if i == 0 and vec in (2, 3):
                    dve.wait_ge(col_a, 1)
                if i == 0 and vec == 4:
                    dve.wait_ge(job_done, job_no[("gate", 0, 1)] + 1)
                if i == 0 and vec == 5:
                    dve.wait_ge(job_done, job_no[("col", 2)] + 1)
                n, src, arrived, value = quarter(vec, i)
                dve.wait_ge(arrived, value)
                link(accumulate(acc[:, vec % 2, :], src[:, 0, :], 2 * i, i == 0))
                accumulate(acc[:, vec % 2, :], src[:, 1, :], 2 * i + 1, False).then_inc(ada_used, 1)
                dve.wait_ge(ada_used, n + 1)

            dve.wait_ge(mod_params_in, 32)
            dve.wait_ge(col_a, 1)
            v.tensor_tensor(mod[:, 0, :], banks[:, 0, 0:8], b_col[:, 0, :], ALU.add)
            link(v.tensor_tensor(mod[:, 1, :], banks[:, 0, 8:16], b_col[:, 1, :], ALU.add))
            v.scalar_tensor_tensor(out=mod[:, 1, :], in0=mod[:, 1, :], scalar=1.0, in1=g_col[:, 0, :],
                                   op0=ALU.add, op1=ALU.mult).then_inc(mod_a, 1)
            dve.wait_ge(mod_a, 1)
            def w_rest(n):
                raw, hi, lo, _, _ = split_chunk(n)
                dve.wait_ge(w_hi_ready, n)
                v.tensor_tensor(lo, raw, hi.bitcast(F32), ALU.subtract).then_inc(w_split, 1)

            for k in range(KD):
                dve.wait_ge(hT_raw, k + 1)
                v.tensor_copy(hT_hi[:, k, :], hT[:, k, :]).then_inc(hT_hi_ready, 1)
                if k % 2 == 0:
                    dve.wait_ge(hT_hi_ready, k + 1)
                    v.tensor_tensor(hT_lo(k), hT[:, k, :], hT_hi[:, k, :].bitcast(F32),
                                    ALU.subtract).then_inc(hT_lo_dve, 1)
            w_rest(1)
            dve.wait_ge(params_in, 16 * N_PARAMS)
            for m in range(2):
                ins = v.tensor_tensor_reduce(out=work[:, 2048 + m * HD:2048 + (m + 1) * HD], in0=lam_in[:, 2 * m, :], in1=lam_in[:, 2 * m + 1, :],
                                             scale=1.0, scalar=0.0, op0=ALU.mult, op1=ALU.add,
                                             accum_out=lam[:, m:m + 1])
            ins.then_inc(lam_ready, 1)
            link(v.tensor_scalar(gqk[:, 0:1], gqk[:, 0:1], HD ** -0.5, None, ALU.mult))
            link(v.tensor_scalar(out_g[:, 0:1], out_g[:, 0:1], 1.0 - LAMBDA_INIT, None, ALU.mult))
            dve.wait_ge(lam_exp, 1)
            link(v.tensor_tensor(neglam, lam[:, 3:4], lam[:, 2:3], ALU.subtract))
            link(v.tensor_scalar(neglam, neglam, -LAMBDA_INIT, None, ALU.add))

            def qk_scale(n):
                dve.wait_ge(qk_raw, n + 1)
                dve.wait_ge(rqk_ready, n + 1)
                v.scalar_tensor_tensor(out=qkT[:, n, :], in0=qkT[:, n, :], scalar=gqk[:, n // 4:n // 4 + 1],
                                       in1=rqk[:, n % 2, :], op0=ALU.mult, op1=ALU.mult).then_inc(qk_dve, 1)

            for n in range(8):
                w_rest(n + 2)
                if n == 7:
                    w_rest(10)
                    w_rest(11)
                if n >= 1:
                    qk_scale(n - 1)
                ada_quarter(GATE_A + n // 4, n % 4)
            qk_scale(7)

            def job_evac(job):
                n = job_no[job]
                src = banks[:, n % 2, :]
                if job[0] == "gate":
                    dve.wait_ge(gate_bias_in, 32)
                    dve.wait_ge(job_done, n + 1)
                    dst = gates[:, job[1], job[2] * 512:job[2] * 512 + 512]
                    v.tensor_tensor(dst, src, dst, ALU.add).then_inc(bank_free[n % 2], 1)
                elif job[0] == "col":
                    dve.wait_ge(job_done, n + 1)
                    w = job[1]
                    v.tensor_tensor(mod[:, w, :], src[:, 0:8], b_col[:, w, :], ALU.add).then_inc(bank_free[n % 2], 1)
                    dve.wait_ge(bank_free[n % 2], freed[job][1])
                    if w == 3:
                        link(v.scalar_tensor_tensor(out=mod[:, 3, :], in0=mod[:, 3, :], scalar=1.0,
                                                    in1=g_col[:, 1, :], op0=ALU.add, op1=ALU.mult))
                        v.tensor_tensor(wrA[:], wr[:], mod[:, 3, :].unsqueeze(2).to_broadcast([P, KD, NR]),
                                        ALU.mult).then_inc(wrA_ready, 1)
                elif job[0] == "shift_router":
                    dve.wait_ge(job_done, n + 1)
                    v.tensor_tensor(router_row[0:1, 1, :], src[0:1, 0:NR], router_row[0:1, 0, :],
                                    ALU.add).then_inc(bank_free[n % 2], 1)

            for job in head_jobs:
                job_evac(job)

            def max_unit(u):
                h, i = u // NT, u % NT
                if u == 0:
                    dve.wait_ge(alibi_ready, DH)
                dve.wait_ge(score_done, u + 1)
                W = (i + 1) * P
                if u >= 2:
                    dve.wait_ge(T_done, T_no[("unit", u - 2)] + 1)
                for m in range(2):
                    ins = v.tensor_tensor_reduce(out=prob[:, u % 2, m, 0:W], in0=banks[:, 2 + 2 * (u % 2) + m, 0:W],
                                                 in1=alibi[:, h, T - W:T], scale=1.0, scalar=-3e38,
                                                 op0=ALU.add, op1=ALU.max, accum_out=mx[:, u % 2, m:m + 1])
                link(ins)
                v.tensor_scalar(nmx[:, u % 2, :], mx[:, u % 2, :], -1.0, None, ALU.mult).then_inc(max_ready, 1)

            def combine_unit(u):
                i = u % NT
                W = (i + 1) * P
                dve.wait_ge(exp_ready, u + 1)
                link(v.reciprocal(rl[:, u % 2, :], lsum[:, u % 2, :]))
                link(v.tensor_scalar(rl[:, u % 2, 1:2], rl[:, u % 2, 1:2], neglam, None, ALU.mult))
                p0, p1 = prob[:, u % 2, 0, 0:W], prob[:, u % 2, 1, 0:W]
                link(v.tensor_scalar(p1, p1, rl[:, u % 2, 1:2], None, ALU.mult))
                v.scalar_tensor_tensor(out=p0, in0=p0, scalar=rl[:, u % 2, 0:1], in1=p1,
                                       op0=ALU.mult, op1=ALU.add).then_inc(prob_ready, 1)

            def out_sums(f):
                n = 4 if f < DH else 8
                if f < DH:
                    dve.wait_ge(pv_done, NT * (f + 1))
                else:
                    dve.wait_ge(spv_done, 2 * (f - DH) + 2)
                o = obuf[:, f % 2, :]
                v.tensor_copy(o, banks[:, 7, :]).then_inc(o_copied, 1)
                dve.wait_ge(o_copied, f + 1)
                if f >= 2:
                    dve.wait_ge(T_done, T_no[("fin", f - 2)] + 1)
                sq = obuf[:, 2 + f % 2, :]
                link(v.tensor_tensor(sq, o, o, ALU.mult))
                v.tensor_reduce(sso[:, f % 2, 0:n], sq.rearrange("p (g w) -> p g w", g=n), X,
                                ALU.add).then_inc(o_sums, 1)

            def out_scale(f):
                n = 4 if f < DH else 8
                dve.wait_ge(o_rstd, f + 1)
                w = 512 // n
                v.tensor_tensor(obuf[:, 2 + f % 2, :].rearrange("p (g w) -> p g w", g=n),
                                obuf[:, f % 2, :].rearrange("p (g w) -> p g w", g=n),
                                ro[:, f % 2, 0:n].unsqueeze(2).to_broadcast([P, n, w]), ALU.mult).then_inc(o_ready, 1)

            def softplus(n):
                dve.wait_ge(ln_ready, n + 1)
                v.scalar_tensor_tensor(out=soft[:, n % 2, :], in0=zps[n % 2][:, 0:ZCOLS], scalar=0.0,
                                       in1=soft[:, n % 2, :], op0=ALU.max, op1=ALU.add).then_inc(soft_raw, 1)

            for s in range(STEPS):
                if 1 <= s < DIFF_STEPS:
                    for job in step_jobs.get(s - 1, ()):
                        job_evac(job)
                if 1 <= s <= NT * DH:
                    combine_unit(s - 1)
                if s < NT * DH:
                    max_unit(s)
                if s < 8:
                    ada_quarter(SCALE_F + s // 4, s % 4)
                for f in range(DH):
                    if s == fin_step(f):
                        out_sums(f)
                    if s == fin_step(f) + 1:
                        out_scale(f)
                if 0 <= s - STICK_0 < SH:
                    softplus(s - STICK_0)
                for f in range(DH, 2 * DH):
                    if s == fin_step(f):
                        out_sums(f)
                        out_scale(f)

            def copy_x2T(t):
                dve.wait_ge(fT_done, t + 1)
                if t >= 2:
                    dve.wait_ge(logits_done, t - 1)
                v.tensor_copy(x2T[:, t % 2, :], banks[:, 6:8, :].rearrange("p b k -> p (b k)")).then_inc(x2T_ready, 1)

            for w in range(2 * NT):
                dve.wait_ge(y_done, w + 1)
                if w >= 2:
                    dve.wait_ge(x2_ready, w - 1)
                else:
                    dve.wait_ge(T_done, T_no[("fin", 7)] + 1)
                v.tensor_tensor(obuf[:, w % 2, :], banks[:, w % 5, :], gates[:, 0, (w % 2) * 512:(w % 2) * 512 + 512],
                                ALU.mult).then_inc(y_scaled, 1)
                if w >= 4 and w < 2 * NT - 1:
                    copy_x2T(w - 4)
            dve.wait_ge(y_scaled, 2 * NT)
            dve.wait_ge(x2_ready, 2 * NT - 1)
            xh = xr[:, NT - 1, 512:1024]
            v.tensor_tensor(xh, xh, obuf[:, (2 * NT - 1) % 2, :], ALU.add).then_inc(x2_ready, 1)
            copy_x2T(NT - 1)

            n32 = NT * 32
            lg = rt[:, 0:NT * NR].rearrange("p (t r) -> p t r", t=NT)
            o1 = NT * NR
            gsel = rt[:, o1:o1 + 16].rearrange("p (t g) -> p t g", t=NT)
            gkey = rt[:, o1 + 16:o1 + 32].rearrange("p (t g) -> p t g", t=NT)
            ge = exp_g.rearrange("p (t g) -> p t g", t=NT)
            prod = rt[:, o1 + 64:o1 + 64 + n32].rearrange("p (t g j) -> p t g j", t=NT, g=G)
            o2 = o1 + 64 + n32
            esel = rt[:, o2:o2 + 32].rearrange("p (t j) -> p t j", t=NT)
            key = rt[:, o2 + 32:o2 + 64].rearrange("p (t j) -> p t j", t=NT)
            oh = [rt[:, o2 + 64 + 32 * k:o2 + 96 + 32 * k].rearrange("p (t j) -> p t j", t=NT) for k in range(2)]
            o3 = o2 + 128
            sc = [rt[:, o3 + 4 * n:o3 + 4 * n + 4] for n in range(10)]
            gmax, kmax, gsum, ggate, m1, m2, den = sc[:7]
            dlt = exp_d
            o4 = o3 + 40
            rank = rt[:, o4:o4 + n32].rearrange("p (t e) -> p t e", t=NT)
            ov = rt[:, o4 + n32:o4 + 2 * n32].rearrange("p (t e) -> p t e", t=NT)
            sel = rt[:, o4 + 2 * n32:o4 + 3 * n32].rearrange("p (t e) -> p t e", t=NT)
            o5 = o4 + 3 * n32
            cnt, extra, incl, obase = (rt[:, o5 + 32 * n:o5 + 32 * n + 32] for n in range(4))
            posf = rt[:, o5 + 128:o5 + 136].rearrange("p (k t) -> p k t", k=2)
            assert o5 + 136 <= 1536 - 8

            def b3(ap, n):
                return ap.unsqueeze(2).to_broadcast([P, NT, n])

            def first_max(src, n, keybuf, onehot):
                link(v.tensor_reduce(kmax, src, X, ALU.max))
                link(v.tensor_tensor(keybuf, src, b3(kmax, n), ALU.is_equal))
                link(v.tensor_tensor(keybuf, keybuf, rev[:, 8 - n:8].unsqueeze(1).to_broadcast([P, NT, n]), ALU.mult))
                link(v.tensor_reduce(den, keybuf, X, ALU.max))
                link(v.tensor_tensor(onehot, keybuf, b3(den, n), ALU.is_equal))

            dve.wait_ge(memset_ready, 5)
            dve.wait_ge(logits_done, NT)
            common = prod.rearrange("p t g j -> p (t g j)")[:, 0:NR]
            link(v.tensor_copy(common, banks[:, 5, NT * NR:(NT + 1) * NR]))
            dve.wait_ge(xnb_ready, NT)
            for t in range(NT):
                ins = v.scalar_tensor_tensor(out=lg[:, t, :], in0=banks[:, 5, t * NR:(t + 1) * NR],
                                             scalar=r2[:, t:t + 1], in1=common, op0=ALU.mult, op1=ALU.add)
            link(ins)
            first_max(lg[:, :, 0:G], G, gkey, gsel)
            v.tensor_tensor(ge, lg[:, :, 0:G], b3(kmax, G), ALU.subtract).then_inc(g_exp_in, 1)
            link(v.tensor_tensor(prod, lg[:, :, G:NR].rearrange("p t (g j) -> p t g j", g=G),
                                 gsel.unsqueeze(3).to_broadcast([P, NT, G, EG]), ALU.mult))
            link(v.tensor_reduce(esel, prod.rearrange("p t g j -> p t j g"), X, ALU.add))
            first_max(esel, EG, key, oh[0])
            link(v.tensor_copy(m1, kmax))
            link(v.scalar_tensor_tensor(out=esel, in0=oh[0], scalar=-1e30, in1=esel, op0=ALU.mult, op1=ALU.add))
            first_max(esel, EG, key, oh[1])
            v.tensor_tensor(dlt, kmax, m1, ALU.subtract).then_inc(d_in, 1)
            for k in range(2):
                ins = v.tensor_tensor(masks[:, k, :, :].rearrange("p t (g j) -> p t g j", g=G),
                                      gsel.unsqueeze(3).to_broadcast([P, NT, G, EG]),
                                      oh[k].unsqueeze(2).to_broadcast([P, NT, G, EG]), ALU.mult)
            link(ins)
            v.tensor_tensor(masks[:, 2, :, :], masks[:, 0, :, :], masks[:, 1, :, :], ALU.add).then_inc(masks_ready, 1)
            dve.wait_ge(rank_done, 1)
            v.tensor_copy(rank, banks[:, 0, 0:n32].rearrange("p (t e) -> p t e", t=NT))
            link(v.tensor_scalar(ints[:, 0:32], banks[:, 0, n32:n32 + 32], float(C - 1), None, ALU.add))
            link(v.tensor_scalar(ints[:, 0:32], ints[:, 0:32], C.bit_length() - 1, None, ALU.arith_shift_right))
            link(v.tensor_copy(cnt, ints[:, 0:32]))
            link(v.tensor_scalar(extra, cnt, -1.0, 0.0, ALU.add, ALU.max))
            link(v.tensor_tensor_scan(incl, extra, zero32, 0.0, ALU.add, ALU.add))
            link(v.tensor_tensor(obase, incl, extra, ALU.subtract))
            link(v.tensor_scalar(obase, obase, float(E - 1), float(C), ALU.add, ALU.mult))
            v.tensor_tensor(obase, obase, e64, ALU.subtract)
            link(v.tensor_scalar(ov, rank, float(C), None, ALU.is_ge))
            v.tensor_tensor(ov, ov, obase.unsqueeze(1).to_broadcast([P, NT, E]), ALU.mult)
            link(v.tensor_tensor(rank, rank, e64.unsqueeze(1).to_broadcast([P, NT, E]), ALU.add))
            link(v.tensor_tensor(rank, rank, ov, ALU.add))
            v.tensor_tensor(sel, rank, masks[:, 0, :, :], ALU.mult)
            link(v.tensor_tensor(ov, rank, masks[:, 1, :, :], ALU.mult))
            v.tensor_reduce(posf[:, 0, :], sel, X, ALU.add)
            link(v.tensor_reduce(posf[:, 1, :], ov, X, ALU.add))
            posi, lo_i = ints[:, 80:88], ints[:, 88:96]
            pos2 = rt[:, o5 + 128:o5 + 136]
            link(v.tensor_copy(posi, pos2))
            link(v.tensor_scalar(lo_i, posi, P - 1, None, ALU.bitwise_and))
            link(v.tensor_scalar(posi, posi, P.bit_length() - 1, None, ALU.logical_shift_right))
            lof, hif = cnt[:, 0:8], cnt[:, 8:16]
            link(v.tensor_copy(lof, lo_i))
            link(v.tensor_copy(hif, posi))
            dve.wait_ge(logits_done, NT)
            v.tensor_tensor(onehot, slot_iota.unsqueeze(1).to_broadcast([P, 2 * NT, P]),
                            lof.unsqueeze(2).to_broadcast([P, 2 * NT, P]), ALU.is_equal)
            hot_col = rt[:, 0:2 * NT * NCOL].rearrange("p (c q) -> p c q", c=2 * NT)
            link(v.tensor_tensor(hot_col, slot_iota[:, 0:NCOL].unsqueeze(1).to_broadcast([P, 2 * NT, NCOL]),
                                 hif.unsqueeze(2).to_broadcast([P, 2 * NT, NCOL]), ALU.is_equal))
            v.tensor_tensor(hot_col, hot_col, pair_id.unsqueeze(2).to_broadcast([P, 2 * NT, NCOL]),
                            ALU.mult).then_inc(onehot_ready, 1)
            dve.wait_ge(onehot_ready, 1)
            dve.wait_ge(table_done, 1)
            found, free = onehot[:, 0, 0:NCOL], onehot[:, 1, 0:NCOL]
            link(v.tensor_copy(found, banks[:, 1, 0:NCOL]))
            link(v.tensor_scalar(free, found, 0.0, float(SKIP), ALU.is_equal, ALU.mult))
            link(v.scalar_tensor_tensor(out=found, in0=found, scalar=-1.0, in1=free, op0=ALU.add, op1=ALU.add))
            v.tensor_copy(tables[:, 1, :], found)
            link(v.tensor_scalar(free, found, float(T), float(-T), ALU.is_ge, ALU.mult))
            v.tensor_tensor(tables[:, 0, :], found, free, ALU.add).then_inc(table_ready, 1)
            dve.wait_ge(table_ready, 1)
            over = rt[0:1, 0:2 * NQOV * E].rearrange("p (b e) -> p b e", e=E)
            nover = sel[0:1, 0, 0:2 * NQOV]
            link(v.tensor_tensor(over, incl[0:1, :].unsqueeze(1).to_broadcast([1, 2 * NQOV, E]),
                                 b_iota[0:1, :].unsqueeze(2).to_broadcast([1, 2 * NQOV, E]), ALU.is_le))
            link(v.tensor_reduce(nover, over, X, ALU.add))
            link(v.tensor_scalar(plan[0:1, 0:2 * NQOV], nover, float(E - 1), None, ALU.min))
            last = plan[0:1, 2 * NQOV:2 * NQOV + 1]
            link(v.tensor_scalar(last, incl[0:1, E - 1:E], 1.0, None, ALU.add))
            v.tensor_scalar(last, last, 1, None, ALU.logical_shift_right).then_inc(plan_ready, 1)
            dve.wait_ge(g_exp, 1)
            link(v.tensor_reduce(gsum, ge, X, ALU.add))
            link(v.reciprocal(ggate, gsum))
            dve.wait_ge(d_exp, 1)
            link(v.tensor_scalar(den, dlt, 1.0, None, ALU.add))
            link(v.reciprocal(den, den))
            link(v.tensor_tensor(wpair[:, 0, :], den, ggate, ALU.mult))
            link(v.tensor_tensor(wpair[:, 1, :], wpair[:, 0, :], dlt, ALU.mult))

            def modulate(n, r):
                dve.wait_ge(eT_done, n)
                dst = heT[:, r, :].rearrange("p (k t) -> p k t", k=KD)
                src = banks[:, 0:2, :].rearrange("p b (k t) -> p (b k) t", t=P)
                v.tensor_tensor(dst, src, mod[:, 3, :].unsqueeze(2).to_broadcast([P, KD, P]), ALU.mult).then_inc(he_mul, 1)
                dve.wait_ge(he_mul, n)
                v.tensor_tensor(dst, dst, mod[:, 2, :].unsqueeze(2).to_broadcast([P, KD, P]), ALU.add).then_inc(heT_ready, 1)

            def gated(n):
                dve.wait_ge(silu_ready, n)
                v.tensor_tensor(ge_act, gact, banks[:, 2, F:2 * F], ALU.mult).then_inc(ge_ready, 1)

            def y_evac(n, r):
                dve.wait_ge(ye_done, n)
                v.tensor_tensor(ysb[:, r, :], banks[:, 4 + 2 * r:6 + 2 * r, :].rearrange("p b k -> p (b k)"),
                                gates[:, 1, :], ALU.mult).then_inc(ysb_ready, 1)

            dve.wait_ge(fT_done, NT)
            dve.wait_ge(xn_stored, 16 * NT)
            modulate(1, 0)

            def pair(q, r, stored, last):
                if not last:
                    modulate(q + 2, 1 - r)
                gated(q + 1)
                if stored is not None:
                    dve.wait_ge(y_stored[r], stored)
                y_evac(q + 1, r)

            pair(0, 0, None, False)
            pair(1, 1, None, False)
            pair(2, 0, 16, False)
            with dve.Fori(1, NQ // 2 - 1) as it:
                pair(it * 2 + 1, 1, it * 16, False)
                pair(it * 2 + 2, 0, it * 16 + 16, False)
            pair(NQ - 1, 1, 16 * (NQ // 2 - 1), True)
            dve.wait_ge(plan_ready, 1)
            nq = dve.value_load(plan[0:1, 2 * NQOV:2 * NQOV + 1], min_val=0, max_val=NQOV)
            with dve.If(nq > 0):
                with dve.Fori(0, nq) as m:
                    modulate(m + (NQ + 1), 0)
                    pair(m + NQ, 0, m * 16 + 16 * (NQ // 2), True)
            for t in range(NT):
                dve.wait_ge(pairs_in[t], 16)
                v.scalar_tensor_tensor(out=xr[:, t, :], in0=fin_pair(t)[:, 0, :], scalar=wpair[:, 0, t:t + 1],
                                       in1=xr[:, t, :], op0=ALU.mult, op1=ALU.add).then_inc(fin_b, 1)
                dve.wait_ge(fin_b, t + 1)
                dve.wait_ge(fin_a, t + 1)
                v.tensor_tensor(xr[:, t, :], xr[:, t, :], fin_pair(t)[:, 1, :], ALU.add).then_inc(fin_c, 1)

        @block.tensor
        def _(pe):
            mm = nc.tensor.matmul
            pe.wait_ge(consts_ready, 4)
            pe.wait_ge(consts_dve, 5)

            def x_T(k):
                for t in range(NT):
                    ins = nc.tensor.transpose(banks[:, XT_BANK[k], t * P:(t + 1) * P], xn[:, t, k * P:(k + 1) * P], ident)
                ins.then_inc(xT_done, 1)

            def column_sums(v, used):
                pe.wait_ge(used, KD)
                for k in range(KD):
                    ins = mm(banks[:, 0, 8 * v + k:8 * v + k + 1],
                             acc[:, v, :].rearrange("p (j k) -> p k j", k=KD)[:, k, :], ones[:, 0:1],
                             start=(v + k == 0), stop=True, skip_group_check=True)
                return ins

            column_sums(0, shift_used)
            pe.wait_ge(xn_ready, NT)
            for k in range(KD - 1):
                x_T(k)
            column_sums(1, scale_used).then_inc(col_a, 1)
            pe.wait_ge(hT_raw, 1)
            pe.wait_ge(hT_hi_ready, 1)
            x_T(KD - 1)

            def wait_freed(job):
                which, value = freed[job]
                pe.wait_ge(qk_raw if which == "qk" else bank_free[which], value)

            def run(job, part=None):
                ks = range(KD) if part is None else range(part * KD // 2, (part + 1) * KD // 2)
                n = job_no[job]
                bank = banks[:, n % 2, :]
                if n >= 2 and part != 1:
                    wait_freed(job_at[n - 2])
                kind = job[0]
                if kind in ("qk", "sq", "sk"):
                    n_in, ch = {"qk": (job[1] // 4, job[1] % 4), "sq": (3, job[1]), "sk": (4, job[1])}[kind]
                    w, arrived, value = piece(n_in)
                    pe.wait_ge(arrived, value)
                    for k in ks:
                        if n == 0:
                            pe.wait_ge(hT_raw, k + 1)
                        ins = mm(bank, w[:, k, ch * P:(ch + 1) * P], hT[:, k, :], start=(k == 0), stop=(k == KD - 1))
                elif kind == "v":
                    w, arrived, value = piece(2 if job[2] == 0 else 5)
                    pe.wait_ge(arrived, value)
                    for k in ks:
                        ins = mm(bank, hT[:, k, job[1] * P:(job[1] + 1) * P], w[:, k, :], start=(k == 0), stop=(k == KD - 1))
                elif kind == "gate":
                    v = 2 if job[1] == 0 else 5
                    pe.wait_ge(ada_used, 4 * (v - 1))
                    ins = mm(bank, ones, acc[:, v % 2, job[2] * 512:job[2] * 512 + 512], start=True, stop=True)
                elif kind == "col":
                    v = job[1] + 1
                    pe.wait_ge(ada_used, 4 * (v - 1))
                    for k in range(KD):
                        ins = mm(bank[:, k:k + 1], acc[:, v % 2, :].rearrange("p (j k) -> p k j", k=KD)[:, k, :],
                                 ones[:, 0:1], start=(k == 0), stop=True, skip_group_check=True)
                elif kind == "shift_router":
                    wait_freed(("col", 2))
                    for k in range(KD):
                        ins = mm(bank[0:1, 0:NR], mod[:, 2, k:k + 1], wr[:, k, :], start=(k == 0), stop=(k == KD - 1))
                if part != 0:
                    ins.then_inc(job_done, 1)

            def qk_norm(n):
                pe.wait_ge(sq_ready, n + 1)
                if n >= 2:
                    pe.wait_ge(rqk_ready, n - 1)
                mm(banks[:, 2 + n % 2, :], halves, sqb[:, n % 2, :], start=True, stop=True).then_inc(norm_done, 1)

            def run_split(job):
                n = job_no[job]
                bank = banks[:, n % 2, :]
                if n >= 2:
                    wait_freed(job_at[n - 2])
                pe.wait_ge(w_split, n if n < 8 else 11)
                if n == 1:
                    pe.wait_ge(hT_lo_dve, KD // 2)
                    pe.wait_ge(hT_lo_pool, KD // 2)
                lo = w_lo_parts[:, (2 if n >= 8 else n // 4) % 2, :].rearrange("p (k n) -> p k n", k=KD)
                for k in range(KD):
                    if job[0] == "qk":
                        part = slice((n % 4) * P, (n % 4 + 1) * P)
                        products = [(w_hi[:, k, part], hT_hi[:, k, :]), (w_hi[:, k, part], hT_lo(k)),
                                    (lo[:, k, part], hT_hi[:, k, :])]
                    else:
                        part = slice(job[1] * P, (job[1] + 1) * P)
                        products = [(hT_hi[:, k, part], w_hi[:, k, :]), (hT_hi[:, k, part], lo[:, k, :]),
                                    (hT_lo(k)[:, part], w_hi[:, k, :])]
                    for m, (still, moving) in enumerate(products):
                        ins = mm(bank, still, moving, start=(k + m == 0), stop=(k == KD - 1 and m == 2))
                ins.then_inc(job_done, 1)

            for i, job in enumerate(head_jobs):
                if i == 0 or job[0] == "gate":
                    run(job)
                else:
                    run_split(job)
                if 1 <= i <= 8:
                    qk_norm(i - 1)

            def scores(u):
                h, i = u // NT, u % NT
                W = (i + 1) * P
                if u == 0:
                    pe.wait_ge(qk_dve, 8)
                    pe.wait_ge(rqk_ready, 8)
                if u >= 2:
                    pe.wait_ge(max_ready, u - 1)
                for m in range(2):
                    q = qkT[m * HD:(m + 1) * HD, h, i * P:(i + 1) * P]
                    k = qkT[m * HD:(m + 1) * HD, 4 + h, 0:W]
                    ins = mm(banks[:, 2 + 2 * (u % 2) + m, 0:W], q, k, start=True, stop=True)
                ins.then_inc(score_done, 1)

            def T_free(n):
                if n >= 1:
                    kind, w = T_order[n - 1]
                    pe.wait_ge(probT_ready if kind == "unit" else mix_ready, w + 1)

            def probT_make(u):
                i = u % NT
                pe.wait_ge(prob_ready, u + 1)
                T_free(T_no[("unit", u)])
                for kb in range(i + 1):
                    ins = nc.tensor.transpose(banks[:, 6, kb * P:(kb + 1) * P], prob[:, u % 2, 0, kb * P:(kb + 1) * P], ident)
                ins.then_inc(T_done, 1)

            def pv(u):
                h, i = u // NT, u % NT
                pe.wait_ge(probT_ready, u + 1)
                if i == 0 and h == 0:
                    wait_freed(("v", NT - 2, 0))
                    wait_freed(("v", NT - 1, 0))
                if i == 0 and h >= 1:
                    pe.wait_ge(o_copied, h)
                for kb in range(i + 1):
                    ins = mm(banks[:, 7, i * P:(i + 1) * P], probT[:, u % 2, kb * P:(kb + 1) * P],
                             val[:, kb, h * P:(h + 1) * P], start=(i == 0 and kb == 0), stop=(kb == i),
                             skip_group_check=True)
                ins.then_inc(pv_done, 1)

            def fin_T(f):
                pe.wait_ge(o_ready, f + 1)
                T_free(T_no[("fin", f)])
                o = obuf[:, 2 + f % 2, :]
                for i in range(NT):
                    ins = nc.tensor.transpose(banks[:, 6, i * P:(i + 1) * P], o[:, i * P:(i + 1) * P], ident)
                ins.then_inc(T_done, 1)

            def stick_scores(n):
                pair, s = n // 2, n % 2
                if n == 0:
                    wait_freed(job_at[len(job_no) - 2])
                    wait_freed(job_at[len(job_no) - 1])
                    pe.wait_ge(max_ready, NT * DH - 1)
                if n == 1:
                    pe.wait_ge(max_ready, NT * DH)
                if n >= 2:
                    pe.wait_ge(stick_raw, n - 1)
                for kb in (0, 1, 3, 2):
                    W = T - kb * P
                    k = qkT[s * HD:(s + 1) * HD, 12 + pair, kb * P:(kb + 1) * P]
                    q = qkT[s * HD:(s + 1) * HD, 8 + pair, kb * P:T]
                    ins = mm(zps[n % 2][:, ZOFF[kb]:ZOFF[kb] + W], k, q, start=(kb != 3), stop=True,
                             skip_group_check=True)
                ins.then_inc(z_done, 1)

            def stick_sums(n):
                pe.wait_ge(soft_ready, n + 1)
                for kb in range(NT):
                    for j in range(kb, NT):
                        W = T - j * P
                        o = ZOFF[kb] + (j - kb) * P
                        ins = mm(zps[n % 2][:, o:o + W], negtri if j == kb else negones,
                                 soft[:, n % 2, ZOFF[j]:ZOFF[j] + W], start=False, stop=True, skip_group_check=True)
                ins.then_inc(tri_done, 1)

            def stick_pv(n):
                pair, s = n // 2, n % 2
                pe.wait_ge(stick_ready, n + 1)
                if s == 0:
                    pe.wait_ge(o_copied, DH + pair)
                for i in range(NT):
                    for kb in range(i + 1):
                        o = ZOFF[kb] + (i - kb) * P
                        ins = mm(banks[:, 7, i * P + s * HD:i * P + (s + 1) * HD], stick[:, n % 2, o:o + P],
                                 val[:, kb, 512 + n * HD:512 + (n + 1) * HD],
                                 start=(s == 0 and i == 0 and kb == 0), stop=(kb == i), skip_group_check=True)
                ins.then_inc(spv_done, 1)

            def out_proj(w, ks=range(KD)):
                t, half = w // 2, w % 2
                if ks[0] == 0:
                    if w == 0:
                        for n in (6, 7):
                            _, arrived, value = piece(n)
                            pe.wait_ge(arrived, value)
                    if w <= 2:
                        pe.wait_ge(stick_raw, SH - 1)
                    elif w <= 4:
                        pe.wait_ge(stick_raw, SH)
                    else:
                        pe.wait_ge(y_scaled, w - 4)
                pe.wait_ge(mix_ready, ks[-1] + 1)
                for k in ks:
                    wv = piece(6 + k // 4)[0]
                    ins = mm(banks[:, w % 5, :], mixT[:, k, t * P:(t + 1) * P],
                             wv[:, k % 4, half * 512:(half + 1) * 512], start=(k == 0), stop=(k == KD - 1))
                if ks[-1] == KD - 1:
                    ins.then_inc(y_done, 1)

            for s in range(STEPS):
                if s < NT * DH:
                    scores(s)
                if 1 <= s <= NT * DH:
                    probT_make(s - 1)
                if 2 <= s < DIFF_STEPS:
                    pv(s - 2)
                for f in range(DH):
                    if s == fin_step(f) + 2:
                        fin_T(f)
                for job, part in step_parts.get(s, ()):
                    run(job, part)
                n = s - STICK_0
                if 0 <= n < SH:
                    stick_scores(n)
                if 1 <= n <= SH:
                    stick_sums(n - 1)
                if 2 <= n <= SH + 1:
                    stick_pv(n - 2)
                for f in range(DH, 2 * DH):
                    if s == fin_step(f) + 2:
                        fin_T(f)
                if n == SH:
                    out_proj(0, range(6))
                if n == SH + 1:
                    out_proj(1, range(6))
                if n == SH + 2:
                    out_proj(0, range(6, 7))
                    out_proj(1, range(6, 7))
                    out_proj(2, range(7))

            def rows_T(t):
                pe.wait_ge(x2_ready, 2 * t + 2)
                if t >= 1:
                    pe.wait_ge(x2T_ready, t)
                for k in range(KD):
                    ins = nc.tensor.transpose(banks[:, 6 + k // 4, (k % 4) * P:(k % 4 + 1) * P],
                                              xr[:, t, :].rearrange("p (j k) -> p k j", k=KD)[:, k, :], ident)
                ins.then_inc(fT_done, 1)

            def logits(t):
                if t == 0:
                    pe.wait_ge(wrA_ready, 1)
                pe.wait_ge(x2T_ready, t + 1)
                if t == 0:
                    mm(banks[:, 5, NT * NR:(NT + 1) * NR], ones[0:1, :], router_row[0:1, 1, :], start=True, stop=True,
                       skip_group_check=True)
                for k in range(KD):
                    ins = mm(banks[:, 5, t * NR:(t + 1) * NR], x2T[:, t % 2, k * P:(k + 1) * P], wrA[:, k, :],
                             start=False, stop=(k == KD - 1), skip_group_check=True)
                ins.then_inc(logits_done, 1)

            out_proj(3, range(7))
            for w in range(4):
                out_proj(w, range(7, 8))
            out_proj(4)
            for t in range(NT - 1):
                rows_T(t)
                if t >= 1:
                    logits(t - 1)
                out_proj(t + 5)
            logits(NT - 2)
            rows_T(NT - 1)
            logits(NT - 1)

            pe.wait_ge(masks_ready, 1)
            for t in range(NT):
                for j in range(t + 1):
                    mm(banks[:, 0, t * E:(t + 1) * E], tri_bf[:] if j == t else ones_bf[:], masks[:, 2, j, :],
                       start=(t == 0), stop=(j == t), skip_group_check=True)
            for j in range(NT):
                ins = mm(banks[:, 0, NT * E:NT * E + E], ones_bf[:], masks[:, 2, j, :], start=False, stop=(j == NT - 1),
                         skip_group_check=True)
            ins.then_inc(rank_done, 1)
            pe.wait_ge(onehot_ready, 1)
            for n in range(2 * NT):
                ins = mm(banks[:, 1, 0:NCOL], onehot[:, n, :], rt[:, n * NCOL:(n + 1) * NCOL],
                         start=(n == 0), stop=(n == 2 * NT - 1))
            ins.then_inc(table_done, 1)

            def expert_T(n, arrived, r):
                pe.wait_ge(arrived[0], arrived[1])
                if n is not None:
                    pe.wait_ge(he_mul, n)
                for k in range(KD):
                    ins = nc.tensor.transpose(banks[:, k // 4, (k % 4) * P:(k % 4 + 1) * P],
                                              rows[:, r, k * P:(k + 1) * P], ident)
                ins.then_inc(eT_done, 1)

            def expert_h(n, place, value, r):
                pe.wait_ge(heT_ready, n)
                for up, arrived, ws in ((0, w1_in, w1s), (1, w3_in, w3s)):
                    pe.wait_ge(arrived[place], value)
                    for k in range(KD):
                        for half in range(2):
                            ins = mm(banks[half * C:(half + 1) * C, 2, up * F:(up + 1) * F],
                                     heT[:, r, k * P + half * C:k * P + (half + 1) * C], ws[2 * place + half][:, k, :],
                                     start=(up + k == 0), stop=(k == KD - 1), skip_group_check=True)
                    ins.then_inc(h_done if up else h1_done, 1)

            def expert_geT(n):
                pe.wait_ge(ge_ready, n)
                for fc in range(FC):
                    ins = nc.tensor.transpose(banks[:, 3, fc * P:(fc + 1) * P], ge_act[:, fc * P:(fc + 1) * P], ident)
                ins.then_inc(geT_done, 1)

            def expert_y(n, n_free, place, value, r):
                pe.wait_ge(geT_ready, n)
                pe.wait_ge(w2_in[place], value)
                if n_free is not None:
                    pe.wait_ge(ysb_ready, n_free)
                for col in range(2):
                    for fc in range(FC):
                        for half in range(2):
                            ins = mm(banks[half * C:(half + 1) * C, 4 + 2 * r + col, :],
                                     geT[:, fc * P + half * C:fc * P + (half + 1) * C],
                                     w2s[2 * place + half][:, fc, col * 512:(col + 1) * 512],
                                     start=(fc == 0), stop=(fc == FC - 1))
                ins.then_inc(ye_done, 1)

            def pair(q, r, place, value, y_free, next_rows):
                if next_rows is not None:
                    expert_T(q + 1, next_rows, 1 - r)
                expert_h(q + 1, place, value, r)
                expert_geT(q + 1)
                expert_y(q + 1, q - 1 if y_free else None, place, value, r)

            def turn(q, more=0):
                return more + 32 * (q // R + 1)

            def rows_of(q, more=0):
                return rows_in[q % 2], more + 16 * (q // 2 + 1)

            expert_T(None, rows_of(0), 0)
            for q in range(3):
                pair(q, q % 2, q % R, turn(q), q >= 2, rows_of(q + 1))
            with pe.Fori(0, (NQ - 4) // 6) as it:
                for q in range(3, 9):
                    pair(it * 6 + q, q % 2, q % R, turn(q, it * 64), True, rows_of(q + 1, it * 48))
            pair(NQ - 1, 1, (NQ - 1) % R, turn(NQ - 1), True, None)
            pe.wait_ge(plan_ready, 1)
            nq = pe.value_load(plan[0:1, 2 * NQOV:2 * NQOV + 1], min_val=0, max_val=NQOV)
            with pe.If(nq > 0):
                with pe.Fori(0, nq) as m:
                    expert_T(m + NQ, (rows_in[0], m * 16 + 16 * (NQ // 2 + 1)), 0)
                    pair(m + NQ, 0, 1, m * 32 + 32 * ((NQ + 1) // R + 1), True, None)


_INS = ["x", "c", "w_ada", "b_ada", "g_attn", "w_in", "q_norm_g", "k_norm_g", "lambda_q1", "lambda_k1",
        "lambda_q2", "lambda_k2", "diff_out_g", "sb_out_g", "w_out", "g_ffn", "w_group", "b_group",
        "w_erouter", "b_expert", "w1", "w3", "w2"]


def kernel(**inputs):
    import numpy as _np
    import concourse.bacc as _bacc
    from concourse import mybir as _mybir
    from concourse.bass_utils import run_bass_kernel_spmd as _run

    nc = _bacc.Bacc("TRN2", target_bir_lowering=False, num_devices=1)
    arrays, args = {}, []
    for name in _INS:
        a = _np.ascontiguousarray(inputs[name])
        arrays[f"in_{name}_dram"] = a
        args.append(nc.dram_tensor(f"in_{name}_dram", a.shape, _mybir.dt.from_np(a.dtype), kind="ExternalInput").ap())
    args.append(nc.dram_tensor("out_0_dram", (1, T, D), _mybir.dt.float32, kind="ExternalOutput").ap())
    hymba_block(nc, *args)
    r = _run(nc, [arrays], core_ids=[0])
    return r.results[0]["out_0_dram"]
```
